# Optimizing a Trainium2 kernel written in Bass

```python
import jax, jax.numpy as jnp
from jax import lax
import numpy as np
import math

D_MODEL = 1024
BATCH = 1
SEQ = 256
DEPTH = 2

N_MEM = 256
D_MIX = D_MODEL
CONV_HEADS = 4
CONV_DIM = D_MIX // 4
CONV_WIDTH = 3
REC_HEADS = 4
REC_DIM = D_MIX // 2
REC_HEAD_DIM = REC_DIM // REC_HEADS
REC_EXPAND = 128
REC_FDIM = REC_HEADS * REC_EXPAND
CHUNK = 64
POOL_DIM = D_MIX - CONV_DIM - REC_DIM
POOL_WINDOWS = (2, 4, 8, 16)
POOL_GROUP = POOL_DIM // len(POOL_WINDOWS)
D_IN = 3 * CONV_DIM + 2 * REC_FDIM + 2 * REC_DIM + POOL_DIM
CA_HEADS = 4
CA_HEAD_DIM = D_MODEL // CA_HEADS
D_FF = 2816
ALPHA = (2.0 * DEPTH) ** 0.25
BETA = (8.0 * DEPTH) ** -0.25
LN_EPS = 1e-5
RMS_EPS = 1e-6


def layer_norm(x, g, b):
    xf = x.astype(jnp.float32)
    mu = jnp.mean(xf, axis=-1, keepdims=True)
    var = jnp.mean(jnp.square(xf - mu), axis=-1, keepdims=True)
    return ((xf - mu) * lax.rsqrt(var + LN_EPS)).astype(x.dtype) * g + b

def swiglu(x, w_gate, w_up, w_down):
    return (jax.nn.silu(x @ w_gate) * (x @ w_up)) @ w_down

def short_gated_conv(h, b_gate, c_gate, w):
    u = c_gate * h
    s = u.shape[1]
    up = jnp.pad(u, ((0, 0), (CONV_WIDTH - 1, 0), (0, 0)))
    y = sum(w[k] * up[:, k:k + s] for k in range(CONV_WIDTH))
    return b_gate * y

def hgrn2(q, f_logit, v, g, lb, norm_g):
    bsz, s, _ = q.shape
    n_chunks = s // CHUNK
    f32 = jnp.float32
    f = lb + (1.0 - lb) * jax.nn.sigmoid(f_logit.astype(f32))
    logf = jnp.log(f)
    k = 1.0 - f

    def to_chunks(t, d):
        return t.reshape(bsz, n_chunks, CHUNK, REC_HEADS, d).transpose(1, 0, 3, 2, 4)

    qc = to_chunks(q.astype(f32), REC_EXPAND)
    kc = to_chunks(k, REC_EXPAND)
    lc = to_chunks(logf, REC_EXPAND)
    vc = to_chunks(v.astype(f32), REC_HEAD_DIM)
    mask = jnp.tril(jnp.ones((CHUNK, CHUNK), dtype=bool))

    def step(state, inp):
        qb, kb, vb, lb_ = inp
        b = jnp.cumsum(lb_, axis=2)
        diff = b[:, :, :, None, :] - b[:, :, None, :, :]
        decay = jnp.exp(jnp.where(mask[:, :, None], diff, -jnp.inf))
        attn = jnp.einsum('bhtd,bhsd,bhtsd->bhts', qb, kb, decay)
        o = (jnp.einsum('bhts,bhsv->bhtv', attn, vb)
             + jnp.einsum('bhtd,bhdv->bhtv', qb * jnp.exp(b), state))
        b_last = b[:, :, -1:, :]
        new_state = (jnp.exp(b_last[:, :, 0, :])[..., None] * state
                     + jnp.einsum('bhsd,bhsv->bhdv', kb * jnp.exp(b_last - b), vb))
        return new_state, o

    s0 = jnp.zeros((bsz, REC_HEADS, REC_EXPAND, REC_HEAD_DIM), f32)
    _, o = lax.scan(step, s0, (qc, kc, vc, lc))
    o = o.transpose(1, 0, 3, 2, 4).reshape(bsz, s, REC_HEADS, REC_HEAD_DIM)
    o = o * lax.rsqrt(jnp.mean(jnp.square(o), axis=-1, keepdims=True) + RMS_EPS)
    o = o * norm_g.reshape(REC_HEADS, REC_HEAD_DIM).astype(f32)
    o = o.reshape(bsz, s, REC_DIM) * jax.nn.sigmoid(g.astype(f32))
    return o.astype(v.dtype)

def multiscale_pool(u, w_pool, scale):
    bsz, s, _ = u.shape
    uf = u.astype(jnp.float32)
    cs = jnp.cumsum(uf, axis=1)
    t = jnp.arange(s)
    groups = []
    for gi, w in enumerate(POOL_WINDOWS):
        sl = slice(gi * POOL_GROUP, (gi + 1) * POOL_GROUP)
        c = cs[:, :, sl]
        win_sum = c - jnp.pad(c, ((0, 0), (w, 0), (0, 0)))[:, :s]
        count = jnp.minimum(t + 1, w).astype(jnp.float32)[None, :, None]
        groups.append(win_sum / count - uf[:, :, sl])
    p = jnp.stack(groups, axis=2).astype(u.dtype)
    y = jnp.einsum('bsgc,gcd->bsgd', p, w_pool).reshape(bsz, s, POOL_DIM)
    return y * scale

def cross_attn(x, mem, wq, wk, wv, wo):
    bsz, s, _ = x.shape
    m = mem.shape[1]
    q = (x @ wq).reshape(bsz, s, CA_HEADS, CA_HEAD_DIM)
    k = (mem @ wk).reshape(bsz, m, CA_HEADS, CA_HEAD_DIM)
    v = (mem @ wv).reshape(bsz, m, CA_HEADS, CA_HEAD_DIM)
    sc = jnp.einsum('bshd,bmhd->bhsm', q, k).astype(jnp.float32) * (CA_HEAD_DIM ** -0.5)
    p = jax.nn.softmax(sc, axis=-1).astype(v.dtype)
    o = jnp.einsum('bhsm,bmhd->bshd', p, v).reshape(bsz, s, D_MODEL)
    return o @ wo

def first_inputs(seed: int = 0) -> dict:
    key = jax.random.key(seed)
    ks = jax.random.split(key, 24)
    f32 = jnp.float32
    nrm = lambda k, shp, sc: jax.random.normal(k, shp, f32) * sc
    return {
        'x': nrm(ks[0], (BATCH, SEQ, D_MODEL), 1.0),
        'mem': nrm(ks[1], (BATCH, N_MEM, D_MODEL), 1.0),
        'ffn1_gate': nrm(ks[2], (DEPTH, D_MODEL, D_FF), BETA * D_MODEL ** -0.5),
        'ffn1_up': nrm(ks[3], (DEPTH, D_MODEL, D_FF), BETA * D_MODEL ** -0.5),
        'ffn1_down': nrm(ks[4], (DEPTH, D_FF, D_MODEL), BETA * D_FF ** -0.5),
        'w_in': nrm(ks[5], (DEPTH, D_MODEL, D_IN), D_MODEL ** -0.5),
        'conv_w': nrm(ks[6], (DEPTH, CONV_WIDTH, CONV_DIM), CONV_WIDTH ** -0.5),
        'rec_lb': nrm(ks[7], (DEPTH, REC_FDIM), 0.5),
        'rec_norm_g': 1.0 + nrm(ks[8], (DEPTH, REC_DIM), 0.02),
        'pool_w': nrm(ks[9], (DEPTH, len(POOL_WINDOWS), POOL_GROUP, POOL_GROUP), POOL_GROUP ** -0.5),
        'pool_scale': 1.0 + nrm(ks[10], (DEPTH, POOL_DIM), 0.02),
        'w_out': nrm(ks[11], (DEPTH, D_MIX, D_MODEL), BETA * D_MIX ** -0.5),
        'ca_q': nrm(ks[12], (DEPTH, D_MODEL, D_MODEL), D_MODEL ** -0.5),
        'ca_k': nrm(ks[13], (DEPTH, D_MODEL, D_MODEL), D_MODEL ** -0.5),
        'ca_v': nrm(ks[14], (DEPTH, D_MODEL, D_MODEL), BETA * D_MODEL ** -0.5),
        'ca_o': nrm(ks[15], (DEPTH, D_MODEL, D_MODEL), BETA * D_MODEL ** -0.5),
        'ffn2_gate': nrm(ks[16], (DEPTH, D_MODEL, D_FF), BETA * D_MODEL ** -0.5),
        'ffn2_up': nrm(ks[17], (DEPTH, D_MODEL, D_FF), BETA * D_MODEL ** -0.5),
        'ffn2_down': nrm(ks[18], (DEPTH, D_FF, D_MODEL), BETA * D_FF ** -0.5),
        'ln_g': 1.0 + nrm(ks[19], (DEPTH, 4, D_MODEL), 0.02),
        'ln_b': nrm(ks[20], (DEPTH, 4, D_MODEL), 0.02),
    }

def first_block(x, mem, ffn1_gate, ffn1_up, ffn1_down, w_in, conv_w, rec_lb, rec_norm_g,
              pool_w, pool_scale, w_out, ca_q, ca_k, ca_v, ca_o,
              ffn2_gate, ffn2_up, ffn2_down, ln_g, ln_b):
    sm = jax.nn.softmax(rec_lb.astype(jnp.float32), axis=0)
    lbs = jnp.cumsum(sm, axis=0) - sm[0:1]
    split_at = np.cumsum([CONV_DIM, CONV_DIM, CONV_DIM, REC_FDIM, REC_FDIM, REC_DIM, REC_DIM])
    h = x
    for l in range(DEPTH):
        h = layer_norm(ALPHA * h + 0.5 * swiglu(h, ffn1_gate[l], ffn1_up[l], ffn1_down[l]),
                       ln_g[l, 0], ln_b[l, 0])
        z = h @ w_in[l]
        cb, cc, ch, rq, rf, ri, rg, pu = jnp.split(z, split_at, axis=-1)
        y_conv = short_gated_conv(ch, cb, cc, conv_w[l])
        y_rec = hgrn2(rq, rf, ri, rg, lbs[l], rec_norm_g[l])
        y_pool = multiscale_pool(pu, pool_w[l], pool_scale[l])
        mix = jnp.concatenate([y_conv, y_rec, y_pool], axis=-1) @ w_out[l]
        h = layer_norm(ALPHA * h + mix, ln_g[l, 1], ln_b[l, 1])
        h = layer_norm(ALPHA * h + cross_attn(h, mem, ca_q[l], ca_k[l], ca_v[l], ca_o[l]),
                       ln_g[l, 2], ln_b[l, 2])
        h = layer_norm(ALPHA * h + 0.5 * swiglu(h, ffn2_gate[l], ffn2_up[l], ffn2_down[l]),
                       ln_g[l, 3], ln_b[l, 3])
    return h


GRID_W = 64
CTX_LEN = 256
N_MIXERS = 2
N_HEADS = 8
N_KV_HEADS = 2
HEAD_DIM = D_MODEL // N_HEADS
KV_REP = N_HEADS // N_KV_HEADS
QKV_DIM = (N_HEADS + 2 * N_KV_HEADS) * HEAD_DIM
Q_BLOCK = 128
WINDOW = 128
ROPE_THETA = 10000.0
NEG_INF = -1e30
N_WINDOW_LAYERS = DEPTH // N_MIXERS
PEER_HEADS = 8
PEER_TOPK = 16
N_KEYS = 128
N_EXPERTS = N_KEYS * N_KEYS
PEER_QDIM = 256
PEER_BLOCK = 128
N_MOD = 6


def rms_norm(x, gain):
    xf = x.astype(jnp.float32)
    y = xf * lax.rsqrt(jnp.mean(xf * xf, axis=-1, keepdims=True) + RMS_EPS)
    return (y * gain.astype(jnp.float32)).astype(x.dtype)

def axial_rope_tables(n_tokens, dtype):
    rows = n_tokens // GRID_W
    row = jnp.repeat(jnp.arange(rows), GRID_W).astype(jnp.float32)
    col = jnp.tile(jnp.arange(GRID_W), rows).astype(jnp.float32)
    half = HEAD_DIM // 2
    inv = ROPE_THETA ** (-jnp.arange(0, half, 2, dtype=jnp.float32) / half)
    ang = jnp.concatenate([row[:, None] * inv, col[:, None] * inv], axis=-1)
    return jnp.cos(ang).astype(dtype), jnp.sin(ang).astype(dtype)

def apply_axial_rope(x, cos, sin):
    n = x.shape[1]
    xr = x.reshape(x.shape[:-1] + (2, 2, HEAD_DIM // 4))
    x1 = xr[..., 0, :]
    x2 = xr[..., 1, :]
    c = cos.reshape(n, 1, 2, HEAD_DIM // 4)
    s = sin.reshape(n, 1, 2, HEAD_DIM // 4)
    out = jnp.stack([x1 * c - x2 * s, x1 * s + x2 * c], axis=-2)
    return out.reshape(x.shape)

def modulate(h, shift, scale):
    return h * (1 + scale) + shift

def project_qkv(h, w_qkv, q_gain, k_gain, rope):
    b, n, _ = h.shape
    y = h @ w_qkv
    q = y[..., : N_HEADS * HEAD_DIM].reshape(b, n, N_HEADS, HEAD_DIM)
    k = y[..., N_HEADS * HEAD_DIM:(N_HEADS + N_KV_HEADS) * HEAD_DIM].reshape(b, n, N_KV_HEADS, HEAD_DIM)
    v = y[..., (N_HEADS + N_KV_HEADS) * HEAD_DIM:].reshape(b, n, N_KV_HEADS, HEAD_DIM)
    q = rms_norm(q, q_gain)
    k = rms_norm(k, k_gain)
    if rope is not None:
        cos, sin = rope
        q = apply_axial_rope(q, cos, sin)
        k = apply_axial_rope(k, cos, sin)
    q = q.reshape(b, n, N_KV_HEADS, KV_REP, HEAD_DIM)
    return q, k, v

def latent_global_attention(q, k, v, kc, vc):
    b, n = q.shape[:2]
    nblk = n // Q_BLOCK
    scale = HEAD_DIM ** -0.5
    ka = jnp.concatenate([kc, k], axis=1)
    va = jnp.concatenate([vc, v], axis=1)
    qb = jnp.moveaxis(q.reshape(b, nblk, Q_BLOCK, N_KV_HEADS, KV_REP, HEAD_DIM), 1, 0)

    def attend_block(qblk):
        s = jnp.einsum('bqgrd,bkgd->bgrqk', qblk, ka).astype(jnp.float32) * scale
        p = jax.nn.softmax(s, axis=-1)
        return jnp.einsum('bgrqk,bkgd->bqgrd', p.astype(va.dtype), va)

    o = lax.map(attend_block, qb)
    return jnp.moveaxis(o, 0, 1).reshape(b, n, N_HEADS * HEAD_DIM)

def latent_window_attention(q, k, v, kc, vc, sink):
    b, n = q.shape[:2]
    nblk = n // Q_BLOCK
    span = Q_BLOCK + 2 * WINDOW
    scale = HEAD_DIM ** -0.5
    kp = jnp.pad(k, ((0, 0), (WINDOW, WINDOW), (0, 0), (0, 0)))
    vp = jnp.pad(v, ((0, 0), (WINDOW, WINDOW), (0, 0), (0, 0)))
    idx = jnp.arange(nblk)[:, None] * Q_BLOCK + jnp.arange(span)[None, :]
    kb = kp[:, idx]
    vb = vp[:, idx]
    kpos = idx - WINDOW
    qpos = jnp.arange(nblk)[:, None] * Q_BLOCK + jnp.arange(Q_BLOCK)[None, :]
    mask = ((kpos[:, None, :] >= 0) & (kpos[:, None, :] < n)
            & (jnp.abs(qpos[:, :, None] - kpos[:, None, :]) <= WINDOW))
    qb = q.reshape(b, nblk, Q_BLOCK, N_KV_HEADS, KV_REP, HEAD_DIM)
    s_loc = jnp.einsum('bnqgrd,bnkgd->bngrqk', qb, kb).astype(jnp.float32) * scale
    s_loc = jnp.where(mask[None, :, None, None], s_loc, NEG_INF)
    s_ctx = jnp.einsum('bnqgrd,bcgd->bngrqc', qb, kc).astype(jnp.float32) * scale
    sk = jnp.broadcast_to(sink.astype(jnp.float32).reshape(N_KV_HEADS, KV_REP, 1, 1),
                          s_loc.shape[:-1] + (1,))
    p = jax.nn.softmax(jnp.concatenate([s_loc, s_ctx, sk], axis=-1), axis=-1)
    p_loc = p[..., :span]
    p_ctx = p[..., span:span + kc.shape[1]]
    o = (jnp.einsum('bngrqk,bnkgd->bnqgrd', p_loc.astype(vb.dtype), vb)
         + jnp.einsum('bngrqc,bcgd->bnqgrd', p_ctx.astype(vc.dtype), vc))
    return o.reshape(b, n, N_HEADS * HEAD_DIM)

def context_attention(qc, kc, vc, sink):
    b, n = qc.shape[:2]
    scale = HEAD_DIM ** -0.5
    s = jnp.einsum('bqgrd,bkgd->bgrqk', qc, kc).astype(jnp.float32) * scale
    if sink is not None:
        sk = jnp.broadcast_to(sink.astype(jnp.float32).reshape(N_KV_HEADS, KV_REP, 1, 1),
                              s.shape[:-1] + (1,))
        p = jax.nn.softmax(jnp.concatenate([s, sk], axis=-1), axis=-1)[..., :n]
    else:
        p = jax.nn.softmax(s, axis=-1)
    o = jnp.einsum('bgrqk,bkgd->bqgrd', p.astype(vc.dtype), vc)
    return o.reshape(b, n, N_HEADS * HEAD_DIM)

def peer_block(hb, w_q, sub_keys, u_tab, v_tab):
    n = hb.shape[0]
    q = (hb @ w_q).reshape(n, PEER_HEADS, PEER_QDIM)
    q1 = q[..., : PEER_QDIM // 2]
    q2 = q[..., PEER_QDIM // 2:]
    s1 = jnp.einsum('nhd,kd->nhk', q1, sub_keys[0]).astype(jnp.float32)
    s2 = jnp.einsum('nhd,kd->nhk', q2, sub_keys[1]).astype(jnp.float32)
    v1, i1 = lax.top_k(s1, PEER_TOPK)
    v2, i2 = lax.top_k(s2, PEER_TOPK)
    cand_s = (v1[..., :, None] + v2[..., None, :]).reshape(n, PEER_HEADS, PEER_TOPK * PEER_TOPK)
    cand_i = (i1[..., :, None] * N_KEYS + i2[..., None, :]).reshape(n, PEER_HEADS, PEER_TOPK * PEER_TOPK)
    top_s, pos = lax.top_k(cand_s, PEER_TOPK)
    expert = jnp.take_along_axis(cand_i, pos, axis=-1)
    g = jax.nn.softmax(top_s, axis=-1)
    u = u_tab[expert]
    act = jax.nn.gelu(jnp.einsum('nhkd,nd->nhk', u, hb).astype(jnp.float32))
    w = (g * act).astype(hb.dtype)
    return jnp.einsum('nhk,nhkd->nd', w, v_tab[expert])

def peer_ffn(h, w_q, sub_keys, u_tab, v_tab):
    b, n, d = h.shape
    hb = h.reshape(-1, PEER_BLOCK, d)
    out = lax.map(lambda blk: peer_block(blk, w_q, sub_keys, u_tab, v_tab), hb)
    return out.reshape(b, n, d)

def second_inputs(seed: int = 0) -> dict:
    key = jax.random.key(seed)
    ks = jax.random.split(key, 18)
    f32 = jnp.float32
    x = jax.random.normal(ks[0], (BATCH, SEQ, D_MODEL), f32)
    c = jax.random.normal(ks[1], (BATCH, D_MODEL), f32)
    ctx = jax.random.normal(ks[2], (BATCH, CTX_LEN, D_MODEL), f32)
    c_ctx = jax.random.normal(ks[3], (D_MODEL,), f32)
    ada_w = jax.random.normal(ks[4], (DEPTH, D_MODEL, N_MOD * D_MODEL), f32) * (0.5 * D_MODEL ** -0.5)
    ada_b = jax.random.normal(ks[5], (DEPTH, N_MOD * D_MODEL), f32) * 0.1
    norm1_gain = 1.0 + 0.02 * jax.random.normal(ks[6], (DEPTH, D_MODEL), f32)
    norm2_gain = 1.0 + 0.02 * jax.random.normal(ks[7], (DEPTH, D_MODEL), f32)
    w_qkv = jax.random.normal(ks[8], (DEPTH, D_MODEL, QKV_DIM), f32) * D_MODEL ** -0.5
    q_norm_gain = 1.0 + 0.02 * jax.random.normal(ks[9], (DEPTH, HEAD_DIM), f32)
    k_norm_gain = 1.0 + 0.02 * jax.random.normal(ks[10], (DEPTH, HEAD_DIM), f32)
    w_o = jax.random.normal(ks[11], (DEPTH, N_HEADS * HEAD_DIM, D_MODEL), f32) * (N_HEADS * HEAD_DIM) ** -0.5
    attn_sinks = jax.random.normal(ks[12], (N_WINDOW_LAYERS, N_HEADS), f32) * 0.5
    peer_w_q = jax.random.normal(ks[13], (DEPTH, D_MODEL, PEER_HEADS * PEER_QDIM), f32) * D_MODEL ** -0.5
    peer_sub_keys = jax.random.normal(ks[14], (DEPTH, 2, N_KEYS, PEER_QDIM // 2), f32) * (PEER_QDIM // 2) ** -0.5
    peer_u = jax.random.normal(ks[15], (DEPTH, N_EXPERTS, D_MODEL), f32) * D_MODEL ** -0.5
    peer_v = jax.random.normal(ks[16], (DEPTH, N_EXPERTS, D_MODEL), f32) * PEER_HEADS ** -0.5
    return {"x": x, "c": c, "ctx": ctx, "c_ctx": c_ctx, "ada_w": ada_w, "ada_b": ada_b,
            "norm1_gain": norm1_gain, "norm2_gain": norm2_gain, "w_qkv": w_qkv,
            "q_norm_gain": q_norm_gain, "k_norm_gain": k_norm_gain, "w_o": w_o,
            "attn_sinks": attn_sinks, "peer_w_q": peer_w_q, "peer_sub_keys": peer_sub_keys,
            "peer_u": peer_u, "peer_v": peer_v}

def second_block(x, c, ctx, c_ctx, ada_w, ada_b, norm1_gain, norm2_gain, w_qkv, q_norm_gain,
              k_norm_gain, w_o, attn_sinks, peer_w_q, peer_sub_keys, peer_u, peer_v):
    n_lat = x.shape[1]
    rope = axial_rope_tables(n_lat, x.dtype)
    xc = ctx
    for i in range(DEPTH):
        last = i == DEPTH - 1
        mod = jax.nn.silu(c) @ ada_w[i] + ada_b[i]
        sh1, sc1, g1, sh2, sc2, g2 = [m[:, None, :] for m in jnp.split(mod, N_MOD, axis=-1)]
        modc = jax.nn.silu(c_ctx) @ ada_w[i] + ada_b[i]
        csh1, csc1, cg1, csh2, csc2, cg2 = jnp.split(modc, N_MOD, axis=-1)

        h = modulate(rms_norm(x, norm1_gain[i]), sh1, sc1)
        hc = modulate(rms_norm(xc, norm1_gain[i]), csh1, csc1)
        q, k, v = project_qkv(h, w_qkv[i], q_norm_gain[i], k_norm_gain[i], rope)
        qc, kc, vc = project_qkv(hc, w_qkv[i], q_norm_gain[i], k_norm_gain[i], None)
        if i % N_MIXERS == 0:
            o = latent_global_attention(q, k, v, kc, vc)
            sink = None
        else:
            sink = attn_sinks[i // N_MIXERS]
            o = latent_window_attention(q, k, v, kc, vc, sink)
        x = x + g1 * (o @ w_o[i])
        if not last:
            oc = context_attention(qc, kc, vc, sink)
            xc = xc + cg1 * (oc @ w_o[i])

        h2 = modulate(rms_norm(x, norm2_gain[i]), sh2, sc2)
        x = x + g2 * peer_ffn(h2, peer_w_q[i], peer_sub_keys[i], peer_u[i], peer_v[i])
        if not last:
            h2c = modulate(rms_norm(xc, norm2_gain[i]), csh2, csc2)
            xc = xc + cg2 * peer_ffn(h2c, peer_w_q[i], peer_sub_keys[i], peer_u[i], peer_v[i])
    return x


def setup_inputs(seed=0):
    out = dict(first_inputs(seed))
    for name, value in second_inputs(seed + 1).items():
        if name != "x":
            out[name + "_2"] = value
    return out


def reference(
    x, mem, ffn1_gate, ffn1_up, ffn1_down, w_in, conv_w, rec_lb, rec_norm_g, pool_w, pool_scale,
    w_out, ca_q, ca_k, ca_v, ca_o, ffn2_gate, ffn2_up, ffn2_down, ln_g, ln_b, c_2, ctx_2,
    c_ctx_2, ada_w_2, ada_b_2, norm1_gain_2, norm2_gain_2, w_qkv_2, q_norm_gain_2,
    k_norm_gain_2, w_o_2, attn_sinks_2, peer_w_q_2, peer_sub_keys_2, peer_u_2, peer_v_2,
):
    x = first_block(
        x, mem, ffn1_gate, ffn1_up, ffn1_down, w_in, conv_w, rec_lb, rec_norm_g, pool_w,
        pool_scale, w_out, ca_q, ca_k, ca_v, ca_o, ffn2_gate, ffn2_up, ffn2_down, ln_g, ln_b,
    )
    return second_block(
        x, c_2, ctx_2, c_ctx_2, ada_w_2, ada_b_2, norm1_gain_2, norm2_gain_2, w_qkv_2,
        q_norm_gain_2, k_norm_gain_2, w_o_2, attn_sinks_2, peer_w_q_2, peer_sub_keys_2,
        peer_u_2, peer_v_2,
    )


_drawn_inputs = setup_inputs


def setup_inputs(seed=0):
    import zlib

    import numpy as np

    out = dict(_drawn_inputs(seed))
    spreads = {}
    factors = {'rec_norm_g': 8.0,
     'pool_scale': 7.025,
     'norm1_gain_2': 8.0,
     'norm2_gain_2': 4.326,
     'q_norm_gain_2': 8.0,
     'k_norm_gain_2': 8.0,
     'attn_sinks_2': 8.0}
    for name, (base, spread) in spreads.items():
        noise = np.random.default_rng([zlib.crc32(name.encode()), seed]).standard_normal(out[name].shape)
        drawn = base * np.exp(spread * noise) if base else spread * noise
        out[name] = __import__('jax').numpy.asarray(drawn.astype(out[name].dtype))
    for name, factor in factors.items():
        out[name] = (out[name] * factor).astype(out[name].dtype)
    return out
```

```python
from contextlib import ExitStack, contextmanager

import numpy as np

import concourse.bass as bass
from concourse import mybir

F32 = mybir.dt.float32
BF16 = mybir.dt.bfloat16
U32 = mybir.dt.uint32
U8 = mybir.dt.uint8
ALU = mybir.AluOpType
ACT = mybir.ActivationFunctionType
AX = mybir.AxisListType.X

P = 128
D = 1024
KT = D // P
T = 256
NB = T // P
L = 2
FT = 2816 // P
ALPHA = (2.0 * L) ** 0.25
LN_EPS = 1e-5
RMS_EPS = 1e-6
CHUNK = 64
REC_H = 4
CA_H = 4
CA_SCALE = 256.0 ** -0.5
HEADS = 8
GROUPS = 2
REP = HEADS // GROUPS
SCALE = 128.0 ** -0.5
N_KEYS = 128
N_EXPERTS = N_KEYS * N_KEYS
PEER_H = 8
TOPK = 16
SLOTS = PEER_H * TOPK
LOWEST = -3.0e38
NEG = -1e30

WR = 4
MIX_CHUNKS = 64
ADA_CHUNKS, QKV_CHUNKS, WO_CHUNKS, PQ_CHUNKS = 48, 12, 8, 16
SECOND_CHUNKS = ADA_CHUNKS + QKV_CHUNKS + WO_CHUNKS + PQ_CHUNKS
GR = 8
FT_STEP = 4
FT_TURNS = (FT - 2) // FT_STEP
HEAD_SLOTS = GR
FT_SLOTS = (SLOTS - HEAD_SLOTS) // (FT_TURNS * FT_STEP)
TURN_SLOTS = FT_SLOTS * FT_STEP
assert HEAD_SLOTS + TURN_SLOTS * FT_TURNS == SLOTS and TURN_SLOTS % GR == 0

CONSTS = dict(ident=128, mean_d=128, rot=128, cos=256, sin=256, rcount=512, restart=256,
              iota=16)
FIRST = dict(ln_g=32, ln_b=32, conv_w=6, lb=4, omlb=4, norm_g=4, pool_scale=2, pool_w=256)
SECOND = dict(ada_b=L * 48, gain1=L * 8, gain2=L * 8, q_gain=L, k_gain=L, sinks=8, c=16)


def columns(parts):
    at, out = 0, {}
    for name, n in parts.items():
        out[name] = (at, n)
        at += n
    return out, at


AHEAD = dict(chunk_done=WR, gate_done=2, up_done=2, down_done=2, row_used=GR, h_done=1, z_done=1, hidden_done=1)


class Lane:

    def __init__(self, eng, refills=()):
        self.eng, self.refills, self.loops, self.count = eng, refills, [], {}

    def begin(self, name):
        return 0 if name in self.refills else AHEAD.get(name, 0)

    def now(self, sem, back=0):
        v = self.count.setdefault(sem.name, self.begin(sem.name)) - back
        for reg, per in self.loops:
            if per.get(sem.name):
                v = reg * per[sem.name] + v
        return v

    def skip(self, sem, by):
        self.count[sem.name] = self.count.get(sem.name, self.begin(sem.name)) + by

    def next(self, sem, by=1):
        self.skip(sem, by)
        return self.now(sem)

    def adds(self, sem, by=1):
        self.skip(sem, by)
        return by

    @contextmanager
    def loop(self, n, **per):
        begun = dict(self.count)
        with self.eng.Fori(0, n) as reg:
            self.loops.append((reg, per))
            yield reg
            self.loops.pop()
        for name, v in self.count.items():
            moved = v - begun.get(name, self.begin(name))
            assert moved == per.get(name, 0), (name, moved, per.get(name, 0))
            self.count[name] += (n - 1) * moved


def program(nc, a, out):
    with ExitStack() as ctx:
        def sems(names):
            return [ctx.enter_context(nc.semaphore(n)) for n in names.split()]

        (consts_in, window_in, vecs_in, masks_in, x_in, mem_in, ctx_in, subk_in) = sems(
            "consts_in window_in vecs_in masks_in x_in mem_in ctx_in subk_in")
        (chunk_done, gate_done, up_done, down_done) = sems(
            "chunk_done gate_done up_done down_done")
        (silu_done, hidden_done, resid_done, mean_done, centred_done, square_done, var_done, std_done,
         scaled_done, h_done) = sems(
            "silu_done hidden_done resid_done mean_done centred_done square_done var_done std_done "
            "scaled_done h_done")
        (layer_vecs, lb_max, lb_exp, eps_set, zeros_set) = sems(
            "layer_vecs lb_max lb_exp eps_set zeros_set")
        (z_done, f_done, log_done, decay_done, exp_done, qk_done, level_done, level_taken, o_done,
         o_square_done, o_ms_done, o_std_done) = sems(
            "z_done f_done log_done decay_done exp_done qk_done level_done level_taken o_done o_square_done "
            "o_ms_done o_std_done")
        (pooled_sums, pool_mm_done, pooled_done, conv_done, rec_done) = sems(
            "pooled_sums pool_mm_done pooled_done conv_done rec_done")
        (cs_done, cmax_done, cexp_done, cprob_done, cpt_done, cpt_taken, co_done, co_taken) = sems(
            "cs_done cmax_done cexp_done cprob_done cpt_done cpt_taken co_done co_taken")
        (c_silu, mods_done, sq2_done, ms2_done, std2_done, norm2_done, mod2_done) = sems(
            "c_silu mods_done sq2_done ms2_done std2_done norm2_done mod2_done")
        (qkv_taken, qk_sq_done, qk_ms_done, qk_std_done, qk_normed, rot_done, roped) = sems(
            "qkv_taken qk_sq_done qk_ms_done qk_std_done qk_normed rot_done roped")
        (s_done, s_taken, s_max, sink_exp, s_exp, s_prob, pt_done, pt_taken, pv_done, pv_taken, x_added) = sems(
            "s_done s_taken s_max sink_exp s_exp s_prob pt_done pt_taken pv_done pv_taken x_added")
        (tm_done, tm_taken, pq_taken, sc_done, sc_taken, top_ready, top_exp, idx_done) = sems(
            "tm_done tm_taken pq_taken sc_done sc_taken top_ready top_exp idx_done")
        (idx_now_done, row_used, dots_done, gelu_done, pout_done, po_tm_done, x_final) = sems(
            "idx_now_done row_used dots_done gelu_done pout_done po_tm_done x_final")
        (pool_pause, dve_pause, dve_step, pool_step, stored) = sems(
            "pool_pause dve_pause dve_step pool_step stored")
        weights_in = sems(" ".join(f"weights_{s}" for s in range(WR)))
        rows_in = sems(" ".join(f"rows_{s}" for s in range(GR)))
        ff_in = [sems(f"{part}_in_0 {part}_in_1") for part in ("gate", "up", "down")]
        ff_done = [gate_done, up_done, down_done]

        def sb(name, cols, dt=F32):
            return ctx.enter_context(nc.sbuf_tensor(name, [P, cols], dt))

        def view(tile, at, *dims):
            n = int(np.prod(dims))
            names = [f"d{i}" for i in range(len(dims))]
            if len(dims) == 1:
                return tile[:, at:at + n]
            return tile[:, at:at + n].rearrange(f"p ({' '.join(names)}) -> p {' '.join(names)}",
                                                **dict(zip(names[1:], dims[1:])))

        x_t = view(sb("x_t", KT * T), 0, KT, T)
        mem_tile = sb("mem_t", KT * T)
        mem_t = view(mem_tile, 0, KT, T)
        window = view(mem_tile, 0, NB, T)
        ctx_t = view(sb("ctx_t", KT * T), 0, KT, T)
        h_tm = view(sb("h_tm", NB * D), 0, NB, D)
        rows = view(sb("rows", GR * D), 0, GR, D)
        fw = view(sb("fw", 2 * 3 * D), 0, 2, 3, D)
        wring = view(sb("wring", WR * D), 0, WR, D)
        keys_t = view(sb("keys_t", GROUPS * 2 * T), 0, GROUPS, 2 * T)
        vals_tile = sb("vals", 4 * T)
        vals = view(vals_tile, 0, 4, GROUPS * P)
        cc, n_consts = columns(CONSTS)
        fc, n_first = columns(FIRST)
        sc_, n_second = columns(SECOND)
        consts = sb("consts", n_consts)
        masks_u32 = sb("masks", 8 * P // 4, U32)
        masks = masks_u32[:, :].bitcast(U8).rearrange("p (i t) -> p i t", t=P)
        first = sb("first", L * n_first)
        cur = sb("cur", n_first)
        second = sb("second", n_second)
        subk = view(sb("subk", L * 2 * N_KEYS), 0, L, 2, N_KEYS)
        mods = view(sb("mods", L * 48 * 2), 0, L, 48, 2)
        gains = view(sb("gains", L * 2 * 8 * 2), 0, L, 2, 8, 2)
        idx = view(sb("idx", NB * SLOTS, U32), 0, NB, SLOTS)
        idx_now = view(sb("idx_now", 2 * GR, U32), 0, 2, GR)
        gates = view(sb("gates", NB * SLOTS), 0, NB, SLOTS)
        dots = sb("dots", SLOTS)
        wts = sb("wts", SLOTS)
        stage = sb("stage", TURN_SLOTS)
        zeros = sb("zeros", 512, BF16)
        eps = sb("eps", 2)
        cond = sb("cond", 2 * KT)
        std = sb("std", T)
        stats = sb("stats", 64)
        lbs = sb("lbs", 32)
        arena = sb("arena", 19044)

        def const(name, *dims):
            at, n = cc[name]
            return view(consts, at, *(dims or (n,)))

        ident, mean_d, rot = const("ident"), const("mean_d"), const("rot")
        cos, sin, restart, iota = const("cos"), const("sin"), const("restart"), const("iota")
        rcount = const("rcount", 2, T)

        def vec(tile, where, name, i=0, n=1):
            at = where[name][0] + i
            return tile[:, at:at + n]

        resid = view(arena, 0, KT, T)
        mix = view(arena, 0, KT, T)
        sq = view(arena, 2048, KT, T)
        z_f, z_q, z_g = (view(arena, 2048 + 1024 * i, REC_H, T) for i in range(3))
        z_h, z_c, z_b = (view(arena, 5120 + 512 * i, 2, T) for i in range(3))
        v_tm = view(arena, 6656, NB, 2, T)
        ca_q, ca_o = (view(arena, 2048 + 2048 * i, KT, T) for i in range(2))
        csum = view(arena, 7680, 4, T)
        dec = [view(arena, 8704 + 1024 * i, 4, T) for i in range(2)]
        ca_e = [view(arena, 7680 + 1024 * i, CA_H, T) for i in range(2)]
        ca_pt = view(arena, 9728, NB, CA_H, P)
        qk = [[view(arena, 10752 + 2048 * i + 1024 * j, 4, T) for j in range(2)] for i in range(2)]
        ca_k = view(arena, 10752, KT, T)
        ca_v = view(arena, 12800, CA_H, NB, T)
        acc2 = [view(arena, 10752 + D * i, D) for i in range(2)]
        attn = view(arena, 14848, 3, REC_H, P)
        conv_u = view(arena, 16384, 2, T + 2)
        pool_u = view(arena, 16900, 2, T + 16)
        pool_s = [view(arena, 17444 + 544 * i, 2, T + 16) for i in range(2)]
        pool_p = view(arena, 18532, 2, T)
        silu = view(arena, 17444, 2, T)
        hidden = view(arena, 17956, 2, T)

        sq2 = view(arena, 0, KT, T)
        scores = view(arena, 0, REP, 2 * T)
        pscore = view(arena, 0, 2 * PEER_H, N_KEYS)
        h2 = view(arena, 2048, KT, T)
        top_i = view(arena, 2048, 2 * PEER_H, TOPK)
        top_sc = view(arena, 2304, PEER_H, TOPK)
        sel = [view(arena, 2432 + 128 * i, SLOTS) for i in range(6)]
        qk_raw = view(arena, 4096, 10, T)
        qk_n = view(arena, 6656, 10, T)
        qk_r = view(arena, 9216, 10, T)
        pt = view(arena, 9216, 4, REP * P)
        o_t = view(arena, 11264, HEADS, T)
        pq_t = view(arena, 4096, 16, T)
        cand = view(arena, 8192, PEER_H, TOPK, TOPK)
        onehot = [view(arena, 10240 + 2048 * i, PEER_H, TOPK, TOPK) for i in range(2)]
        cand2 = view(arena, 14336, PEER_H, TOPK * TOPK)
        pscore2 = view(arena, 16384, 2 * PEER_H, N_KEYS)
        top_v = view(arena, 18432, 2 * PEER_H, TOPK)
        top_iu = arena[:, 18688:18944].bitcast(U32).rearrange("p (j k) -> p j k", k=TOPK)
        pos_u = arena[:, 3200:3584].bitcast(U32)

        ps_a = ctx.enter_context(nc.psum_tensor("ps_a", [P, 2048], F32))
        ps_b = ctx.enter_context(nc.psum_tensor("ps_b", [P, 1024], F32))
        ps_c = ctx.enter_context(nc.psum_tensor("ps_c", [P, 512], F32))
        ps_d = ctx.enter_context(nc.psum_tensor("ps_d", [P, 512], F32))
        acc_t = view(ps_a, 0, KT, T)
        block = ctx.enter_context(nc.Block())

        @block.sync
        def _(eng):
            sp = Lane(eng, ("chunk_done", "gate_done", "up_done", "down_done"))
            eng.dma_start(consts[:, :], a["consts"]).then_inc(consts_in, 16)
            eng.dma_start(second[:, :], a["vecs2"]).then_inc(vecs_in, 16)
            eng.dma_start(ctx_t, a["ctx_t"]).then_inc(ctx_in, 16)
            eng.dma_start(subk, a["subk"]).then_inc(subk_in, 16)
            eng.dma_start(first[:, :], a["vecs1"]).then_inc(vecs_in, 16)
            eng.dma_start(masks_u32[:, :], a["masks"]).then_inc(masks_in, 16)
            eng.dma_start(x_t, a["x_t"]).then_inc(x_in, 16)
            eng.dma_start(mem_t, a["mem_t"]).then_inc(mem_in, 16)

            def chunk_loads(src, at, n):
                def load(s, row):
                    eng.wait_ge(chunk_done, sp.next(chunk_done))
                    eng.dma_start(wring[:, s, :], row).then_inc(weights_in[s], sp.adds(weights_in[s], 16))
                turns = n // WR
                per = {f"weights_{s}": 16 for s in range(WR)}
                if turns > 2:
                    with sp.loop(turns, chunk_done=WR, **per) as i:
                        for s in range(WR):
                            load(s, src[bass.ds(i * WR + (at + s), 1), :, :].rearrange("a p c -> (a p) c"))
                else:
                    for j in range(n):
                        load(j % WR, src[bass.ds(at + j, 1), :, :].rearrange("a p c -> (a p) c"))

            def ff_loads(tile, ft, part):
                eng.wait_ge(ff_done[part], sp.next(ff_done[part]))
                eng.dma_start(
                    fw[:, ft % 2, part, :], a["ffn"][bass.ds(tile, 1), part, :, :].rearrange("a p c -> (a p) c")).then_inc(ff_in[part][ft % 2], sp.adds(ff_in[part][ft % 2], 16))

            chunk_loads(a["second_w"], 0, SECOND_CHUNKS)
            chunk_loads(a["second_w"], SECOND_CHUNKS, ADA_CHUNKS)
            ff_per = {f"{n}_in_{s}": 16 for n in ("gate", "up", "down") for s in range(2)}
            ff_turn = {k: 16 * FT_STEP // 2 for k in ff_per} | dict(gate_done=FT_STEP, up_done=FT_STEP,
                                                                    down_done=FT_STEP)
            ff_layer = {k: 16 * FT for k in ff_per} | dict(gate_done=2 * FT, up_done=2 * FT, down_done=2 * FT)
            with sp.loop(L, chunk_done=MIX_CHUNKS, **{f"weights_{s}": 16 * MIX_CHUNKS // WR for s in range(WR)},
                         **ff_layer) as l:
                for w in range(2):
                    for ft in range(2):
                        for part in range(3):
                            ff_loads(l * (2 * FT) + (w * FT + ft), ft, part)
                    if w == 0:
                        chunk_loads(a["mix_w"], l * MIX_CHUNKS, WR)
                    else:
                        chunk_loads(a["mix_w"], l * MIX_CHUNKS + (MIX_CHUNKS - WR), WR)
                    with sp.loop(FT_TURNS, **ff_turn) as i:
                        for ft in range(FT_STEP):
                            for part in range(3):
                                ff_loads(l * (2 * FT) + (w * FT + 2 + ft) + i * FT_STEP, ft, part)
                    if w == 0:
                        chunk_loads(a["mix_w"], l * MIX_CHUNKS + WR, MIX_CHUNKS - 2 * WR)
            chunk_loads(a["second_w"], ADA_CHUNKS, SECOND_CHUNKS - ADA_CHUNKS)
            chunk_loads(a["second_w"], SECOND_CHUNKS + ADA_CHUNKS + 8, 4)
            eng.wait_ge(chunk_done, sp.now(chunk_done))
            eng.dma_start(window, a["window"]).then_inc(window_in, 16)
            chunk_loads(a["second_w"], SECOND_CHUNKS + ADA_CHUNKS, SECOND_CHUNKS - ADA_CHUNKS)
            eng.wait_ge(x_final, sp.next(x_final, 3))
            eng.dma_start(out, x_t).then_inc(stored, 16)
            eng.wait_ge(stored, 16)

        @block.gpsimd
        def _(eng):
            po = Lane(eng, ("row_used",))
            G = nc.gpsimd

            def pause():
                eng.sem_inc(pool_pause, 1)

            def gather(table, where, base=None):
                per = {f"rows_{s}": 32 for s in range(GR)}
                with po.loop(SLOTS // (2 * GR), row_used=2 * GR, idx_now_done=2, **per) as i:
                    for half in range(2):
                        eng.wait_ge(row_used, po.now(row_used, -1))
                        G.tensor_copy(
                            idx_now[:, half, :], where[:, bass.ds(i * (2 * GR) + half * GR, GR)]).then_inc(idx_now_done, po.adds(idx_now_done))
                        eng.wait_ge(idx_now_done, po.now(idx_now_done))
                        for s in range(GR):
                            eng.wait_ge(row_used, po.next(row_used))
                            pause()
                            G.indirect_dma_start(
                                rows[:, s, :], None, table,
                                bass.IndirectOffsetOnAxis(ap=idx_now[:, half, s:s + 1], axis=0)).then_inc(rows_in[s], po.adds(rows_in[s], 16))

            def pooling():
                def step(ins):
                    ins.then_inc(pool_step, po.adds(pool_step))
                    eng.wait_ge(pool_step, po.now(pool_step))
                eng.wait_ge(z_done, po.next(z_done, 10))
                s0, s1 = pool_s
                src, n = pool_u, 1
                for g, dst in enumerate((s0, s1, s0, s1)):
                    step(G.tensor_tensor(dst[:, :, 2 * n - 1:], src[:, :, 2 * n - 1:],
                                         src[:, :, n - 1:T + 16 - n], ALU.add))
                    t, half = g // 2, slice(64 * (g % 2), 64 * (g % 2) + 64)
                    step(G.tensor_tensor(pool_p[half, t, :], dst[half, t, 16:], rcount[half, t, :], ALU.mult))
                    last = G.tensor_tensor(pool_p[half, t, :], pool_p[half, t, :], pool_u[half, t, 16:], ALU.subtract)
                    if g < 3:
                        step(last)
                    src, n = dst, 2 * n
                last.then_inc(pooled_sums, po.adds(pooled_sums))
                eng.wait_ge(pooled_sums, po.now(pooled_sums))
                pause()
                po.skip(z_done, 14)

            slots = dict(row_used=2 * SLOTS, idx_now_done=4 * SLOTS // (2 * GR),
                         **{f"rows_{s}": 64 * SLOTS // (2 * GR) for s in range(GR)})
            eng.wait_ge(idx_done, po.next(idx_done, 2))
            with po.loop(L, z_done=24, pooled_sums=1, pool_step=11, **slots) as l:
                where = idx[:, bass.ds(l, 1), :].rearrange("p a s -> p (a s)")
                gather(a["peer_u"], where)
                pooling()
                gather(a["peer_v"], where)
            with po.loop(L, idx_done=2, **{k: 2 * v for k, v in slots.items()}):
                eng.wait_ge(idx_done, po.next(idx_done, 2))
                pause()
                for b in range(NB):
                    gather(a["peer_u"], idx[:, b, :])
                    gather(a["peer_v"], idx[:, b, :])

        @block.tensor
        def _(eng):
            pe = Lane(eng)
            mm = nc.tensor.matmul

            def chunk(s):
                eng.wait_ge(weights_in[s], pe.next(weights_in[s], 16))
                return wring[:, s, :]

            def acc_groups(src, act_ready=None):
                for j in range(KT):
                    w = chunk(j % WR)
                    for k in range(KT):
                        if j == 0 and act_ready:
                            act_ready(k)
                        ins = mm(acc_t[:, j, :], w[:, k * P:(k + 1) * P], src[:, k, :], start=k == 0, stop=k == KT - 1)
                    ins.then_inc(chunk_done, pe.adds(chunk_done))

            def fm_group(c, bank, src, act_ready=None):
                for t in range(2):
                    w = chunk((c + t) % WR)
                    for k in range(KT):
                        if t == 0 and act_ready:
                            act_ready(k)
                        ins = mm(bank[:, t * T:(t + 1) * T], w[:, k * P:(k + 1) * P], src[:, k, :],
                                 start=k == 0, stop=k == KT - 1)
                    ins.then_inc(chunk_done, pe.adds(chunk_done))

            def tm_group(c, bank, src):
                w = [chunk((c + t) % WR) for t in range(2)]
                for b in range(NB):
                    for k in range(KT):
                        ins = mm(bank[:, b * T:(b + 1) * T], src[:, k, b * P:(b + 1) * P],
                                 w[k // 4][:, (k % 4) * T:(k % 4 + 1) * T], start=k == 0, stop=k == KT - 1)
                        if b == NB - 1 and k in (3, 7):
                            ins.then_inc(chunk_done, pe.adds(chunk_done))

            def mean_of(src, bank, weights, ready, n_ready):
                for k in range(KT):
                    if k % (KT // n_ready) == 0:
                        eng.wait_ge(ready, pe.next(ready))
                    ins = mm(bank, weights, src[:, k, :], start=k == 0, stop=k == KT - 1)
                return ins

            def ada(l):
                with pe.loop(ADA_CHUNKS // WR, chunk_done=WR, **{f"weights_{s}": 16 for s in range(WR)}) as i:
                    for s in range(WR):
                        w = chunk(s)
                        for k in range(KT):
                            ins = mm(ps_d[:, bass.ds(i * (2 * WR) + 2 * s, 2)], w[:, k * P:(k + 1) * P],
                                     cond[:, 2 * k:2 * k + 2], start=k == 0, stop=k == KT - 1)
                        ins.then_inc(chunk_done, pe.adds(chunk_done))

            def rms():
                mean_of(sq2, ps_c[:, 0:T], mean_d, sq2_done, 4).then_inc(ms2_done, pe.adds(ms2_done))

            def mod_ready(k):
                eng.wait_ge(mod2_done, pe.next(mod2_done))

            def qkv(full, c0=0):
                ready = mod_ready
                for g in range(4 if full else 0):
                    if g >= 2:
                        eng.wait_ge(qkv_taken, pe.next(qkv_taken))
                    fm_group(2 * g, ps_b[:, (g % 2) * 512:(g % 2 + 1) * 512], h2, ready)
                    ready = None
                if full:
                    eng.wait_ge(qkv_taken, pe.next(qkv_taken))
                fm_group(0, ps_b[:, 0:512], h2, ready)
                if full:
                    eng.wait_ge(qkv_taken, pe.next(qkv_taken))
                tm_group(2, ps_b[:, 512:1024], h2)
                eng.wait_ge(qkv_taken, pe.next(qkv_taken, 2))

            def qk_stats(banks):
                for j, bank in banks:
                    eng.wait_ge(qk_sq_done, pe.next(qk_sq_done))
                    ins = mm(bank, mean_d, view(arena, 9216 + 512 * j, 512), start=True, stop=True)
                ins.then_inc(qk_ms_done, pe.adds(qk_ms_done))

            qk_banks = [(j, ps_a[:, j * 512:(j + 1) * 512]) for j in range(4)] + [(4, ps_d[:, :])]

            def rotate():
                eng.wait_ge(qk_normed, pe.next(qk_normed))
                for j, bank in qk_banks:
                    ins = mm(bank, rot, view(arena, 6656 + 512 * j, 512), start=True, stop=True)
                ins.then_inc(rot_done, pe.adds(rot_done))

            def attention(blocks):
                n, units = len(blocks) * P, NB * GROUPS
                eng.wait_ge(roped, pe.next(roped))

                def unit_scores(u):
                    b, g = u // GROUPS, u % GROUPS
                    if u:
                        eng.wait_ge(s_taken, pe.next(s_taken))
                    for r in range(REP):
                        ins = mm(ps_a[:, r * 512:r * 512 + n], qk_n[:, REP * g + r, b * P:(b + 1) * P],
                                 keys_t[:, g, 0:n], start=True, stop=True)
                    ins.then_inc(s_done, pe.adds(s_done))

                unit_scores(0)
                for u in range(units):
                    if u + 1 < units:
                        unit_scores(u + 1)
                    eng.wait_ge(s_prob, pe.next(s_prob))
                    for j in blocks:
                        if u or j >= 2:
                            eng.wait_ge(pt_taken, pe.next(pt_taken))
                        for r in range(REP):
                            ins = nc.tensor.transpose((ps_c, ps_d)[j % 2][:, r * P:(r + 1) * P],
                                                      scores[:, r, j * P:(j + 1) * P], ident)
                        ins.then_inc(pt_done, pe.adds(pt_done))
                    eng.wait_ge(pt_taken, pe.now(pt_taken, -2))
                    if u >= 2:
                        eng.wait_ge(pv_taken, pe.next(pv_taken))
                    for j in blocks:
                        ins = mm(ps_b[:, (u % 2) * 512:(u % 2 + 1) * 512], vals[:, j, u % GROUPS * P:(u % GROUPS + 1) * P],
                                 pt[:, j, :], start=j == blocks[0], stop=j == blocks[-1])
                    ins.then_inc(pv_done, pe.adds(pv_done))
                pe.skip(pt_taken, 2)
                eng.wait_ge(s_taken, pe.next(s_taken))
                eng.wait_ge(pv_taken, pe.next(pv_taken, 2))

            def project_out():
                acc_groups(o_t)

            def peer_scores(l):
                rms()
                for k in range(KT):
                    eng.wait_ge(mod2_done, pe.next(mod2_done))
                for b in range(NB):
                    for k in range(KT):
                        ins = nc.tensor.transpose(ps_a[:, b * D + k * P:b * D + (k + 1) * P],
                                                  h2[:, k, b * P:(b + 1) * P], ident)
                ins.then_inc(tm_done, pe.adds(tm_done))
                for g in range(8):
                    if g >= 2:
                        eng.wait_ge(pq_taken, pe.next(pq_taken))
                    fm_group(2 * g, ps_b[:, (g % 2) * 512:(g % 2 + 1) * 512], h2)
                eng.wait_ge(pq_taken, pe.next(pq_taken, 2))
                eng.wait_ge(tm_taken, pe.next(tm_taken))
                for b in range(NB):
                    if b:
                        eng.wait_ge(sc_taken, pe.next(sc_taken))
                    for j in range(2 * PEER_H):
                        ins = mm(ps_a[:, j * N_KEYS:(j + 1) * N_KEYS], pq_t[:, j, b * P:(b + 1) * P],
                                 subk[:, l, j % 2, :], start=True, stop=True)
                    ins.then_inc(sc_done, pe.adds(sc_done))
                eng.wait_ge(sc_taken, pe.next(sc_taken))

            def finish():
                eng.wait_ge(pout_done, pe.next(pout_done, NB))
                for k in range(KT):
                    for b in range(NB):
                        ins = nc.tensor.transpose(acc_t[:, k, b * P:(b + 1) * P], h_tm[:, b, k * P:(k + 1) * P], ident)
                ins.then_inc(po_tm_done, pe.adds(po_tm_done))

            eng.sem_inc(chunk_done, AHEAD["chunk_done"])
            eng.sem_inc(gate_done, AHEAD["gate_done"])
            eng.sem_inc(up_done, AHEAD["up_done"])
            eng.sem_inc(down_done, AHEAD["down_done"])
            eng.wait_ge(consts_in, 16)
            eng.wait_ge(subk_in, 16)
            eng.wait_ge(c_silu, pe.next(c_silu))
            ada(0)
            rms()
            qkv(True)
            qk_stats(qk_banks)
            attention([0, 1])
            project_out()
            peer_scores(0)
            ada(1)

            eng.wait_ge(x_in, 16)
            eng.wait_ge(mem_in, 16)
            eng.wait_ge(zeros_set, 1)

            def feed_forward(h_ready):
                for j in range(4):
                    mm(ps_a[:, j * 512:(j + 1) * 512], zeros[:, 0:P], zeros[:, :], start=True, stop=False,
                       skip_group_check=True)

                def gate_up(ft, first=False):
                    bank = ps_b[:, (ft % 2) * 512:(ft % 2 + 1) * 512]
                    for part in range(2):
                        eng.wait_ge(ff_in[part][ft % 2], pe.next(ff_in[part][ft % 2], 16))
                        for k in range(KT):
                            if first and part == 0:
                                h_ready(k)
                            ins = mm(bank[:, part * T:(part + 1) * T], fw[:, ft % 2, part, k * P:(k + 1) * P],
                                     x_t[:, k, :], start=k == 0, stop=k == KT - 1)
                        ins.then_inc(ff_done[part], pe.adds(ff_done[part]))

                def down(ft, last=False):
                    eng.wait_ge(hidden_done, pe.next(hidden_done))
                    eng.wait_ge(ff_in[2][ft % 2], pe.next(ff_in[2][ft % 2], 16))
                    for j in range(KT):
                        ins = mm(acc_t[:, j, :], fw[:, ft % 2, 2, j * P:(j + 1) * P], hidden[:, ft % 2, :],
                                 start=False, stop=last, skip_group_check=True)
                        if j == KT - 1:
                            ins.then_inc(down_done, pe.adds(down_done))

                gate_up(0, True)
                per = {f"{n}_in_{s}": 16 * FT_STEP // 2 for n in ("gate", "up", "down") for s in range(2)}
                with pe.loop(FT_TURNS, hidden_done=FT_STEP, gate_done=FT_STEP, up_done=FT_STEP, down_done=FT_STEP,
                             **per):
                    for q in range(FT_STEP):
                        gate_up(q + 1)
                        down(q)
                gate_up(FT - 1)
                down(FT - 2)
                down(FT - 1, True)

            def layer_norm():
                mean_of(resid, ps_c[:, 0:T], mean_d, resid_done, 4).then_inc(mean_done, pe.adds(mean_done))
                mean_of(sq, ps_d[:, 0:T], mean_d, square_done, 4).then_inc(var_done, pe.adds(var_done))

            def h_take(k):
                eng.wait_ge(h_done, pe.next(h_done))

            def h_have(k):
                if k == 0:
                    eng.wait_ge(h_done, pe.now(h_done))

            ff = {f"{n}_in_{s}": 16 * FT for n in ("gate", "up", "down") for s in range(2)}
            with pe.loop(L, chunk_done=MIX_CHUNKS, **{f"weights_{s}": 16 * MIX_CHUNKS // WR for s in range(WR)},
                         hidden_done=2 * FT, gate_done=2 * FT, up_done=2 * FT, down_done=2 * FT, **ff,
                         h_done=4 * KT, resid_done=16, square_done=16, mean_done=4, var_done=4, z_done=24,
                         qk_done=9, level_done=9, level_taken=9, o_done=1, o_square_done=2, o_ms_done=1,
                         pooled_sums=1, pool_mm_done=1, pooled_done=1, conv_done=1, rec_done=1, cs_done=NB,
                         cprob_done=NB, cpt_done=2 * NB, cpt_taken=2 * NB, co_done=NB, co_taken=NB) as l:
                feed_forward(h_have)
                layer_norm()

                def group(g, c, src, ready=None, tm=False):
                    if g:
                        eng.wait_ge(z_done, pe.now(z_done, 1))
                    bank = ps_b[:, (g % 2) * 512:(g % 2 + 1) * 512]
                    if tm:
                        tm_group(c, bank, src)
                    else:
                        fm_group(c, bank, src, ready)
                    pe.skip(z_done, 1)

                def level(i):
                    eng.wait_ge(qk_done, pe.next(qk_done))
                    if i >= 2:
                        eng.wait_ge(level_taken, pe.next(level_taken))
                    q, k = (z_q, z_f) if i == 0 else qk[i % 2]
                    for b in range(NB if i < 8 else 1):
                        for h in range(REC_H):
                            ks = slice(b * P, (b + 1) * P)
                            qs = ks if i < 8 else slice(P, 2 * P)
                            ins = mm(ps_a[:, (i % 2) * 1024 + b * 512 + h * P:(i % 2) * 1024 + b * 512 + (h + 1) * P],
                                     k[:, h, ks], q[:, h, qs], start=True, stop=True)
                    ins.then_inc(level_done, pe.adds(level_done))

                for g in range(4):
                    group(g, 2 * g, x_t, h_take if g == 0 else None)
                for g in range(4, 12):
                    group(g, 2 * g, x_t, tm=g < 6)
                    level(g - 4)
                level(8)
                eng.wait_ge(level_taken, pe.next(level_taken, 2))
                eng.wait_ge(z_done, pe.now(z_done, 0))
                for h in range(REC_H):
                    o = ps_a[:, 1024 + h * T:1024 + (h + 1) * T]
                    vs = [v_tm[:, h // 2, b, (h % 2) * P:(h % 2 + 1) * P] for b in range(NB)]
                    mm(o[:, 0:P], vs[0], attn[:, 0, h, :], start=True, stop=True)
                    mm(o[:, P:T], vs[0], attn[:, 2, h, :], start=True, stop=False)
                    ins = mm(o[:, P:T], vs[1], attn[:, 1, h, :], start=False, stop=True)
                ins.then_inc(o_done, pe.adds(o_done))
                eng.wait_ge(pooled_sums, pe.next(pooled_sums))
                eng.wait_ge(mods_done, L)
                for t in range(2):
                    at = fc["pool_w"][0] + t * P
                    ins = mm(ps_d[:, t * T:(t + 1) * T], cur[:, at:at + P], pool_p[:, t, :], start=True, stop=True)
                ins.then_inc(pool_mm_done, pe.adds(pool_mm_done))
                group(12, 24, mem_t)
                for j in range(2):
                    eng.wait_ge(o_square_done, pe.next(o_square_done))
                    ins = mm(ps_a[:, j * 512:(j + 1) * 512], mean_d, view(arena, 8704 + 512 * j, 512),
                             start=True, stop=True)
                ins.then_inc(o_ms_done, pe.adds(o_ms_done))
                for g in range(13, 20):
                    group(g, 2 * g, mem_t, tm=g >= 16)
                for part_done in (pooled_done, conv_done, rec_done):
                    eng.wait_ge(part_done, pe.next(part_done))
                acc_groups(mix)
                layer_norm()
                for g in range(20, 24):
                    group(g, 2 * g, x_t, h_take if g == 20 else None)
                eng.wait_ge(z_done, pe.now(z_done, 0))
                def ca_scores(b):
                    for h in range(CA_H):
                        for c in range(2):
                            ins = mm(ps_a[:, b * 1024 + h * T:b * 1024 + (h + 1) * T],
                                     ca_q[:, 2 * h + c, b * P:(b + 1) * P], ca_k[:, 2 * h + c, :],
                                     start=c == 0, stop=c == 1)
                    ins.then_inc(cs_done, pe.adds(cs_done))
                ca_scores(0)
                ca_scores(1)
                for b in range(NB):
                    eng.wait_ge(cprob_done, pe.next(cprob_done))
                    for m in range(NB):
                        for h in range(CA_H):
                            ins = nc.tensor.transpose((ps_c, ps_d)[m][:, h * P:(h + 1) * P],
                                                      ca_e[b][:, h, m * P:(m + 1) * P], ident)
                        ins.then_inc(cpt_done, pe.adds(cpt_done))
                    eng.wait_ge(cpt_taken, pe.next(cpt_taken, 2))
                    if b:
                        eng.wait_ge(co_taken, pe.next(co_taken))
                    for h in range(CA_H):
                        for c in range(2):
                            for m in range(NB):
                                ins = mm(ps_b[:, (2 * h + c) * P:(2 * h + c + 1) * P],
                                         ca_v[:, h, m, c * P:(c + 1) * P], ca_pt[:, m, h, :],
                                         start=m == 0, stop=m == 1)
                    ins.then_inc(co_done, pe.adds(co_done))
                eng.wait_ge(co_taken, pe.next(co_taken))
                acc_groups(ca_o)
                layer_norm()
                feed_forward(h_take)
                layer_norm()
                pe.skip(h_done, KT)

            finish()
            for l in range(L):
                rms()
                qkv(True)
                qk_stats(qk_banks)
                rotate()
                attention([0, 1, 2, 3])
                project_out()
                peer_scores(l)
                if l == 0:
                    rms()
                    qkv(False)
                    qk_stats(qk_banks[4:])
                    eng.wait_ge(roped, pe.next(roped))
                finish()

        @block.scalar
        def _(eng):
            ac = Lane(eng)

            def act(out, in_, func, **k):
                return nc.scalar.activation(out, in_, func, **k)

            def rms(src, l, part, who):
                for j in range(4):
                    act(
                        sq2[:, 2 * j:2 * j + 2, :], src[:, 2 * j:2 * j + 2, :], ACT.Square).then_inc(sq2_done, ac.adds(sq2_done))
                eng.wait_ge(ms2_done, ac.next(ms2_done))
                act(std[:, :], ps_c[:, 0:T], ACT.Sqrt, bias=eps[:, 1:2]).then_inc(std2_done, ac.adds(std2_done))
                for k in range(KT):
                    if k % 2 == 0:
                        eng.wait_ge(norm2_done, ac.next(norm2_done))
                    act(h2[:, k, :], h2[:, k, :], ACT.Identity, scale=gains[:, l, part, k, who:who + 1],
                                            bias=mods[:, l, 24 * part + k, who:who + 1]).then_inc(mod2_done, ac.adds(mod2_done))

            def qkv(full, first_block):
                for g in (range(5) if full else [4]):
                    bank = ps_b[:, (g % 2) * 512:(g % 2 + 1) * 512]
                    eng.wait_ge(chunk_done, ac.next(chunk_done, 2))
                    act(view(arena, 9216 + 512 * g, 512), bank, ACT.Square).then_inc(qk_sq_done, ac.adds(qk_sq_done))
                    act(view(arena, 4096 + 512 * g, 512), bank, ACT.Copy).then_inc(qkv_taken, ac.adds(qkv_taken))
                eng.wait_ge(chunk_done, ac.next(chunk_done, 2))
                act(
                    view(vals_tile, first_block * T, 512), ps_b[:, 512:1024], ACT.Copy).then_inc(qkv_taken, ac.adds(qkv_taken))
                eng.wait_ge(qk_ms_done, ac.next(qk_ms_done))
                if full:
                    act(view(arena, 9216, 2048), ps_a[:, :], ACT.Sqrt, scale=D / P, bias=eps[:, 1:2])
                act(view(arena, 9216 + 2048, 512), ps_d[:, :], ACT.Sqrt, scale=D / P,
                                           bias=eps[:, 1:2]).then_inc(qk_std_done, ac.adds(qk_std_done))

            def attention(blocks, sink):
                n = len(blocks) * P
                for u in range(NB * GROUPS):
                    b, g = u // GROUPS, u % GROUPS
                    eng.wait_ge(s_max, ac.next(s_max))
                    if sink:
                        act(stats[:, 16:20], stats[:, 12:16], ACT.Exp).then_inc(sink_exp, ac.adds(sink_exp))
                    for r in range(REP):
                        ins = act(scores[:, r, 0:n], scores[:, r, 0:n], ACT.Exp, bias=stats[:, 4 + r:5 + r],
                                  accum_out=stats[:, 8 + r:9 + r])
                    ins.then_inc(s_exp, ac.adds(s_exp))
                    if u:
                        eng.wait_ge(pv_done, ac.now(pv_done))
                    for j in blocks:
                        eng.wait_ge(pt_done, ac.next(pt_done))
                        act(pt[:, j, :], (ps_c, ps_d)[j % 2][:, :], ACT.Copy).then_inc(pt_taken, ac.adds(pt_taken))
                    eng.wait_ge(pv_done, ac.next(pv_done))
                    act(o_t[:, REP * g:REP * (g + 1), b * P:(b + 1) * P],
                                           ps_b[:, (u % 2) * 512:(u % 2 + 1) * 512].rearrange("p (r t) -> p r t", t=P),
                                           ACT.Copy).then_inc(pv_taken, ac.adds(pv_taken))

            def peer_scores(src, l, who):
                ac.skip(chunk_done, WO_CHUNKS)
                eng.wait_ge(x_added, ac.next(x_added, KT))
                rms(src, l, 1, who)
                eng.wait_ge(tm_done, ac.next(tm_done))
                for j in range(4):
                    ins = act(h_tm[:, j // 2, (j % 2) * 512:(j % 2 + 1) * 512], ps_a[:, j * 512:(j + 1) * 512], ACT.Copy)
                ins.then_inc(tm_taken, ac.adds(tm_taken))
                for g in range(8):
                    eng.wait_ge(chunk_done, ac.next(chunk_done, 2))
                    act(pq_t[:, 2 * g:2 * g + 2, :],
                                           ps_b[:, (g % 2) * 512:(g % 2 + 1) * 512], ACT.Copy).then_inc(pq_taken, ac.adds(pq_taken))
                for b in range(NB):
                    eng.wait_ge(sc_done, ac.next(sc_done))
                    if b:
                        eng.wait_ge(idx_done, ac.next(idx_done))
                    for j in range(4):
                        ins = act(pscore[:, 4 * j:4 * j + 4, :], ps_a[:, j * 512:(j + 1) * 512], ACT.Copy)
                    ins.then_inc(sc_taken, ac.adds(sc_taken))
                    eng.wait_ge(top_ready, ac.next(top_ready))
                    act(top_sc[:, :, :], top_sc[:, :, :], ACT.Exp).then_inc(top_exp, ac.adds(top_exp))
                ac.skip(idx_done, 1)

            def peer_gelu():
                eng.wait_ge(dots_done, ac.next(dots_done))
                act(wts[:, :], dots[:, :], ACT.Gelu_apprx_tanh).then_inc(gelu_done, ac.adds(gelu_done))

            eng.sem_inc(h_done, AHEAD["h_done"])
            eng.sem_inc(z_done, AHEAD["z_done"])
            eng.wait_ge(vecs_in, 32)
            at = sc_["c"][0]
            act(cond[:, :], second[:, at:at + 2 * KT], ACT.Silu).then_inc(c_silu, ac.adds(c_silu))
            eng.wait_ge(lb_max, ac.next(lb_max))
            act(lbs[:, 8:16], lbs[:, 0:8], ACT.Exp).then_inc(lb_exp, ac.adds(lb_exp))
            ac.skip(chunk_done, ADA_CHUNKS)
            eng.wait_ge(ctx_in, 16)
            eng.wait_ge(eps_set, ac.next(eps_set))
            rms(ctx_t, 0, 0, 1)
            qkv(True, 0)
            attention([0, 1], False)
            peer_scores(ctx_t, 0, 1)
            ac.skip(chunk_done, ADA_CHUNKS)

            def feed_forward():
                def tile(ft):
                    eng.wait_ge(up_done, ac.next(up_done))
                    act(
                        silu[:, ft % 2, :], ps_b[:, (ft % 2) * 512:(ft % 2) * 512 + T], ACT.Silu).then_inc(silu_done, ac.adds(silu_done))
                tile(0)
                with ac.loop(FT_TURNS, up_done=FT_STEP, silu_done=FT_STEP, hidden_done=FT_STEP):
                    for q in range(FT_STEP):
                        eng.wait_ge(hidden_done, ac.now(hidden_done))
                        tile(q + 1)
                        ac.skip(hidden_done, 1)
                eng.wait_ge(hidden_done, ac.now(hidden_done))
                tile(FT - 1)
                ac.skip(hidden_done, 2)

            def layer_norm(n):
                for j in range(4):
                    eng.wait_ge(centred_done, ac.next(centred_done))
                    act(
                        sq[:, 2 * j:2 * j + 2, :], resid[:, 2 * j:2 * j + 2, :], ACT.Square).then_inc(square_done, ac.adds(square_done))
                eng.wait_ge(var_done, ac.next(var_done))
                act(std[:, :], ps_d[:, 0:T], ACT.Sqrt, bias=eps[:, 0:1]).then_inc(std_done, ac.adds(std_done))
                for k in range(KT):
                    if k % 2 == 0:
                        eng.wait_ge(scaled_done, ac.next(scaled_done))
                    act(x_t[:, k, :], resid[:, k, :], ACT.Identity, scale=vec(cur, fc, "ln_g", n * KT + k),
                                         bias=vec(cur, fc, "ln_b", n * KT + k)).then_inc(h_done, ac.adds(h_done))

            with ac.loop(L, chunk_done=MIX_CHUNKS, up_done=2 * FT, silu_done=2 * FT, hidden_done=2 * FT,
                         centred_done=16, square_done=16, var_done=4, std_done=4, scaled_done=16, h_done=4 * KT,
                         z_done=24, f_done=1, log_done=1, decay_done=8, exp_done=8, o_done=1, o_square_done=2,
                         o_ms_done=1, o_std_done=1, pool_mm_done=1, pooled_done=1, cmax_done=NB, cexp_done=NB,
                         cpt_done=2 * NB, cpt_taken=2 * NB, co_done=NB, co_taken=NB, dots_done=1, gelu_done=1,
                         layer_vecs=1, qk_done=9) as l:
                eng.wait_ge(layer_vecs, ac.next(layer_vecs))
                feed_forward()
                layer_norm(0)

                def group(g, dst, func=ACT.Copy):
                    eng.wait_ge(chunk_done, ac.next(chunk_done, 2))
                    act(dst, ps_b[:, (g % 2) * 512:(g % 2 + 1) * 512], func).then_inc(z_done, ac.adds(z_done))

                def exps(i):
                    eng.wait_ge(decay_done, ac.next(decay_done))
                    act(dec[i % 2], dec[i % 2], ACT.Exp).then_inc(exp_done, ac.adds(exp_done))

                group(0, z_f[:, 0:2, :], ACT.Sigmoid)
                group(1, z_f[:, 2:4, :], ACT.Sigmoid)
                group(2, z_q[:, 0:2, :])
                group(3, z_q[:, 2:4, :])
                eng.wait_ge(f_done, ac.next(f_done))
                act(dec[0], z_f, ACT.Ln).then_inc(log_done, ac.adds(log_done))
                for g, dst in ((4, v_tm[:, 0]), (5, v_tm[:, 1]), (6, z_h), (7, z_c), (8, z_b)):
                    group(g, dst)
                    exps(g - 3)
                group(9, pool_u[:, :, 16:])
                exps(6)
                group(10, z_g[:, 0:2, :], ACT.Sigmoid)
                exps(7)
                group(11, z_g[:, 2:4, :], ACT.Sigmoid)
                exps(8)
                eng.wait_ge(o_done, ac.next(o_done))
                eng.wait_ge(qk_done, ac.next(qk_done, 9))
                for j in range(2):
                    act(view(arena, 8704 + 512 * j, 512), ps_a[:, 1024 + 512 * j:1536 + 512 * j],
                                                ACT.Square).then_inc(o_square_done, ac.adds(o_square_done))
                eng.wait_ge(pool_mm_done, ac.next(pool_mm_done))
                for t in range(2):
                    ins = act(mix[:, 6 + t, :], ps_d[:, t * T:(t + 1) * T], ACT.Copy, scale=vec(cur, fc, "pool_scale", t))
                ins.then_inc(pooled_done, ac.adds(pooled_done))
                group(12, ca_k[:, 0:2, :])
                eng.wait_ge(o_ms_done, ac.next(o_ms_done))
                act(view(arena, 9728, 1024), ps_a[:, 0:1024], ACT.Sqrt, scale=D / P,
                                          bias=eps[:, 1:2]).then_inc(o_std_done, ac.adds(o_std_done))
                peer_gelu()
                for g in range(13, 16):
                    group(g, ca_k[:, 2 * g - 24:2 * g - 22, :])
                for g in range(16, 20):
                    group(g, ca_v[:, g - 16])
                ac.skip(chunk_done, KT)
                layer_norm(1)
                for g in range(20, 24):
                    group(g, ca_q[:, 2 * g - 40:2 * g - 38, :])
                for b in range(NB):
                    eng.wait_ge(cmax_done, ac.next(cmax_done))
                    for h in range(CA_H):
                        ins = act(ca_e[b][:, h, :], ps_a[:, b * 1024 + h * T:b * 1024 + (h + 1) * T], ACT.Exp,
                                  scale=CA_SCALE, bias=stats[:, 24 + 4 * b + h:25 + 4 * b + h],
                                  accum_out=stats[:, 32 + 4 * b + h:33 + 4 * b + h])
                    ins.then_inc(cexp_done, ac.adds(cexp_done))
                for b in range(NB):
                    if b:
                        eng.wait_ge(co_done, ac.now(co_done))
                    for m in range(NB):
                        eng.wait_ge(cpt_done, ac.next(cpt_done))
                        act(ca_pt[:, m, :, :], (ps_c, ps_d)[m][:, :], ACT.Copy).then_inc(cpt_taken, ac.adds(cpt_taken))
                    eng.wait_ge(co_done, ac.next(co_done))
                    for j in range(2):
                        ins = act(ca_o[:, 4 * j:4 * j + 4, b * P:(b + 1) * P],
                                  ps_b[:, j * 512:(j + 1) * 512].rearrange("p (k t) -> p k t", t=P), ACT.Copy)
                    ins.then_inc(co_taken, ac.adds(co_taken))
                ac.skip(chunk_done, KT)
                layer_norm(2)
                feed_forward()
                layer_norm(3)

            for l in range(L):
                eng.wait_ge(x_final, ac.next(x_final))
                eng.wait_ge(h_done, ac.now(h_done))
                rms(x_t, l, 0, 0)
                qkv(True, 2)
                attention([0, 1, 2, 3], l == 1)
                peer_scores(x_t, l, 0)
                if l == 0:
                    rms(ctx_t, 1, 0, 1)
                    qkv(False, 0)
                for b in range(NB):
                    peer_gelu()

        @block.vector
        def _(eng):
            ve = Lane(eng, ("down_done",))
            V = nc.vector
            phase = [0]

            def bcast(ap, *shape):
                return ap.to_broadcast([P, *shape])

            def modulation(l):
                eng.wait_ge(chunk_done, ve.next(chunk_done, ADA_CHUNKS))
                at = sc_["ada_b"][0] + 48 * l
                V.tensor_tensor(mods[:, l], ps_d[:, 0:96].rearrange("p (j w) -> p j w", w=2),
                                     bcast(second[:, at:at + 48].unsqueeze(2), 48, 2), ALU.add).then_inc(dve_step, ve.adds(dve_step))
                eng.wait_ge(dve_step, ve.now(dve_step))
                for part in range(2):
                    at = sc_[("gain1", "gain2")[part]][0] + 8 * l
                    ins = V.scalar_tensor_tensor(gains[:, l, part], mods[:, l, 24 * part + 8:24 * part + 16, :], 1.0,
                                                 bcast(second[:, at:at + 8].unsqueeze(2), 8, 2), ALU.add, ALU.mult)
                    if part == 0:
                        ins.then_inc(dve_step, ve.adds(dve_step))
                eng.wait_ge(dve_step, ve.now(dve_step))
                ins.then_inc(mods_done, ve.adds(mods_done))

            def rms(src):
                eng.wait_ge(std2_done, ve.next(std2_done))
                V.reciprocal(std[:, :], std[:, :]).then_inc(dve_step, ve.adds(dve_step))
                eng.wait_ge(dve_step, ve.now(dve_step))
                for j in range(4):
                    V.tensor_tensor(h2[:, 2 * j:2 * j + 2, :], src[:, 2 * j:2 * j + 2, :],
                                                         bcast(std[:, :].unsqueeze(1), 2, T), ALU.mult).then_inc(norm2_done, ve.adds(norm2_done))

            def qk_norm(l, first_tile, rope, key_at):
                n = 10 - first_tile
                eng.wait_ge(qk_std_done, ve.next(qk_std_done))
                eng.wait_ge(qkv_taken, ve.next(qkv_taken, 6 if n == 10 else 2))
                V.reciprocal(qk_r[:, first_tile:10, :], qk_r[:, first_tile:10, :]).then_inc(dve_step, ve.adds(dve_step))
                eng.wait_ge(dve_step, ve.now(dve_step))
                gq, gk = (second[:, sc_[g][0] + l:sc_[g][0] + l + 1] for g in ("q_gain", "k_gain"))
                k_out = qk_n[:, 8:10, :] if rope else keys_t[:, :, key_at:key_at + T]
                last = V.scalar_tensor_tensor(k_out, qk_raw[:, 8:10, :], gk, qk_r[:, 8:10, :], ALU.mult, ALU.mult)
                if n == 10:
                    last.then_inc(dve_step, ve.adds(dve_step))
                    last = V.scalar_tensor_tensor(qk_n[:, 0:8, :], qk_raw[:, 0:8, :], gq, qk_r[:, 0:8, :], ALU.mult,
                                                  ALU.mult)
                if not rope:
                    eng.wait_ge(dve_step, ve.now(dve_step))
                    last.then_inc(roped, ve.adds(roped))
                    return
                last.then_inc(qk_normed, ve.adds(qk_normed))
                eng.wait_ge(dve_step, ve.now(dve_step))
                eng.wait_ge(qk_normed, ve.now(qk_normed))
                V.tensor_tensor(
                    qk_raw, qk_n, bcast(cos.unsqueeze(1), 10, T), ALU.mult).then_inc(dve_step, ve.adds(dve_step))
                eng.wait_ge(rot_done, ve.next(rot_done))
                V.tensor_tensor(
                    qk_r[:, 0:8, :], view(ps_a, 0, 8, T), bcast(sin.unsqueeze(1), 8, T), ALU.mult).then_inc(dve_step, ve.adds(dve_step))
                V.tensor_tensor(
                    qk_r[:, 8:10, :], view(ps_d, 0, 2, T), bcast(sin.unsqueeze(1), 2, T), ALU.mult).then_inc(dve_step, ve.adds(dve_step))
                eng.wait_ge(dve_step, ve.now(dve_step))
                V.tensor_tensor(
                    keys_t[:, :, key_at:key_at + T], qk_raw[:, 8:10, :], qk_r[:, 8:10, :], ALU.add).then_inc(dve_step, ve.adds(dve_step))
                eng.wait_ge(dve_step, ve.now(dve_step))
                V.tensor_tensor(
                    qk_n[:, 0:8, :], qk_raw[:, 0:8, :], qk_r[:, 0:8, :], ALU.add).then_inc(roped, ve.adds(roped))

            def attention(blocks, windowed):
                n = len(blocks) * P
                for u in range(NB * GROUPS):
                    b, g = u // GROUPS, u % GROUPS
                    if u:
                        eng.wait_ge(pt_done, ve.next(pt_done, len(blocks)))
                    eng.wait_ge(s_done, ve.next(s_done))
                    ps = ps_a[:, :].rearrange("p (r k) -> p r k", r=REP)
                    if windowed:
                        V.scalar_tensor_tensor(scores[:, :, T:2 * T], ps[:, :, T:2 * T], SCALE,
                                                    bcast(window[:, b, :].unsqueeze(1), REP, T), ALU.mult, ALU.add).then_inc(dve_step, ve.adds(dve_step))
                    k = T if windowed else n
                    V.tensor_scalar(
                        scores[:, :, 0:k], ps[:, :, 0:k], SCALE, None, ALU.mult).then_inc(s_taken, ve.adds(s_taken))
                    eng.wait_ge(dve_step, ve.now(dve_step))
                    eng.wait_ge(s_taken, ve.now(s_taken))
                    V.tensor_reduce(stats[:, 0:4], scores[:, :, 0:n], AX, ALU.max).then_inc(dve_step, ve.adds(dve_step))
                    eng.wait_ge(dve_step, ve.now(dve_step))
                    if windowed:
                        sink = second[:, sc_["sinks"][0] + REP * g:sc_["sinks"][0] + REP * (g + 1)]
                        V.tensor_tensor(
                            stats[:, 0:4], stats[:, 0:4], sink, ALU.max).then_inc(dve_step, ve.adds(dve_step))
                        eng.wait_ge(dve_step, ve.now(dve_step))
                        V.tensor_tensor(
                            stats[:, 12:16], sink, stats[:, 0:4], ALU.subtract).then_inc(dve_step, ve.adds(dve_step))
                        eng.wait_ge(dve_step, ve.now(dve_step))
                    V.tensor_scalar(stats[:, 4:8], stats[:, 0:4], -1.0, None, ALU.mult).then_inc(s_max, ve.adds(s_max))
                    if windowed:
                        eng.wait_ge(sink_exp, ve.next(sink_exp))
                    eng.wait_ge(s_exp, ve.next(s_exp))
                    if windowed:
                        V.tensor_tensor(
                            stats[:, 8:12], stats[:, 8:12], stats[:, 16:20], ALU.add).then_inc(dve_step, ve.adds(dve_step))
                        eng.wait_ge(dve_step, ve.now(dve_step))
                    V.reciprocal(stats[:, 20:24], stats[:, 8:12]).then_inc(dve_step, ve.adds(dve_step))
                    eng.wait_ge(dve_step, ve.now(dve_step))
                    V.tensor_tensor(scores[:, :, 0:n], scores[:, :, 0:n],
                                                     bcast(stats[:, 20:24].unsqueeze(2), REP, n), ALU.mult).then_inc(s_prob, ve.adds(s_prob))
                ve.skip(pt_done, len(blocks))

            def gated_add(x, ps, l, part, who, sig):
                for k in range(KT):
                    ins = V.scalar_tensor_tensor(x[:, k, :], ps[:, k, :], mods[:, l, 24 * part + 16 + k, who:who + 1],
                                                 x[:, k, :], ALU.mult, ALU.add)
                    if sig is x_added:
                        ins.then_inc(sig, ve.adds(sig))
                    elif k < KT - 1:
                        ins.then_inc(dve_step, ve.adds(dve_step))
                    else:
                        eng.wait_ge(dve_step, ve.now(dve_step))
                        ins.then_inc(sig, ve.adds(sig))

            def top_experts(l, b):
                J, H = range(2 * PEER_H), range(PEER_H)
                eng.wait_ge(sc_taken, ve.next(sc_taken))

                def best(values, left, top, at, js):
                    for j in js:
                        V.max(top[:, j, 0:8], values[:, j, :]).then_inc(dve_step, ve.adds(dve_step))
                    eng.wait_ge(dve_step, ve.now(dve_step))
                    for j in js:
                        V.max_index(
                            at[:, j, 0:8], top[:, j, 0:8], values[:, j, :]).then_inc(dve_step, ve.adds(dve_step))
                    for j in js:
                        V.match_replace(
                            left[:, j, :], top[:, j, 0:8], values[:, j, :], LOWEST).then_inc(dve_step, ve.adds(dve_step))
                    eng.wait_ge(dve_step, ve.now(dve_step))
                    for j in js:
                        V.max(top[:, j, 8:16], left[:, j, :]).then_inc(dve_step, ve.adds(dve_step))
                    eng.wait_ge(dve_step, ve.now(dve_step))
                    for j in js:
                        V.max_index(
                            at[:, j, 8:16], top[:, j, 8:16], left[:, j, :]).then_inc(dve_step, ve.adds(dve_step))
                    eng.wait_ge(dve_step, ve.now(dve_step))

                best(pscore, pscore2, top_v, top_iu, J)
                V.tensor_copy(top_i, top_iu).then_inc(dve_step, ve.adds(dve_step))
                halves = top_v.rearrange("p (h c) a -> p h c a", c=2)
                V.tensor_tensor(cand, bcast(halves[:, :, 0, :].unsqueeze(3), PEER_H, TOPK, TOPK),
                                     bcast(halves[:, :, 1, :].unsqueeze(2), PEER_H, TOPK, TOPK), ALU.add).then_inc(dve_step, ve.adds(dve_step))
                eng.wait_ge(dve_step, ve.now(dve_step))
                pos = pos_u[:, 0:SLOTS]
                best(cand.rearrange("p h a b -> p h (a b)"), cand2, top_sc, pos.rearrange("p (h k) -> p h k", k=TOPK), H)
                gate = gates[:, b, :].rearrange("p (h k) -> p h k", k=TOPK)
                V.tensor_copy(stats[:, 0:8], top_sc[:, :, 0]).then_inc(dve_step, ve.adds(dve_step))
                eng.wait_ge(dve_step, ve.now(dve_step))
                V.tensor_tensor(top_sc, top_sc, bcast(stats[:, 0:8].unsqueeze(2), PEER_H, TOPK),
                                                    ALU.subtract).then_inc(top_ready, ve.adds(top_ready))
                V.tensor_scalar(
                    pos_u[:, SLOTS:2 * SLOTS], pos, 4, None, ALU.logical_shift_right).then_inc(dve_step, ve.adds(dve_step))
                V.tensor_scalar(
                    pos_u[:, 2 * SLOTS:], pos, 15, None, ALU.bitwise_and).then_inc(dve_step, ve.adds(dve_step))
                eng.wait_ge(dve_step, ve.now(dve_step))
                for c in range(2):
                    V.tensor_copy(
                        sel[c], pos_u[:, (1 + c) * SLOTS:(2 + c) * SLOTS]).then_inc(dve_step, ve.adds(dve_step))
                eng.wait_ge(dve_step, ve.now(dve_step))
                ids = top_i.rearrange("p (h c) a -> p h c a", c=2)
                flat = [o.rearrange("p h k a -> p (h k) a") for o in onehot]
                for c in range(2):
                    V.tensor_tensor(flat[c], bcast(sel[c].unsqueeze(2), SLOTS, TOPK),
                                         bcast(iota.unsqueeze(1), SLOTS, TOPK), ALU.is_equal).then_inc(dve_step, ve.adds(dve_step))
                eng.wait_ge(dve_step, ve.now(dve_step))
                for c in range(2):
                    V.tensor_tensor(onehot[c], onehot[c], bcast(ids[:, :, c, :].unsqueeze(2), PEER_H, TOPK, TOPK),
                                         ALU.mult).then_inc(dve_step, ve.adds(dve_step))
                eng.wait_ge(dve_step, ve.now(dve_step))
                for c in range(2):
                    V.tensor_reduce(sel[2 + c], flat[c], AX, ALU.add).then_inc(dve_step, ve.adds(dve_step))
                eng.wait_ge(dve_step, ve.now(dve_step))
                V.tensor_scalar(
                    sel[4], sel[2], float(N_KEYS), float(l * N_EXPERTS), ALU.mult, ALU.add).then_inc(dve_step, ve.adds(dve_step))
                eng.wait_ge(dve_step, ve.now(dve_step))
                V.tensor_tensor(sel[5], sel[4], sel[3], ALU.add).then_inc(dve_step, ve.adds(dve_step))
                eng.wait_ge(dve_step, ve.now(dve_step))
                V.tensor_copy(idx[:, b, :], sel[5]).then_inc(dve_step, ve.adds(dve_step))
                eng.wait_ge(top_exp, ve.next(top_exp))
                V.tensor_reduce(stats[:, 8:16], top_sc, AX, ALU.add).then_inc(dve_step, ve.adds(dve_step))
                eng.wait_ge(dve_step, ve.now(dve_step))
                V.reciprocal(stats[:, 16:24], stats[:, 8:16]).then_inc(dve_step, ve.adds(dve_step))
                eng.wait_ge(dve_step, ve.now(dve_step))
                V.tensor_tensor(gate, top_sc, bcast(stats[:, 16:24].unsqueeze(2), PEER_H, TOPK),
                                                   ALU.mult).then_inc(idx_done, ve.adds(idx_done))

            def dot_slot(s, h, out):
                eng.wait_ge(rows_in[s], ve.next(rows_in[s], 16))
                eng.wait_ge(row_used, ve.now(row_used, 1))
                V.scalar_tensor_tensor(
                    acc2[s % 2], rows[:, s, :], 1.0, h, ALU.mult, ALU.mult, accum_out=out).then_inc(row_used, ve.adds(row_used))

            def sum_slot(s, w, first=False):
                eng.wait_ge(rows_in[s], ve.next(rows_in[s], 16))
                if first:
                    ins = V.tensor_scalar(acc2[s % 2], rows[:, s, :], w, None, ALU.mult)
                else:
                    eng.wait_ge(row_used, ve.now(row_used, 1))
                    ins = V.scalar_tensor_tensor(acc2[s % 2], rows[:, s, :], w, acc2[s % 2], ALU.mult, ALU.add)
                ins.then_inc(row_used, ve.adds(row_used))

            def head_slots(summing, h):
                for s in range(HEAD_SLOTS):
                    if summing:
                        sum_slot(s, wts[:, s:s + 1], s < 2)
                    else:
                        dot_slot(s, h, dots[:, s:s + 1])

            def turn_begin(summing, i):
                eng.wait_ge(dve_step, ve.now(dve_step))
                if summing:
                    eng.wait_ge(row_used, ve.now(row_used))
                    V.tensor_copy(
                        stage[:, :], wts[:, bass.ds(i * TURN_SLOTS + HEAD_SLOTS, TURN_SLOTS)]).then_inc(dve_step, ve.adds(dve_step))
                    eng.wait_ge(dve_step, ve.now(dve_step))

            def turn_slots(summing, h, at, n):
                for q in range(at, at + n):
                    if summing:
                        sum_slot(q % GR, stage[:, q:q + 1])
                    else:
                        dot_slot(q % GR, h, stage[:, q:q + 1])

            def turn_end(summing, i):
                if not summing:
                    eng.wait_ge(row_used, ve.now(row_used))
                    V.tensor_copy(
                        dots[:, bass.ds(i * TURN_SLOTS + HEAD_SLOTS, TURN_SLOTS)], stage[:, :]).then_inc(dve_step, ve.adds(dve_step))

            def phase_end(summing, out):
                eng.wait_ge(row_used, ve.now(row_used))
                if summing:
                    V.tensor_tensor(out, acc2[0], acc2[1], ALU.add).then_inc(pout_done, ve.adds(pout_done))
                    eng.wait_ge(pout_done, ve.now(pout_done))
                else:
                    eng.wait_ge(dve_step, ve.now(dve_step))
                    V.tensor_copy(dots[:, 0:1], dots[:, 0:1]).then_inc(dots_done, ve.adds(dots_done))

            def weigh(gate):
                eng.wait_ge(gelu_done, ve.next(gelu_done))
                V.tensor_tensor(wts[:, :], wts[:, :], gate, ALU.mult).then_inc(dve_step, ve.adds(dve_step))
                eng.wait_ge(dve_step, ve.now(dve_step))

            per_turn = dict(row_used=TURN_SLOTS, dve_step=1, **{f"rows_{s}": 16 * TURN_SLOTS // GR for s in range(GR)})

            def peer(b):
                for summing in (False, True):
                    head_slots(summing, h_tm[:, b, :])
                    with ve.loop(FT_TURNS, **per_turn) as i:
                        turn_begin(summing, i)
                        turn_slots(summing, h_tm[:, b, :], 0, TURN_SLOTS)
                        turn_end(summing, i)
                    phase_end(summing, h_tm[:, b, :])
                    if not summing:
                        weigh(gates[:, b, :])

            V.memset(zeros[:, :], 0.0).then_inc(zeros_set, ve.adds(zeros_set))
            V.memset(eps[:, 0:1], LN_EPS).then_inc(dve_step, ve.adds(dve_step))
            eng.wait_ge(dve_step, ve.now(dve_step))
            V.memset(eps[:, 1:2], RMS_EPS).then_inc(eps_set, ve.adds(eps_set))
            eng.sem_inc(row_used, AHEAD["row_used"])
            eng.sem_inc(hidden_done, AHEAD["hidden_done"])
            eng.wait_ge(vecs_in, 32)
            eng.wait_ge(consts_in, 16)
            raw = [vec(first, fc, "lb", l * n_first, 4) for l in range(L)]
            V.tensor_tensor(lbs[:, 24:28], raw[0], raw[1], ALU.max).then_inc(dve_step, ve.adds(dve_step))
            eng.wait_ge(dve_step, ve.now(dve_step))
            V.tensor_tensor(lbs[:, 0:4], raw[0], lbs[:, 24:28], ALU.subtract).then_inc(dve_step, ve.adds(dve_step))
            eng.wait_ge(dve_step, ve.now(dve_step))
            V.tensor_tensor(lbs[:, 4:8], raw[1], lbs[:, 24:28], ALU.subtract).then_inc(lb_max, ve.adds(lb_max))
            eng.wait_ge(lb_exp, ve.next(lb_exp))
            V.tensor_tensor(lbs[:, 16:20], lbs[:, 8:12], lbs[:, 12:16], ALU.add).then_inc(dve_step, ve.adds(dve_step))
            eng.wait_ge(dve_step, ve.now(dve_step))
            V.reciprocal(lbs[:, 20:24], lbs[:, 16:20]).then_inc(dve_step, ve.adds(dve_step))
            eng.wait_ge(dve_step, ve.now(dve_step))
            for l in range(L):
                V.tensor_tensor(
                    lbs[:, 4 * l:4 * l + 4], lbs[:, 8 + 4 * l:12 + 4 * l], lbs[:, 20:24], ALU.mult).then_inc(dve_step, ve.adds(dve_step))
            eng.wait_ge(dve_step, ve.now(dve_step))
            V.tensor_tensor(lbs[:, 8:12], lbs[:, 0:4], lbs[:, 4:8], ALU.add).then_inc(dve_step, ve.adds(dve_step))
            eng.wait_ge(dve_step, ve.now(dve_step))
            for l, upto in enumerate((lbs[:, 0:4], lbs[:, 8:12])):
                V.tensor_tensor(raw[l], upto, lbs[:, 0:4], ALU.subtract).then_inc(dve_step, ve.adds(dve_step))
            eng.wait_ge(dve_step, ve.now(dve_step))
            for l in range(L):
                V.tensor_scalar(
                    vec(first, fc, "omlb", l * n_first, 4), raw[l], -1.0, 1.0, ALU.mult, ALU.add).then_inc(dve_step, ve.adds(dve_step))
            eng.wait_ge(dve_step, ve.now(dve_step))

            modulation(0)
            rms(ctx_t)
            ve.skip(chunk_done, QKV_CHUNKS)
            qk_norm(0, 0, False, 0)
            attention([0, 1], False)

            def project_out(x, l, who):
                for j in range(4):
                    eng.wait_ge(chunk_done, ve.next(chunk_done, 2))
                gated_add(x, acc_t, l, 0, who, x_added)

            project_out(ctx_t, 0, 1)
            eng.wait_ge(x_added, ve.now(x_added))
            rms(ctx_t)
            ve.skip(chunk_done, PQ_CHUNKS)
            for b in range(NB):
                top_experts(0, b)
            modulation(1)

            eng.wait_ge(dve_step, ve.now(dve_step))
            eng.wait_ge(idx_done, ve.now(idx_done))
            V.memset(attn, 0.0).then_inc(dve_step, ve.adds(dve_step))
            V.memset(conv_u[:, :, 0:2], 0.0).then_inc(dve_step, ve.adds(dve_step))
            V.memset(pool_u[:, :, 0:16], 0.0).then_inc(dve_step, ve.adds(dve_step))
            for s in pool_s:
                V.memset(s, 0.0).then_inc(dve_step, ve.adds(dve_step))
            eng.wait_ge(masks_in, 16)
            eng.wait_ge(x_in, 16)
            eng.wait_ge(dve_step, ve.now(dve_step))

            def feed_forward(l, summing):
                h = h_tm[:, bass.ds(l, 1), :].rearrange("p a d -> p (a d)")

                def tile(ft):
                    eng.wait_ge(up_done, ve.next(up_done))
                    eng.wait_ge(silu_done, ve.next(silu_done))
                    eng.wait_ge(down_done, ve.next(down_done))
                    V.scalar_tensor_tensor(
                        hidden[:, ft % 2, :], ps_b[:, (ft % 2) * 512 + T:(ft % 2 + 1) * 512], 0.5, silu[:, ft % 2, :],
                        ALU.mult, ALU.mult).then_inc(hidden_done, ve.adds(hidden_done))

                tile(0)
                head_slots(summing, h)
                with ve.loop(FT_TURNS, up_done=FT_STEP, silu_done=FT_STEP, down_done=FT_STEP, hidden_done=FT_STEP,
                             **per_turn) as i:
                    turn_begin(summing, i)
                    for q in range(FT_STEP):
                        tile(q + 1)
                        turn_slots(summing, h, q * FT_SLOTS, FT_SLOTS)
                    turn_end(summing, i)
                tile(FT - 1)
                phase_end(summing, h)
                eng.wait_ge(down_done, ve.now(down_done, -2))

            def layer_norm(wait=0):
                for j in range(4):
                    if wait == 2 or (wait and j == 0):
                        eng.wait_ge(chunk_done, ve.next(chunk_done, wait))
                    V.scalar_tensor_tensor(
                        resid[:, 2 * j:2 * j + 2, :], x_t[:, 2 * j:2 * j + 2, :], ALPHA, acc_t[:, 2 * j:2 * j + 2, :],
                        ALU.mult, ALU.add).then_inc(resid_done, ve.adds(resid_done))
                eng.wait_ge(mean_done, ve.next(mean_done))
                eng.wait_ge(resid_done, ve.now(resid_done))
                for j in range(4):
                    V.tensor_tensor(
                        resid[:, 2 * j:2 * j + 2, :], resid[:, 2 * j:2 * j + 2, :],
                        bcast(ps_c[:, 0:T].unsqueeze(1), 2, T), ALU.subtract).then_inc(centred_done, ve.adds(centred_done))
                eng.wait_ge(std_done, ve.next(std_done))
                V.reciprocal(std[:, :], std[:, :]).then_inc(dve_step, ve.adds(dve_step))
                eng.wait_ge(dve_step, ve.now(dve_step))
                eng.wait_ge(centred_done, ve.now(centred_done))
                for j in range(4):
                    V.tensor_tensor(
                        resid[:, 2 * j:2 * j + 2, :], resid[:, 2 * j:2 * j + 2, :],
                        bcast(std[:, :].unsqueeze(1), 2, T), ALU.mult).then_inc(scaled_done, ve.adds(scaled_done))

            all_slots = {f"rows_{s}": 32 * SLOTS // GR for s in range(GR)}
            with ve.loop(L, chunk_done=MIX_CHUNKS, up_done=2 * FT, silu_done=2 * FT, down_done=2 * FT, hidden_done=2 * FT,
                         resid_done=16, mean_done=4, centred_done=16, std_done=4, scaled_done=16, h_done=4 * KT,
                         z_done=24, f_done=1, log_done=1, decay_done=8, exp_done=8, qk_done=9, level_done=9,
                         level_taken=9, o_std_done=1, conv_done=1, rec_done=1, cs_done=NB, cmax_done=NB, cexp_done=NB,
                         cprob_done=NB, row_used=2 * SLOTS, pout_done=1, dots_done=1, gelu_done=1, layer_vecs=1,
                         dve_step=DVE_STEPS, **all_slots) as l:
                eng.wait_ge(h_done, ve.now(h_done))
                V.tensor_copy(
                    cur[:, :], first[:, bass.ds(l * n_first, n_first)]).then_inc(layer_vecs, ve.adds(layer_vecs))
                feed_forward(l, False)
                layer_norm()

                eng.wait_ge(z_done, ve.next(z_done, 2))
                eng.wait_ge(layer_vecs, ve.now(layer_vecs))
                for h in range(REC_H):
                    ins = V.tensor_scalar(z_f[:, h, :], z_f[:, h, :], vec(cur, fc, "omlb", h), vec(cur, fc, "lb", h),
                                          ALU.mult, ALU.add)
                    if h < REC_H - 1:
                        ins.then_inc(dve_step, ve.adds(dve_step))
                eng.wait_ge(dve_step, ve.now(dve_step))
                ins.then_inc(f_done, ve.adds(f_done))
                eng.wait_ge(log_done, ve.next(log_done))
                V.tensor_scalar(z_f, z_f, -1.0, 1.0, ALU.mult, ALU.add).then_inc(dve_step, ve.adds(dve_step))
                for h in range(REC_H):
                    V.tensor_tensor_scan(
                        csum[:, h, :], restart, dec[0][:, h, :], 0.0, ALU.mult, ALU.add).then_inc(dve_step, ve.adds(dve_step))
                eng.wait_ge(dve_step, ve.now(dve_step))

                def decays(i):
                    if i == 8:
                        d = dec[0].rearrange("p h (c s) -> p h c s", s=CHUNK)
                        b = csum.rearrange("p h (c s) -> p h c s", s=CHUNK)
                        end = [b[:, :, c, CHUNK - 1:CHUNK] for c in range(4)]
                        both = stats[:, 40:44].unsqueeze(2)
                        V.tensor_tensor(both, end[0], end[1], ALU.add).then_inc(dve_step, ve.adds(dve_step))
                        eng.wait_ge(dve_step, ve.now(dve_step))
                        full = (REC_H, CHUNK)
                        V.tensor_tensor(
                            d[:, :, 0, :], bcast(both, *full), b[:, :, 0, :], ALU.subtract).then_inc(dve_step, ve.adds(dve_step))
                        V.tensor_tensor(
                            d[:, :, 1, :], bcast(end[1], *full), b[:, :, 1, :], ALU.subtract).then_inc(dve_step, ve.adds(dve_step))
                        V.tensor_copy(d[:, :, 2, :], b[:, :, 2, :]).then_inc(dve_step, ve.adds(dve_step))
                        last = V.tensor_tensor(d[:, :, 3, :], b[:, :, 3, :], bcast(end[2], *full), ALU.add)
                    else:
                        m = 1 << (i - 1)
                        n = REC_H * T // (2 * m)
                        d = dec[i % 2].rearrange("p h t -> p (h t)").rearrange("p (n c s) -> p n c s", c=2, s=m)
                        b = csum.rearrange("p h t -> p (h t)").rearrange("p (n c s) -> p n c s", c=2, s=m)
                        mid = bcast(b[:, :, 0, m - 1:m], n, m)
                        V.tensor_tensor(
                            d[:, :, 0, :], mid, b[:, :, 0, :], ALU.subtract).then_inc(dve_step, ve.adds(dve_step))
                        if m == CHUNK:
                            last = V.tensor_copy(d[:, :, 1, :], b[:, :, 1, :])
                        else:
                            last = V.tensor_tensor(d[:, :, 1, :], b[:, :, 1, :], mid, ALU.subtract)
                    eng.wait_ge(dve_step, ve.now(dve_step))
                    last.then_inc(decay_done, ve.adds(decay_done))

                def take_level(i):
                    eng.wait_ge(level_done, ve.next(level_done))
                    eng.sem_inc(dve_pause, 1)
                    for b in range(NB if i < 8 else 1):
                        ps = view(ps_a, (i % 2) * 1024 + b * 512, REC_H, P)
                        if i == 8:
                            last = V.tensor_copy(attn[:, 2], ps)
                        else:
                            last = V.copy_predicated(attn[:, b], bcast(masks[:, i, :].unsqueeze(1), REC_H, P), ps)
                            if b == 0:
                                last.then_inc(dve_step, ve.adds(dve_step))
                    eng.wait_ge(dve_step, ve.now(dve_step))
                    last.then_inc(level_taken, ve.adds(level_taken))

                decays(1)
                eng.wait_ge(z_done, ve.next(z_done, 2))
                eng.wait_ge(dve_step, ve.now(dve_step))
                V.memset(
                    stats[:, 44:45], 0.0).then_inc(qk_done, ve.adds(qk_done))
                decays(2)
                for i in range(1, 9):
                    eng.wait_ge(exp_done, ve.next(exp_done))
                    if i >= 2:
                        take_level(i - 2)
                    V.tensor_tensor(qk[i % 2][0], z_q, dec[i % 2], ALU.mult).then_inc(dve_step, ve.adds(dve_step))
                    ins = V.tensor_tensor(qk[i % 2][1], z_f, dec[i % 2], ALU.mult)
                    eng.wait_ge(dve_step, ve.now(dve_step))
                    ins.then_inc(qk_done, ve.adds(qk_done))
                    if i + 2 <= 8:
                        eng.wait_ge(qk_done, ve.now(qk_done))
                        decays(i + 2)
                take_level(7)
                take_level(8)
                eng.wait_ge(z_done, ve.next(z_done, 5))
                V.tensor_tensor(conv_u[:, :, 2:], z_c, z_h, ALU.mult).then_inc(dve_step, ve.adds(dve_step))
                eng.wait_ge(dve_step, ve.now(dve_step))
                for t in range(2):
                    V.tensor_scalar(
                        mix[:, t, :], conv_u[:, t, 0:T], vec(cur, fc, "conv_w", 3 * t), None, ALU.mult).then_inc(dve_step, ve.adds(dve_step))
                for j in range(1, 3):
                    eng.wait_ge(dve_step, ve.now(dve_step))
                    for t in range(2):
                        V.scalar_tensor_tensor(mix[:, t, :], conv_u[:, t, j:j + T], vec(cur, fc, "conv_w", 3 * t + j),
                                                    mix[:, t, :], ALU.mult, ALU.add).then_inc(dve_step, ve.adds(dve_step))
                eng.wait_ge(dve_step, ve.now(dve_step))
                V.tensor_tensor(mix[:, 0:2, :], mix[:, 0:2, :], z_b, ALU.mult).then_inc(conv_done, ve.adds(conv_done))
                eng.wait_ge(z_done, ve.next(z_done, 3))
                eng.wait_ge(o_std_done, ve.next(o_std_done))
                r = dec[1]
                V.reciprocal(r, r).then_inc(dve_step, ve.adds(dve_step))
                eng.wait_ge(dve_step, ve.now(dve_step))
                V.tensor_tensor(dec[0], view(ps_a, 1024, REC_H, T), r, ALU.mult).then_inc(dve_step, ve.adds(dve_step))
                eng.wait_ge(dve_step, ve.now(dve_step))
                for h in range(REC_H):
                    ins = V.scalar_tensor_tensor(mix[:, 2 + h, :], dec[0][:, h, :], vec(cur, fc, "norm_g", h), z_g[:, h, :],
                                                 ALU.mult, ALU.mult)
                    if h < REC_H - 1:
                        ins.then_inc(dve_step, ve.adds(dve_step))
                eng.wait_ge(dve_step, ve.now(dve_step))
                ins.then_inc(rec_done, ve.adds(rec_done))
                weigh(gates[:, bass.ds(l, 1), :].rearrange("p a s -> p (a s)"))
                ve.skip(z_done, 12)
                ve.skip(chunk_done, 40)
                layer_norm(KT)
                ve.skip(chunk_done, KT)
                for b in range(NB):
                    eng.wait_ge(cs_done, ve.next(cs_done))
                    mx, neg = stats[:, 48 + 4 * b:52 + 4 * b], stats[:, 24 + 4 * b:28 + 4 * b]
                    V.tensor_reduce(
                        mx, view(ps_a, b * 1024, CA_H, T), AX, ALU.max).then_inc(dve_step, ve.adds(dve_step))
                    eng.wait_ge(dve_step, ve.now(dve_step))
                    V.tensor_scalar(neg, mx, -CA_SCALE, None, ALU.mult).then_inc(cmax_done, ve.adds(cmax_done))
                for b in range(NB):
                    eng.wait_ge(cexp_done, ve.next(cexp_done))
                    rs = stats[:, 32 + 4 * b:36 + 4 * b]
                    V.reciprocal(stats[:, 48 + 4 * b:52 + 4 * b], rs).then_inc(dve_step, ve.adds(dve_step))
                    eng.wait_ge(dve_step, ve.now(dve_step))
                    V.tensor_tensor(
                        ca_e[b], ca_e[b], bcast(stats[:, 48 + 4 * b:52 + 4 * b].unsqueeze(2), CA_H, T), ALU.mult).then_inc(cprob_done, ve.adds(cprob_done))
                layer_norm(2)
                feed_forward(l, True)
                layer_norm()
                ve.skip(h_done, 4 * KT)

            eng.wait_ge(po_tm_done, ve.next(po_tm_done))
            gated_add(ctx_t, acc_t, 0, 1, 1, x_final)
            eng.wait_ge(h_done, ve.now(h_done))
            for l in range(L):
                if l == 1:
                    eng.wait_ge(window_in, 16)
                rms(x_t)
                ve.skip(chunk_done, QKV_CHUNKS)
                qk_norm(l, 0, True, T)
                attention([0, 1, 2, 3], l == 1)
                project_out(x_t, l, 0)
                eng.wait_ge(x_added, ve.now(x_added))
                rms(x_t)
                ve.skip(chunk_done, PQ_CHUNKS)
                for b in range(NB):
                    top_experts(l, b)
                if l == 0:
                    rms(ctx_t)
                    ve.skip(chunk_done, 4)
                    qk_norm(1, 8, False, 0)
                    eng.wait_ge(roped, ve.now(roped))
                eng.wait_ge(dve_step, ve.now(dve_step))
                eng.wait_ge(idx_done, ve.now(idx_done))
                for b in range(NB):
                    peer(b)
                eng.wait_ge(po_tm_done, ve.next(po_tm_done))
                gated_add(x_t, acc_t, l, 1, 0, x_final)
                eng.wait_ge(x_final, ve.now(x_final))


DVE_STEPS = 66


def shape_constants():
    t = np.arange(T)
    c = {"ident": np.eye(P), "mean_d": np.full((P, P), 1.0 / D)}
    rot = np.zeros((P, P))
    for d in range(P):
        if d // 32 % 2 == 0:
            rot[d + 32, d] = -1.0
        else:
            rot[d - 32, d] = 1.0
    c["rot"] = rot
    half = P // 2
    inv = np.float32(10000.0) ** (-np.arange(0, half, 2, dtype=np.float32) / np.float32(half))
    place = np.stack([t // 64, t % 64]).astype(np.float32)
    d = np.arange(P)
    angle = place[d // 64] * inv[d % 32][:, None].astype(np.float32)
    c["cos"], c["sin"] = np.cos(angle), np.sin(angle)
    count = np.stack([np.minimum(t + 1, w) for w in (2, 4, 8, 16)]).astype(np.float32)
    c["rcount"] = np.stack([(np.float32(1) / count)[2 * i + d // 64] for i in range(2)], 1).reshape(P, -1)
    c["restart"] = np.broadcast_to(t % CHUNK != 0, (P, T))
    q = np.arange(P)[:, None, None] + P * np.arange(NB)[None, :, None]
    window = np.where(np.abs(q - t[None, None, :]) <= 128, 0.0, NEG).astype(np.float32)
    c["iota"] = np.broadcast_to(np.arange(TOPK), (P, TOPK))
    s, u = np.arange(P)[:, None], np.arange(P)[None, :]
    masks = [s == u]
    for m in (1, 2, 4, 8, 16, 32, 64):
        masks.append((s // (2 * m) == u // (2 * m)) & (s // m % 2 == 0) & (u // m % 2 == 1))
    consts = np.concatenate([np.asarray(c[n], np.float32).reshape(P, -1) for n in CONSTS], 1)
    return consts, np.stack(masks, 1).astype(np.uint8).reshape(P, -1).view(np.uint32), window


def laid_out(x):
    def fm(v):
        return np.moveaxis(v.reshape(*v.shape[:-1], -1, P), -1, 0)

    def fm_chunks(w):
        return w.reshape(KT, P, -1, P).transpose(2, 1, 0, 3).reshape(-1, P, D)

    def tm_chunks(w):
        return w.reshape(2, 4, P, -1, T).transpose(3, 0, 2, 1, 4).reshape(-1, P, D)

    def act(v):
        return v.T.reshape(KT, P, T).transpose(1, 0, 2)

    ffn, mixw, secw = [], [], []
    for l in range(L):
        for w in ("ffn1", "ffn2"):
            ffn.append(np.stack([fm_chunks(x[w + "_gate"][l]), fm_chunks(x[w + "_up"][l]),
                                 x[w + "_down"][l].reshape(FT, P, D)], 1))
        cb, cc, ch, rq, rf, ri, rg, pu = np.split(x["w_in"][l], np.cumsum([256, 256, 256, 512, 512, 512, 512]), axis=1)
        mixw += [fm_chunks(rf), fm_chunks(rq), tm_chunks(ri), fm_chunks(ch), fm_chunks(cc), fm_chunks(cb),
                 fm_chunks(pu), fm_chunks(rg), fm_chunks(x["ca_k"][l]), tm_chunks(x["ca_v"][l]),
                 fm_chunks(x["w_out"][l]), fm_chunks(x["ca_q"][l]), fm_chunks(x["ca_o"][l])]
        secw += [fm_chunks(x["ada_w_2"][l]), fm_chunks(x["w_qkv_2"][l][:, :1280]), tm_chunks(x["w_qkv_2"][l][:, 1280:]),
                 fm_chunks(x["w_o_2"][l]), fm_chunks(x["peer_w_q_2"][l])]
    vecs1 = []
    for l in range(L):
        blocks = np.zeros((P, 2, P), np.float32)
        for g in range(4):
            at = slice(64 * (g % 2), 64 * (g % 2) + 64)
            blocks[at, g // 2, at] = x["pool_w"][l, g]
        parts = dict(ln_g=fm(x["ln_g"][l]), ln_b=fm(x["ln_b"][l]), conv_w=fm(x["conv_w"][l]).transpose(0, 2, 1),
                     lb=fm(x["rec_lb"][l]), omlb=np.zeros((P, 4), np.float32), norm_g=fm(x["rec_norm_g"][l]),
                     pool_scale=fm(x["pool_scale"][l]), pool_w=blocks)
        vecs1 += [parts[n].reshape(P, -1) for n in FIRST]
    rows = lambda v: np.broadcast_to(v.reshape(1, -1), (P, v.size))
    parts = dict(ada_b=fm(x["ada_b_2"]), gain1=fm(x["norm1_gain_2"]), gain2=fm(x["norm2_gain_2"]),
                 q_gain=x["q_norm_gain_2"].T, k_gain=x["k_norm_gain_2"].T, sinks=rows(x["attn_sinks_2"][0]),
                 c=np.stack([fm(x["c_2"][0]), fm(x["c_ctx_2"])], 2))
    consts, masks, window = shape_constants()
    return dict(consts=consts, masks=masks, window=window, vecs1=np.concatenate(vecs1, 1),
                vecs2=np.concatenate([parts[n].reshape(P, -1) for n in SECOND], 1),
                x_t=act(x["x"][0]), mem_t=act(x["mem"][0]), ctx_t=act(x["ctx_2"][0]), ffn=np.concatenate(ffn),
                mix_w=np.concatenate(mixw), second_w=np.concatenate(secw),
                subk=x["peer_sub_keys_2"].transpose(3, 0, 1, 2),
                peer_u=x["peer_u_2"].reshape(-1, D), peer_v=x["peer_v_2"].reshape(-1, D))


def kernel(**inputs):
    import concourse.bacc as bacc
    from concourse.bass_utils import run_bass_kernel_spmd

    nc = bacc.Bacc("TRN2", target_bir_lowering=False, num_devices=1)
    arrays, args = {}, {}
    for name, v in laid_out({n: np.asarray(v) for n, v in inputs.items()}).items():
        v = np.ascontiguousarray(v)
        arrays[f"in_{name}"] = v
        args[name] = nc.dram_tensor(f"in_{name}", v.shape, mybir.dt.from_np(v.dtype), kind="ExternalInput").ap()
    out = nc.dram_tensor("out_x", (P, KT, T), F32, kind="ExternalOutput").ap()
    program(nc, args, out)
    r = run_bass_kernel_spmd(nc, [arrays], core_ids=[0])
    got = r.results[0]["out_x"]
    return np.ascontiguousarray(got.transpose(2, 1, 0).reshape(1, T, D))
```

```python
from contextlib import ExitStack, contextmanager

import numpy as np

import concourse.bass as bass
from concourse import mybir

F32 = mybir.dt.float32
BF16 = mybir.dt.bfloat16
U32 = mybir.dt.uint32
U8 = mybir.dt.uint8
ALU = mybir.AluOpType
ACT = mybir.ActivationFunctionType
AX = mybir.AxisListType.X

P = 128
D = 1024
KT = D // P
T = 256
NB = T // P
L = 2
FT = 2816 // P
ALPHA = (2.0 * L) ** 0.25
LN_EPS = 1e-5
RMS_EPS = 1e-6
CHUNK = 64
REC_H = 4
CA_H = 4
CA_SCALE = 256.0 ** -0.5
HEADS = 8
GROUPS = 2
REP = HEADS // GROUPS
SCALE = 128.0 ** -0.5
N_KEYS = 128
N_EXPERTS = N_KEYS * N_KEYS
PEER_H = 8
TOPK = 16
SLOTS = PEER_H * TOPK
LOWEST = -3.0e38
NEG = -1e30

WR = 4
MIX_CHUNKS = 64
ADA_CHUNKS, QKV_CHUNKS, WO_CHUNKS, PQ_CHUNKS = 48, 12, 8, 16
SECOND_CHUNKS = ADA_CHUNKS + QKV_CHUNKS + WO_CHUNKS + PQ_CHUNKS
GR = 8
FT_STEP = 4
FT_TURNS = (FT - 2) // FT_STEP
TURN_SLOTS = 2 * GR
FT_SLOTS = TURN_SLOTS // FT_STEP
HEAD_SLOTS = GR
FF_SLOTS = HEAD_SLOTS + TURN_SLOTS * FT_TURNS
EARLY_DOTS = 8
LEVEL_DOTS = 2
LATE_DOTS = SLOTS - FF_SLOTS - EARLY_DOTS - 8 * LEVEL_DOTS
MIX_SUMS = 8, 16, 16
assert sum(MIX_SUMS) + FF_SLOTS == SLOTS and LATE_DOTS % TURN_SLOTS == 0

CONSTS = dict(ident=128, mean_d=128, rot=128, cos=256, sin=256, rcount=512, restart=256,
              iota=16)
FIRST = dict(ln_g=32, ln_b=32, conv_w=6, lb=4, omlb=4, norm_g=4, pool_scale=2, pool_w=256)
SECOND = dict(ada_b=L * 48, gain1=L * 8, gain2=L * 8, q_gain=L, k_gain=L, sinks=8, c=16)


def columns(parts):
    at, out = 0, {}
    for name, n in parts.items():
        out[name] = (at, n)
        at += n
    return out, at


AHEAD = dict(chunk_done=WR, gate_done=2, up_done=2, down_done=2, row_used=GR, h_done=1, z_done=1, hidden_done=1)


class Lane:

    def __init__(self, eng, refills=()):
        self.eng, self.refills, self.loops, self.count = eng, refills, [], {}

    def begin(self, name):
        return 0 if name in self.refills else AHEAD.get(name, 0)

    def now(self, sem, back=0):
        v = self.count.setdefault(sem.name, self.begin(sem.name)) - back
        for reg, per in self.loops:
            if per.get(sem.name):
                v = reg * per[sem.name] + v
        return v

    def skip(self, sem, by):
        self.count[sem.name] = self.count.get(sem.name, self.begin(sem.name)) + by

    def next(self, sem, by=1):
        self.skip(sem, by)
        return self.now(sem)

    def adds(self, sem, by=1):
        self.skip(sem, by)
        return by

    @contextmanager
    def loop(self, n, **per):
        begun = dict(self.count)
        with self.eng.Fori(0, n) as reg:
            self.loops.append((reg, per))
            yield reg
            self.loops.pop()
        for name, v in self.count.items():
            moved = v - begun.get(name, self.begin(name))
            assert moved == per.get(name, 0), (name, moved, per.get(name, 0))
            self.count[name] += (n - 1) * moved


def program(nc, a, out):
    with ExitStack() as ctx:
        def sems(names):
            return [ctx.enter_context(nc.semaphore(n)) for n in names.split()]

        (consts_in, window_in, vecs_in, masks_in, x_in, mem_in, ctx_in, subk_in) = sems(
            "consts_in window_in vecs_in masks_in x_in mem_in ctx_in subk_in")
        (chunk_done, gate_done, up_done, down_done) = sems(
            "chunk_done gate_done up_done down_done")
        (silu_done, hidden_done, resid_done, mean_done, centred_done, square_done, var_done, std_done,
         scaled_done, h_done) = sems(
            "silu_done hidden_done resid_done mean_done centred_done square_done var_done std_done "
            "scaled_done h_done")
        (layer_vecs, lb_max, lb_exp, eps_set, zeros_set) = sems(
            "layer_vecs lb_max lb_exp eps_set zeros_set")
        (z_done, f_done, log_done, decay_done, exp_done, qk_done, level_done, level_taken, o_done,
         o_square_done, o_ms_done, o_std_done) = sems(
            "z_done f_done log_done decay_done exp_done qk_done level_done level_taken o_done o_square_done "
            "o_ms_done o_std_done")
        (pooled_sums, pool_mm_done, pooled_done, conv_done, rec_done) = sems(
            "pooled_sums pool_mm_done pooled_done conv_done rec_done")
        (cs_done, cmax_done, cexp_done, cprob_done, cpt_done, cpt_taken, co_done, co_taken) = sems(
            "cs_done cmax_done cexp_done cprob_done cpt_done cpt_taken co_done co_taken")
        (c_silu, ada_taken, ada_done, mods_done, sq2_done, ms2_done, std2_done, norm2_done, mod2_done) = sems(
            "c_silu ada_taken ada_done mods_done sq2_done ms2_done std2_done norm2_done mod2_done")
        (qkv_taken, qk_sq_done, qk_ms_done, qk_std_done, rot_done, rot_taken, roped) = sems(
            "qkv_taken qk_sq_done qk_ms_done qk_std_done rot_done rot_taken roped")
        (s_done, s_max, sink_exp, s_exp, s_prob, pt_done, pt_taken, pv_done, pv_taken, x_added) = sems(
            "s_done s_max sink_exp s_exp s_prob pt_done pt_taken pv_done pv_taken x_added")
        (tm_done, tm_taken, pq_taken, sc_done, sc_taken, top_ready, top_exp, idx_done) = sems(
            "tm_done tm_taken pq_taken sc_done sc_taken top_ready top_exp idx_done")
        (idx_now_done, row_used, dots_done, gelu_done, pout_done, po_tm_done, x_final) = sems(
            "idx_now_done row_used dots_done gelu_done pout_done po_tm_done x_final")
        (pool_pause, dve_pause, dve_step, stored) = sems(
            "pool_pause dve_pause dve_step stored")
        weights_in = sems(" ".join(f"weights_{s}" for s in range(WR)))
        rows_in = sems(" ".join(f"rows_{s}" for s in range(GR)))
        ff_in = [sems(f"{part}_in_0 {part}_in_1") for part in ("gate", "up", "down")]
        ff_done = [gate_done, up_done, down_done]

        def sb(name, cols, dt=F32):
            return ctx.enter_context(nc.sbuf_tensor(name, [P, cols], dt))

        def view(tile, at, *dims):
            n = int(np.prod(dims))
            names = [f"d{i}" for i in range(len(dims))]
            if len(dims) == 1:
                return tile[:, at:at + n]
            return tile[:, at:at + n].rearrange(f"p ({' '.join(names)}) -> p {' '.join(names)}",
                                                **dict(zip(names[1:], dims[1:])))

        x_t = view(sb("x_t", KT * T), 0, KT, T)
        mem_tile = sb("mem_t", KT * T)
        mem_t = view(mem_tile, 0, KT, T)
        window = view(mem_tile, 0, NB, T)
        ctx_t = view(sb("ctx_t", KT * T), 0, KT, T)
        h_tm = view(sb("h_tm", NB * D), 0, NB, D)
        rows = view(sb("rows", GR * D), 0, GR, D)
        fw = view(sb("fw", 2 * 3 * D), 0, 2, 3, D)
        wring = view(sb("wring", WR * D), 0, WR, D)
        keys_t = view(sb("keys_t", GROUPS * 2 * T), 0, GROUPS, 2 * T)
        vals_tile = sb("vals", 4 * T)
        vals = view(vals_tile, 0, 4, GROUPS * P)
        cc, n_consts = columns(CONSTS)
        fc, n_first = columns(FIRST)
        sc_, n_second = columns(SECOND)
        consts = sb("consts", n_consts)
        masks_u32 = sb("masks", 8 * P // 4, U32)
        masks = masks_u32[:, :].bitcast(U8).rearrange("p (i t) -> p i t", t=P)
        first = sb("first", L * n_first)
        cur = sb("cur", n_first)
        second = sb("second", n_second)
        subk = view(sb("subk", L * 2 * N_KEYS), 0, L, 2, N_KEYS)
        mods = view(sb("mods", L * 48 * 2), 0, L, 48, 2)
        gains = view(sb("gains", L * 2 * 8 * 2), 0, L, 2, 8, 2)
        idx = view(sb("idx", NB * SLOTS, U32), 0, NB, SLOTS)
        idx_now = view(sb("idx_now", 2 * GR, U32), 0, 2, GR)
        gates = view(sb("gates", NB * SLOTS), 0, NB, SLOTS)
        dots = sb("dots", SLOTS)
        wts = sb("wts", SLOTS)
        stage = sb("stage", TURN_SLOTS)
        zeros = sb("zeros", 512, BF16)
        eps = sb("eps", 2)
        cond = sb("cond", 2 * KT)
        std = sb("std", T)
        stats = sb("stats", 64)
        lbs = sb("lbs", 32)
        arena = sb("arena", 19044)

        def const(name, *dims):
            at, n = cc[name]
            return view(consts, at, *(dims or (n,)))

        ident, mean_d, rot = const("ident"), const("mean_d"), const("rot")
        cos, sin, restart, iota = const("cos"), const("sin"), const("restart"), const("iota")
        rcount = const("rcount", 2, T)

        def vec(tile, where, name, i=0, n=1):
            at = where[name][0] + i
            return tile[:, at:at + n]

        resid = view(arena, 0, KT, T)
        mix = view(arena, 0, KT, T)
        sq = view(arena, 2048, KT, T)
        z_f, z_q, z_g = (view(arena, 2048 + 1024 * i, REC_H, T) for i in range(3))
        z_h, z_c, z_b = (view(arena, 5120 + 512 * i, 2, T) for i in range(3))
        v_tm = view(arena, 6656, NB, 2, T)
        ca_q, ca_o = (view(arena, 2048 + 2048 * i, KT, T) for i in range(2))
        csum = view(arena, 7680, 4, T)
        dec = [view(arena, 8704 + 1024 * i, 4, T) for i in range(2)]
        ca_e = [view(arena, 1024 * i, CA_H, T) for i in range(2)]
        ca_pt = view(arena, 9728, NB, CA_H, P)
        qk = [[view(arena, 10752 + 2048 * i + 1024 * j, 4, T) for j in range(2)] for i in range(2)]
        ca_k = view(arena, 10752, KT, T)
        ca_v = view(arena, 12800, CA_H, NB, T)
        acc_levels = [view(arena, D * i, D) for i in range(2)]
        acc_first = [view(arena, 7680 + D * i, D) for i in range(2)]
        attn = view(arena, 14848, 3, REC_H, P)
        conv_u = view(arena, 16384, 2, T + 2)
        pool_u = view(arena, 16900, 2, T + 16)
        pool_s = [view(arena, 17444 + 544 * i, 2, T + 16) for i in range(2)]
        pool_p = view(arena, 18532, 2, T)
        silu = view(arena, 17444, 2, T)
        hidden = view(arena, 17956, 2, T)

        sq2 = view(arena, 0, KT, T)
        probs = [view(arena, at, REP, 2 * T) for at in (0, 13312)]
        over_sum = [view(arena, 15360 + 512 * i, REP, P) for i in range(2)]
        pscore = [view(arena, at, 2 * PEER_H, N_KEYS) for at in (0, 10240)]
        h2 = view(arena, 2048, KT, T)
        top_i = view(arena, 2048, 2 * PEER_H, TOPK)
        top_sc = [view(arena, 2304 + 128 * b, PEER_H, TOPK) for b in range(NB)]
        sel = [view(arena, 2560 + 128 * i, SLOTS) for i in range(6)]
        pos_u = arena[:, 3328:3712].bitcast(U32)
        qk_raw = view(arena, 4096, 10, T)
        qk_n = view(arena, 6656, 10, T)
        qk_r = view(arena, 9216, 10, T)
        pt = view(arena, 9216, 4, REP * P)
        o_t = view(arena, 11264, HEADS, T)
        pq_t = view(arena, 4096, 16, T)
        cand = view(arena, 8192, PEER_H, TOPK * TOPK)
        top_v = view(arena, 12288, 2 * PEER_H, TOPK)
        top_iu = arena[:, 12544:12800].bitcast(U32).rearrange("p (j k) -> p j k", k=TOPK)
        cand2 = view(arena, 12800, PEER_H, TOPK * TOPK)
        onehot = [view(arena, at, PEER_H, TOPK, TOPK) for at in (8192, 12800)]
        pscore2 = view(arena, 14848, 2 * PEER_H, N_KEYS)
        acc_second = [view(arena, 16896 + D * i, D) for i in range(2)]
        list_now = [arena[:, 14848:15360], arena[:, 15360:15872], arena[:, 15872:15936],
                    arena[:, 15936:16000].bitcast(U32)]
        ada_row = view(arena, 16896, 2, 512)

        ps_a = ctx.enter_context(nc.psum_tensor("ps_a", [P, 2048], F32))
        ps_b = ctx.enter_context(nc.psum_tensor("ps_b", [P, 1024], F32))
        ps_c = ctx.enter_context(nc.psum_tensor("ps_c", [P, 512], F32))
        ps_d = ctx.enter_context(nc.psum_tensor("ps_d", [P, 512], F32))
        acc_t = view(ps_a, 0, KT, T)
        block = ctx.enter_context(nc.Block())

        @block.sync
        def _(eng):
            sp = Lane(eng, ("chunk_done", "gate_done", "up_done", "down_done"))
            eng.dma_start(consts[:, :], a["consts"]).then_inc(consts_in, 16)
            eng.dma_start(second[:, :], a["vecs2"]).then_inc(vecs_in, 16)
            eng.dma_start(ctx_t, a["ctx_t"]).then_inc(ctx_in, 16)
            eng.dma_start(subk, a["subk"]).then_inc(subk_in, 16)
            eng.dma_start(first[:, :], a["vecs1"]).then_inc(vecs_in, 16)
            eng.dma_start(masks_u32[:, :], a["masks"]).then_inc(masks_in, 16)
            eng.dma_start(x_t, a["x_t"]).then_inc(x_in, 16)
            eng.dma_start(mem_t, a["mem_t"]).then_inc(mem_in, 16)

            def chunk_loads(src, at, n):
                def load(s, row):
                    eng.wait_ge(chunk_done, sp.next(chunk_done))
                    eng.dma_start(wring[:, s, :], row).then_inc(weights_in[s], sp.adds(weights_in[s], 16))
                turns = n // WR
                per = {f"weights_{s}": 16 for s in range(WR)}
                if turns > 2:
                    with sp.loop(turns, chunk_done=WR, **per) as i:
                        for s in range(WR):
                            load(s, src[bass.ds(i * WR + (at + s), 1), :, :].rearrange("a p c -> (a p) c"))
                else:
                    for j in range(n):
                        load(j % WR, src[bass.ds(at + j, 1), :, :].rearrange("a p c -> (a p) c"))

            def ff_loads(tile, ft, part):
                eng.wait_ge(ff_done[part], sp.next(ff_done[part]))
                eng.dma_start(
                    fw[:, ft % 2, part, :], a["ffn"][bass.ds(tile, 1), part, :, :].rearrange("a p c -> (a p) c")).then_inc(ff_in[part][ft % 2], sp.adds(ff_in[part][ft % 2], 16))

            chunk_loads(a["second_w"], 0, SECOND_CHUNKS)
            chunk_loads(a["second_w"], SECOND_CHUNKS, ADA_CHUNKS)
            ff_per = {f"{n}_in_{s}": 16 for n in ("gate", "up", "down") for s in range(2)}
            ff_turn = {k: 16 * FT_STEP // 2 for k in ff_per} | dict(gate_done=FT_STEP, up_done=FT_STEP,
                                                                    down_done=FT_STEP)
            ff_layer = {k: 16 * FT for k in ff_per} | dict(gate_done=2 * FT, up_done=2 * FT, down_done=2 * FT)
            with sp.loop(L, chunk_done=MIX_CHUNKS, **{f"weights_{s}": 16 * MIX_CHUNKS // WR for s in range(WR)},
                         **ff_layer) as l:
                for w in range(2):
                    for ft in range(2):
                        for part in range(3):
                            ff_loads(l * (2 * FT) + (w * FT + ft), ft, part)
                    if w == 0:
                        chunk_loads(a["mix_w"], l * MIX_CHUNKS, WR)
                    else:
                        chunk_loads(a["mix_w"], l * MIX_CHUNKS + (MIX_CHUNKS - WR), WR)
                    with sp.loop(FT_TURNS, **ff_turn) as i:
                        for ft in range(FT_STEP):
                            for part in range(3):
                                ff_loads(l * (2 * FT) + (w * FT + 2 + ft) + i * FT_STEP, ft, part)
                    if w == 0:
                        chunk_loads(a["mix_w"], l * MIX_CHUNKS + WR, MIX_CHUNKS - 2 * WR)
            chunk_loads(a["second_w"], ADA_CHUNKS, SECOND_CHUNKS - ADA_CHUNKS)
            chunk_loads(a["second_w"], SECOND_CHUNKS + ADA_CHUNKS + 8, 4)
            eng.wait_ge(chunk_done, sp.now(chunk_done))
            eng.dma_start(window, a["window"]).then_inc(window_in, 16)
            chunk_loads(a["second_w"], SECOND_CHUNKS + ADA_CHUNKS, SECOND_CHUNKS - ADA_CHUNKS)
            eng.wait_ge(x_final, sp.next(x_final, 3 * KT))
            eng.dma_start(out, x_t).then_inc(stored, 16)
            eng.wait_ge(stored, 16)

        @block.gpsimd
        def _(eng):
            po = Lane(eng, ("row_used",))
            G = nc.gpsimd

            def pause():
                eng.sem_inc(pool_pause, 1)

            def gather(table, where):
                per = {f"rows_{s}": 32 for s in range(GR)}
                with po.loop(SLOTS // (2 * GR), row_used=2 * GR, idx_now_done=2, **per) as i:
                    for half in range(2):
                        eng.wait_ge(row_used, po.now(row_used, -1))
                        G.tensor_copy(
                            idx_now[:, half, :], where[:, bass.ds(i * (2 * GR) + half * GR, GR)]).then_inc(idx_now_done, po.adds(idx_now_done))
                        eng.wait_ge(idx_now_done, po.now(idx_now_done))
                        for s in range(GR):
                            eng.wait_ge(row_used, po.next(row_used))
                            pause()
                            G.indirect_dma_start(
                                rows[:, s, :], None, table,
                                bass.IndirectOffsetOnAxis(ap=idx_now[:, half, s:s + 1], axis=0)).then_inc(rows_in[s], po.adds(rows_in[s], 16))

            slots = dict(row_used=2 * SLOTS, idx_now_done=4 * SLOTS // (2 * GR),
                         **{f"rows_{s}": 64 * SLOTS // (2 * GR) for s in range(GR)})
            with po.loop(L, idx_done=1, **slots) as l:
                eng.wait_ge(idx_done, po.next(idx_done))
                pause()
                where = idx[:, bass.ds(l, 1), :].rearrange("p a s -> p (a s)")
                gather(a["peer_u"], where)
                gather(a["peer_v"], where)
            with po.loop(L, idx_done=NB, **{k: 2 * v for k, v in slots.items()}):
                for b in range(NB):
                    eng.wait_ge(idx_done, po.next(idx_done))
                    pause()
                    gather(a["peer_u"], idx[:, b, :])
                    gather(a["peer_v"], idx[:, b, :])

        @block.tensor
        def _(eng):
            pe = Lane(eng)
            mm = nc.tensor.matmul

            def chunk(s):
                eng.wait_ge(weights_in[s], pe.next(weights_in[s], 16))
                return wring[:, s, :]

            def acc_groups(src, act_ready=None):
                for j in range(KT):
                    w = chunk(j % WR)
                    for k in range(KT):
                        if j == 0 and act_ready:
                            act_ready(k)
                        ins = mm(acc_t[:, j, :], w[:, k * P:(k + 1) * P], src[:, k, :], start=k == 0, stop=k == KT - 1)
                    ins.then_inc(chunk_done, pe.adds(chunk_done))

            def fm_group(c, bank, src, act_ready=None):
                for t in range(2):
                    w = chunk((c + t) % WR)
                    for k in range(KT):
                        if t == 0 and act_ready:
                            act_ready(k)
                        ins = mm(bank[:, t * T:(t + 1) * T], w[:, k * P:(k + 1) * P], src[:, k, :],
                                 start=k == 0, stop=k == KT - 1)
                    ins.then_inc(chunk_done, pe.adds(chunk_done))

            def tm_group(c, bank, src):
                w = [chunk((c + t) % WR) for t in range(2)]
                for b in range(NB):
                    for k in range(KT):
                        ins = mm(bank[:, b * T:(b + 1) * T], src[:, k, b * P:(b + 1) * P],
                                 w[k // 4][:, (k % 4) * T:(k % 4 + 1) * T], start=k == 0, stop=k == KT - 1)
                        if b == NB - 1 and k in (3, 7):
                            ins.then_inc(chunk_done, pe.adds(chunk_done))

            def mean_of(src, bank, weights, ready, n_ready):
                for k in range(KT):
                    if k % (KT // n_ready) == 0:
                        eng.wait_ge(ready, pe.next(ready))
                    ins = mm(bank, weights, src[:, k, :], start=k == 0, stop=k == KT - 1)
                return ins

            def ada():
                per = {f"weights_{s}": 32 for s in range(WR)}
                with pe.loop(ADA_CHUNKS // (2 * WR), chunk_done=2 * WR, ada_taken=2, ada_done=1, **per) as i:
                    for half in range(2):
                        for s in range(WR):
                            w = chunk(s)
                            for k in range(2):
                                ins = mm(ps_b[0:2, half * 512:(half + 1) * 512], cond[:, 4 * s + 2 * k:4 * s + 2 * k + 2],
                                         w[:, k * 512:(k + 1) * 512], start=s + k == 0, stop=(s, k) == (WR - 1, 1))
                            ins.then_inc(chunk_done, pe.adds(chunk_done))
                    for half in range(2):
                        eng.wait_ge(ada_taken, pe.next(ada_taken))
                        for q in range(4):
                            ins = mm(ps_d[:, bass.ds(i * 16 + half * 8 + 2 * q, 2)], ada_row[0:2, half, q * P:(q + 1) * P],
                                     ident[0:2, 0:2], start=True, stop=True)
                    ins.then_inc(ada_done, pe.adds(ada_done))

            def rms():
                mean_of(sq2, ps_c[:, 0:T], mean_d, sq2_done, 4).then_inc(ms2_done, pe.adds(ms2_done))

            def mod_ready(k):
                eng.wait_ge(mod2_done, pe.next(mod2_done))

            def qkv(groups, rope):
                def stats(n, g):
                    eng.wait_ge(qk_sq_done, pe.next(qk_sq_done))
                    if n >= 2:
                        eng.wait_ge(qk_std_done, pe.next(qk_std_done))
                    mm(ps_a[:, (g % 2) * 512:(g % 2 + 1) * 512], mean_d, view(arena, 9216 + 512 * g, 512),
                       start=True, stop=True).then_inc(qk_ms_done, pe.adds(qk_ms_done))
                    eng.wait_ge(qkv_taken, pe.next(qkv_taken))
                    if rope:
                        if n >= 2:
                            eng.wait_ge(rot_taken, pe.next(rot_taken))
                        mm(ps_a[:, 1024 + (g % 2) * 512:1024 + (g % 2 + 1) * 512], rot, view(arena, 4096 + 512 * g, 512),
                           start=True, stop=True).then_inc(rot_done, pe.adds(rot_done))

                for n, g in enumerate(groups):
                    fm_group(2 * g, ps_b[:, (g % 2) * 512:(g % 2 + 1) * 512], h2, None if n else mod_ready)
                    if n:
                        stats(n - 1, groups[n - 1])
                tm_group(2, ps_b[:, 512:1024], h2)
                stats(len(groups) - 1, groups[-1])
                eng.wait_ge(qkv_taken, pe.next(qkv_taken))
                pe.skip(qk_std_done, min(len(groups), 2))
                pe.skip(rot_taken, 2 if rope else 0)

            def attention(blocks, windowed):
                n, units = len(blocks) * P, NB * GROUPS
                eng.wait_ge(roped, pe.next(roped))

                def unit_scores(u):
                    b, g = u // GROUPS, u % GROUPS
                    if u:
                        eng.wait_ge(s_exp, pe.next(s_exp))
                    for r in range(REP):
                        q = qk_n[:, REP * g + r, b * P:(b + 1) * P]
                        if windowed:
                            mm(ps_a[:, r * 512:r * 512 + T], q, keys_t[:, g, 0:T], start=True, stop=True)
                            mm(ps_a[:, r * 512 + T:r * 512 + 2 * T], q, keys_t[:, g, T:2 * T], start=True, stop=False)
                            ins = mm(ps_a[:, r * 512 + T:r * 512 + 2 * T], ident, window[:, b, :], start=False, stop=True)
                        else:
                            ins = mm(ps_a[:, r * 512:r * 512 + n], q, keys_t[:, g, 0:n], start=True, stop=True)
                    ins.then_inc(s_done, pe.adds(s_done))

                unit_scores(0)
                for u in range(units):
                    if u + 1 < units:
                        unit_scores(u + 1)
                    eng.wait_ge(s_prob, pe.next(s_prob))
                    for j in blocks:
                        if u or j >= 2:
                            eng.wait_ge(pt_taken, pe.next(pt_taken))
                        for r in range(REP):
                            ins = mm((ps_c, ps_d)[j % 2][:, r * P:(r + 1) * P], probs[u % 2][:, r, j * P:(j + 1) * P],
                                     over_sum[u % 2][:, r, :], start=True, stop=True)
                        ins.then_inc(pt_done, pe.adds(pt_done))
                    eng.wait_ge(pt_taken, pe.now(pt_taken, -2))
                    if u >= 2:
                        eng.wait_ge(pv_taken, pe.next(pv_taken))
                    for j in blocks:
                        ins = mm(ps_b[:, (u % 2) * 512:(u % 2 + 1) * 512],
                                 vals[:, j, u % GROUPS * P:(u % GROUPS + 1) * P], pt[:, j, :],
                                 start=j == blocks[0], stop=j == blocks[-1])
                    ins.then_inc(pv_done, pe.adds(pv_done))
                pe.skip(pt_taken, 2)
                eng.wait_ge(s_exp, pe.next(s_exp))
                eng.wait_ge(pv_taken, pe.next(pv_taken, 2))

            def project_out():
                acc_groups(o_t)

            def peer_scores(l):
                rms()
                for k in range(KT):
                    eng.wait_ge(mod2_done, pe.next(mod2_done))
                for b in range(NB):
                    for k in range(KT):
                        ins = nc.tensor.transpose(ps_a[:, b * D + k * P:b * D + (k + 1) * P],
                                                  h2[:, k, b * P:(b + 1) * P], ident)
                ins.then_inc(tm_done, pe.adds(tm_done))
                for g in range(8):
                    if g >= 2:
                        eng.wait_ge(pq_taken, pe.next(pq_taken))
                    fm_group(2 * g, ps_b[:, (g % 2) * 512:(g % 2 + 1) * 512], h2)
                eng.wait_ge(pq_taken, pe.next(pq_taken, 2))
                eng.wait_ge(tm_taken, pe.next(tm_taken))
                for b in range(NB):
                    if b:
                        eng.wait_ge(sc_taken, pe.next(sc_taken))
                    for j in range(2 * PEER_H):
                        ins = mm(ps_a[:, j * N_KEYS:(j + 1) * N_KEYS], pq_t[:, j, b * P:(b + 1) * P],
                                 subk[:, l, j % 2, :], start=True, stop=True)
                    ins.then_inc(sc_done, pe.adds(sc_done))
                eng.wait_ge(sc_taken, pe.next(sc_taken))

            def finish():
                eng.wait_ge(pout_done, pe.next(pout_done, NB))
                for k in range(KT):
                    for b in range(NB):
                        ins = nc.tensor.transpose(acc_t[:, k, b * P:(b + 1) * P], h_tm[:, b, k * P:(k + 1) * P], ident)
                ins.then_inc(po_tm_done, pe.adds(po_tm_done))

            eng.sem_inc(chunk_done, AHEAD["chunk_done"])
            eng.sem_inc(gate_done, AHEAD["gate_done"])
            eng.sem_inc(up_done, AHEAD["up_done"])
            eng.sem_inc(down_done, AHEAD["down_done"])
            eng.wait_ge(consts_in, 16)
            eng.wait_ge(subk_in, 16)
            eng.wait_ge(c_silu, pe.next(c_silu))
            ada()
            rms()
            qkv([0, 1, 2, 3, 4], False)
            attention([0, 1], False)
            project_out()
            peer_scores(0)
            ada()

            eng.wait_ge(x_in, 16)
            eng.wait_ge(mem_in, 16)
            eng.wait_ge(zeros_set, 1)

            def feed_forward(h_ready):
                for j in range(4):
                    mm(ps_a[:, j * 512:(j + 1) * 512], zeros[:, 0:P], zeros[:, :], start=True, stop=False,
                       skip_group_check=True)

                def gate_up(ft, first=False):
                    bank = ps_b[:, (ft % 2) * 512:(ft % 2 + 1) * 512]
                    for part in range(2):
                        eng.wait_ge(ff_in[part][ft % 2], pe.next(ff_in[part][ft % 2], 16))
                        for k in range(KT):
                            if first and part == 0:
                                h_ready(k)
                            ins = mm(bank[:, part * T:(part + 1) * T], fw[:, ft % 2, part, k * P:(k + 1) * P],
                                     x_t[:, k, :], start=k == 0, stop=k == KT - 1)
                        ins.then_inc(ff_done[part], pe.adds(ff_done[part]))

                def down(ft, last=False):
                    eng.wait_ge(hidden_done, pe.next(hidden_done))
                    eng.wait_ge(ff_in[2][ft % 2], pe.next(ff_in[2][ft % 2], 16))
                    for j in range(KT):
                        ins = mm(acc_t[:, j, :], fw[:, ft % 2, 2, j * P:(j + 1) * P], hidden[:, ft % 2, :],
                                 start=False, stop=last, skip_group_check=True)
                        if j == KT - 1:
                            ins.then_inc(down_done, pe.adds(down_done))

                gate_up(0, True)
                per = {f"{n}_in_{s}": 16 * FT_STEP // 2 for n in ("gate", "up", "down") for s in range(2)}
                with pe.loop(FT_TURNS, hidden_done=FT_STEP, gate_done=FT_STEP, up_done=FT_STEP, down_done=FT_STEP,
                             **per):
                    for q in range(FT_STEP):
                        gate_up(q + 1)
                        down(q)
                gate_up(FT - 1)
                down(FT - 2)
                down(FT - 1, True)

            def layer_norm():
                mean_of(resid, ps_c[:, 0:T], mean_d, resid_done, 4).then_inc(mean_done, pe.adds(mean_done))
                mean_of(sq, ps_d[:, 0:T], mean_d, square_done, 4).then_inc(var_done, pe.adds(var_done))

            def h_take(k):
                eng.wait_ge(h_done, pe.next(h_done))

            def h_have(k):
                if k == 0:
                    eng.wait_ge(h_done, pe.now(h_done))

            ff = {f"{n}_in_{s}": 16 * FT for n in ("gate", "up", "down") for s in range(2)}
            with pe.loop(L, chunk_done=MIX_CHUNKS, **{f"weights_{s}": 16 * MIX_CHUNKS // WR for s in range(WR)},
                         hidden_done=2 * FT, gate_done=2 * FT, up_done=2 * FT, down_done=2 * FT, **ff,
                         h_done=4 * KT, resid_done=16, square_done=16, mean_done=4, var_done=4, z_done=24,
                         qk_done=9, level_done=9, level_taken=9, o_done=1, o_square_done=2, o_ms_done=1,
                         pooled_sums=1, pool_mm_done=1, pooled_done=1, conv_done=1, rec_done=1, cs_done=NB,
                         cprob_done=NB, cpt_done=2 * NB, cpt_taken=2 * NB, co_done=NB, co_taken=NB) as l:
                feed_forward(h_have)
                layer_norm()

                def group(g, c, src, ready=None, tm=False):
                    if g:
                        eng.wait_ge(z_done, pe.now(z_done, 1))
                    bank = ps_b[:, (g % 2) * 512:(g % 2 + 1) * 512]
                    if tm:
                        tm_group(c, bank, src)
                    else:
                        fm_group(c, bank, src, ready)
                    pe.skip(z_done, 1)

                def level(i):
                    eng.wait_ge(qk_done, pe.next(qk_done))
                    if i >= 2:
                        eng.wait_ge(level_taken, pe.next(level_taken))
                    q, k = (z_q, z_f) if i == 0 else qk[i % 2]
                    for b in range(NB if i < 8 else 1):
                        for h in range(REC_H):
                            ks = slice(b * P, (b + 1) * P)
                            qs = ks if i < 8 else slice(P, 2 * P)
                            ins = mm(ps_a[:, (i % 2) * 1024 + b * 512 + h * P:(i % 2) * 1024 + b * 512 + (h + 1) * P],
                                     k[:, h, ks], q[:, h, qs], start=True, stop=True)
                    ins.then_inc(level_done, pe.adds(level_done))

                for g in range(4):
                    group(g, 2 * g, x_t, h_take if g == 0 else None)
                for g in range(4, 12):
                    group(g, 2 * g, x_t, tm=g < 6)
                    level(g - 4)
                level(8)
                eng.wait_ge(level_taken, pe.next(level_taken, 2))
                eng.wait_ge(z_done, pe.now(z_done, 0))
                for h in range(REC_H):
                    o = ps_a[:, 1024 + h * T:1024 + (h + 1) * T]
                    vs = [v_tm[:, h // 2, b, (h % 2) * P:(h % 2 + 1) * P] for b in range(NB)]
                    mm(o[:, 0:P], vs[0], attn[:, 0, h, :], start=True, stop=True)
                    mm(o[:, P:T], vs[0], attn[:, 2, h, :], start=True, stop=False)
                    ins = mm(o[:, P:T], vs[1], attn[:, 1, h, :], start=False, stop=True)
                ins.then_inc(o_done, pe.adds(o_done))
                group(12, 24, mem_t)
                for j in range(2):
                    eng.wait_ge(o_square_done, pe.next(o_square_done))
                    ins = mm(ps_a[:, j * 512:(j + 1) * 512], mean_d, view(arena, 8704 + 512 * j, 512),
                             start=True, stop=True)
                ins.then_inc(o_ms_done, pe.adds(o_ms_done))
                for g in range(13, 20):
                    group(g, 2 * g, mem_t, tm=g >= 16)
                eng.wait_ge(pooled_sums, pe.next(pooled_sums))
                eng.wait_ge(mods_done, L)
                for t in range(2):
                    at = fc["pool_w"][0] + t * P
                    ins = mm(ps_d[:, t * T:(t + 1) * T], cur[:, at:at + P], pool_p[:, t, :], start=True, stop=True)
                ins.then_inc(pool_mm_done, pe.adds(pool_mm_done))
                for part_done in (pooled_done, conv_done, rec_done):
                    eng.wait_ge(part_done, pe.next(part_done))
                acc_groups(mix)
                layer_norm()
                for g in range(20, 24):
                    group(g, 2 * g, x_t, h_take if g == 20 else None)
                eng.wait_ge(z_done, pe.now(z_done, 0))
                def ca_scores(b):
                    for h in range(CA_H):
                        for c in range(2):
                            ins = mm(ps_a[:, b * 1024 + h * T:b * 1024 + (h + 1) * T],
                                     ca_q[:, 2 * h + c, b * P:(b + 1) * P], ca_k[:, 2 * h + c, :],
                                     start=c == 0, stop=c == 1)
                    ins.then_inc(cs_done, pe.adds(cs_done))
                ca_scores(0)
                ca_scores(1)
                for b in range(NB):
                    eng.wait_ge(cprob_done, pe.next(cprob_done))
                    for m in range(NB):
                        for h in range(CA_H):
                            ins = nc.tensor.transpose((ps_c, ps_d)[m][:, h * P:(h + 1) * P],
                                                      ca_e[b][:, h, m * P:(m + 1) * P], ident)
                        ins.then_inc(cpt_done, pe.adds(cpt_done))
                    eng.wait_ge(cpt_taken, pe.next(cpt_taken, 2))
                    if b:
                        eng.wait_ge(co_taken, pe.next(co_taken))
                    for h in range(CA_H):
                        for c in range(2):
                            for m in range(NB):
                                ins = mm(ps_b[:, (2 * h + c) * P:(2 * h + c + 1) * P],
                                         ca_v[:, h, m, c * P:(c + 1) * P], ca_pt[:, m, h, :],
                                         start=m == 0, stop=m == 1)
                    ins.then_inc(co_done, pe.adds(co_done))
                eng.wait_ge(co_taken, pe.next(co_taken))
                acc_groups(ca_o)
                layer_norm()
                feed_forward(h_take)
                layer_norm()
                pe.skip(h_done, KT)

            for l in range(L):
                rms()
                if l == 0:
                    finish()
                    eng.wait_ge(x_final, pe.next(x_final, KT))
                qkv([0, 1, 2, 3, 4], True)
                if l == 1:
                    eng.wait_ge(window_in, 16)
                attention([0, 1, 2, 3], l == 1)
                project_out()
                peer_scores(l)
                if l == 0:
                    rms()
                    qkv([4], False)
                    eng.wait_ge(roped, pe.next(roped))
                finish()

        @block.scalar
        def _(eng):
            ac = Lane(eng)

            def act(out, in_, func, **k):
                return nc.scalar.activation(out, in_, func, **k)

            def rms(src, l, part, who, ready=None):
                for j in range(4):
                    if ready is not None:
                        eng.wait_ge(ready, ac.next(ready, 2))
                    act(
                        sq2[:, 2 * j:2 * j + 2, :], src[:, 2 * j:2 * j + 2, :], ACT.Square).then_inc(sq2_done, ac.adds(sq2_done))
                eng.wait_ge(ms2_done, ac.next(ms2_done))
                act(std[:, :], ps_c[:, 0:T], ACT.Sqrt, bias=eps[:, 1:2]).then_inc(std2_done, ac.adds(std2_done))
                for k in range(KT):
                    if k % 2 == 0:
                        eng.wait_ge(norm2_done, ac.next(norm2_done))
                    act(h2[:, k, :], h2[:, k, :], ACT.Identity, scale=gains[:, l, part, k, who:who + 1],
                                            bias=mods[:, l, 24 * part + k, who:who + 1]).then_inc(mod2_done, ac.adds(mod2_done))

            def qkv(l, groups, first_block):
                def deviation(g):
                    eng.wait_ge(qk_ms_done, ac.next(qk_ms_done))
                    act(view(arena, 9216 + 512 * g, 512), ps_a[:, (g % 2) * 512:(g % 2 + 1) * 512], ACT.Sqrt,
                        scale=D / P, bias=eps[:, 1:2]).then_inc(qk_std_done, ac.adds(qk_std_done))

                for n, g in enumerate(groups):
                    bank = ps_b[:, (g % 2) * 512:(g % 2 + 1) * 512]
                    gain = second[:, sc_["q_gain" if g < 4 else "k_gain"][0] + l:][:, 0:1]
                    eng.wait_ge(chunk_done, ac.next(chunk_done, 2))
                    act(view(arena, 9216 + 512 * g, 512), bank, ACT.Square).then_inc(qk_sq_done, ac.adds(qk_sq_done))
                    act(view(arena, 4096 + 512 * g, 512), bank, ACT.Copy, scale=gain).then_inc(
                        qkv_taken, ac.adds(qkv_taken))
                    if n:
                        deviation(groups[n - 1])
                eng.wait_ge(chunk_done, ac.next(chunk_done, 2))
                act(view(vals_tile, first_block * T, 512), ps_b[:, 512:1024], ACT.Copy).then_inc(
                    qkv_taken, ac.adds(qkv_taken))
                deviation(groups[-1])

            def attention(blocks, sink):
                n, units = len(blocks) * P, NB * GROUPS

                def exps(u):
                    eng.wait_ge(s_max, ac.next(s_max))
                    if sink:
                        act(stats[:, 16:20], stats[:, 12:16], ACT.Exp).then_inc(sink_exp, ac.adds(sink_exp))
                    for r in range(REP):
                        ins = act(probs[u % 2][:, r, 0:n], ps_a[:, r * 512:r * 512 + n], ACT.Exp, scale=SCALE,
                                  bias=stats[:, 4 + r:5 + r], accum_out=stats[:, 8 + r:9 + r])
                    ins.then_inc(s_exp, ac.adds(s_exp))

                exps(0)
                for u in range(units):
                    b, g = u // GROUPS, u % GROUPS
                    if u:
                        eng.wait_ge(pv_done, ac.now(pv_done))
                    for j in blocks:
                        eng.wait_ge(pt_done, ac.next(pt_done))
                        act(pt[:, j, :], (ps_c, ps_d)[j % 2][:, :], ACT.Copy).then_inc(pt_taken, ac.adds(pt_taken))
                    if u + 1 < units:
                        exps(u + 1)
                    eng.wait_ge(pv_done, ac.next(pv_done))
                    act(o_t[:, REP * g:REP * (g + 1), b * P:(b + 1) * P],
                        ps_b[:, (u % 2) * 512:(u % 2 + 1) * 512].rearrange("p (r t) -> p r t", t=P),
                        ACT.Copy).then_inc(pv_taken, ac.adds(pv_taken))

            def peer_scores(src, l, who):
                ac.skip(chunk_done, WO_CHUNKS)
                rms(src, l, 1, who, x_added)
                eng.wait_ge(tm_done, ac.next(tm_done))
                for j in range(4):
                    ins = act(h_tm[:, j // 2, (j % 2) * 512:(j % 2 + 1) * 512], ps_a[:, j * 512:(j + 1) * 512], ACT.Copy)
                ins.then_inc(tm_taken, ac.adds(tm_taken))
                for g in range(8):
                    eng.wait_ge(chunk_done, ac.next(chunk_done, 2))
                    act(pq_t[:, 2 * g:2 * g + 2, :],
                                           ps_b[:, (g % 2) * 512:(g % 2 + 1) * 512], ACT.Copy).then_inc(pq_taken, ac.adds(pq_taken))
                for b in range(NB):
                    eng.wait_ge(sc_done, ac.next(sc_done))
                    for j in range(4):
                        ins = act(pscore[b][:, 4 * j:4 * j + 4, :], ps_a[:, j * 512:(j + 1) * 512], ACT.Copy)
                    ins.then_inc(sc_taken, ac.adds(sc_taken))

            def top_exps(b):
                eng.wait_ge(top_ready, ac.next(top_ready))
                act(top_sc[b], top_sc[b], ACT.Exp).then_inc(top_exp, ac.adds(top_exp))

            def ada():
                with ac.loop(ADA_CHUNKS // (2 * WR), chunk_done=2 * WR, ada_taken=2):
                    for half in range(2):
                        eng.wait_ge(chunk_done, ac.next(chunk_done, WR))
                        act(ada_row[0:2, half, :], ps_b[0:2, half * 512:(half + 1) * 512], ACT.Copy).then_inc(
                            ada_taken, ac.adds(ada_taken))

            def peer_gelu():
                eng.wait_ge(dots_done, ac.next(dots_done))
                act(wts[:, :], dots[:, :], ACT.Gelu_apprx_tanh).then_inc(gelu_done, ac.adds(gelu_done))

            eng.sem_inc(h_done, AHEAD["h_done"])
            eng.sem_inc(z_done, AHEAD["z_done"])
            eng.wait_ge(vecs_in, 32)
            at = sc_["c"][0]
            act(cond[:, :], second[:, at:at + 2 * KT], ACT.Silu).then_inc(c_silu, ac.adds(c_silu))
            eng.wait_ge(lb_max, ac.next(lb_max))
            act(lbs[:, 8:16], lbs[:, 0:8], ACT.Exp).then_inc(lb_exp, ac.adds(lb_exp))
            ada()
            eng.wait_ge(ctx_in, 16)
            eng.wait_ge(eps_set, ac.next(eps_set))
            rms(ctx_t, 0, 0, 1)
            qkv(0, range(5), 0)
            attention([0, 1], False)
            peer_scores(ctx_t, 0, 1)
            ada()
            for b in range(NB):
                top_exps(b)

            def feed_forward():
                def tile(ft):
                    eng.wait_ge(up_done, ac.next(up_done))
                    act(
                        silu[:, ft % 2, :], ps_b[:, (ft % 2) * 512:(ft % 2) * 512 + T], ACT.Silu).then_inc(silu_done, ac.adds(silu_done))
                tile(0)
                with ac.loop(FT_TURNS, up_done=FT_STEP, silu_done=FT_STEP, hidden_done=FT_STEP):
                    for q in range(FT_STEP):
                        eng.wait_ge(hidden_done, ac.now(hidden_done))
                        tile(q + 1)
                        ac.skip(hidden_done, 1)
                eng.wait_ge(hidden_done, ac.now(hidden_done))
                tile(FT - 1)
                ac.skip(hidden_done, 2)

            def layer_norm(n):
                for j in range(4):
                    eng.wait_ge(centred_done, ac.next(centred_done))
                    act(
                        sq[:, 2 * j:2 * j + 2, :], resid[:, 2 * j:2 * j + 2, :], ACT.Square).then_inc(square_done, ac.adds(square_done))
                eng.wait_ge(var_done, ac.next(var_done))
                act(std[:, :], ps_d[:, 0:T], ACT.Sqrt, bias=eps[:, 0:1]).then_inc(std_done, ac.adds(std_done))
                for k in range(KT):
                    if k % 2 == 0:
                        eng.wait_ge(scaled_done, ac.next(scaled_done))
                    act(x_t[:, k, :], resid[:, k, :], ACT.Identity, scale=vec(cur, fc, "ln_g", n * KT + k),
                                         bias=vec(cur, fc, "ln_b", n * KT + k)).then_inc(h_done, ac.adds(h_done))

            with ac.loop(L, chunk_done=MIX_CHUNKS, up_done=2 * FT, silu_done=2 * FT, hidden_done=2 * FT,
                         centred_done=16, square_done=16, var_done=4, std_done=4, scaled_done=16, h_done=4 * KT,
                         z_done=24, f_done=1, log_done=1, decay_done=8, exp_done=8, o_done=1, o_square_done=2,
                         o_ms_done=1, o_std_done=1, pool_mm_done=1, pooled_done=1, cmax_done=NB, cexp_done=NB,
                         cpt_done=2 * NB, cpt_taken=2 * NB, co_done=NB, co_taken=NB, dots_done=1, gelu_done=1,
                         layer_vecs=1, qk_done=9) as l:
                eng.wait_ge(layer_vecs, ac.next(layer_vecs))
                feed_forward()
                layer_norm(0)

                def group(g, dst, func=ACT.Copy):
                    eng.wait_ge(chunk_done, ac.next(chunk_done, 2))
                    act(dst, ps_b[:, (g % 2) * 512:(g % 2 + 1) * 512], func).then_inc(z_done, ac.adds(z_done))

                def exps(i):
                    eng.wait_ge(decay_done, ac.next(decay_done))
                    act(dec[i % 2], dec[i % 2], ACT.Exp).then_inc(exp_done, ac.adds(exp_done))

                group(0, z_f[:, 0:2, :], ACT.Sigmoid)
                group(1, z_f[:, 2:4, :], ACT.Sigmoid)
                group(2, z_q[:, 0:2, :])
                group(3, z_q[:, 2:4, :])
                eng.wait_ge(f_done, ac.next(f_done))
                act(dec[0], z_f, ACT.Ln).then_inc(log_done, ac.adds(log_done))
                for g, dst in ((4, v_tm[:, 0]), (5, v_tm[:, 1]), (6, z_h), (7, z_c), (8, z_b)):
                    group(g, dst)
                    exps(g - 3)
                group(9, pool_u[:, :, 16:])
                exps(6)
                group(10, z_g[:, 0:2, :], ACT.Sigmoid)
                exps(7)
                group(11, z_g[:, 2:4, :], ACT.Sigmoid)
                exps(8)
                eng.wait_ge(o_done, ac.next(o_done))
                eng.wait_ge(qk_done, ac.next(qk_done, 9))
                for j in range(2):
                    act(view(arena, 8704 + 512 * j, 512), ps_a[:, 1024 + 512 * j:1536 + 512 * j],
                                                ACT.Square).then_inc(o_square_done, ac.adds(o_square_done))
                group(12, ca_k[:, 0:2, :])
                eng.wait_ge(o_ms_done, ac.next(o_ms_done))
                act(view(arena, 9728, 1024), ps_a[:, 0:1024], ACT.Sqrt, scale=D / P,
                                          bias=eps[:, 1:2]).then_inc(o_std_done, ac.adds(o_std_done))
                for g in range(13, 16):
                    group(g, ca_k[:, 2 * g - 24:2 * g - 22, :])
                for g in range(16, 20):
                    group(g, ca_v[:, g - 16])
                eng.wait_ge(pool_mm_done, ac.next(pool_mm_done))
                for t in range(2):
                    ins = act(mix[:, 6 + t, :], ps_d[:, t * T:(t + 1) * T], ACT.Copy, scale=vec(cur, fc, "pool_scale", t))
                ins.then_inc(pooled_done, ac.adds(pooled_done))
                peer_gelu()
                ac.skip(chunk_done, KT)
                layer_norm(1)
                for g in range(20, 24):
                    group(g, ca_q[:, 2 * g - 40:2 * g - 38, :])
                for b in range(NB):
                    eng.wait_ge(cmax_done, ac.next(cmax_done))
                    for h in range(CA_H):
                        ins = act(ca_e[b][:, h, :], ps_a[:, b * 1024 + h * T:b * 1024 + (h + 1) * T], ACT.Exp,
                                  scale=CA_SCALE, bias=stats[:, 24 + 4 * b + h:25 + 4 * b + h],
                                  accum_out=stats[:, 32 + 4 * b + h:33 + 4 * b + h])
                    ins.then_inc(cexp_done, ac.adds(cexp_done))
                for b in range(NB):
                    if b:
                        eng.wait_ge(co_done, ac.now(co_done))
                    for m in range(NB):
                        eng.wait_ge(cpt_done, ac.next(cpt_done))
                        act(ca_pt[:, m, :, :], (ps_c, ps_d)[m][:, :], ACT.Copy).then_inc(cpt_taken, ac.adds(cpt_taken))
                    eng.wait_ge(co_done, ac.next(co_done))
                    for j in range(2):
                        ins = act(ca_o[:, 4 * j:4 * j + 4, b * P:(b + 1) * P],
                                  ps_b[:, j * 512:(j + 1) * 512].rearrange("p (k t) -> p k t", t=P), ACT.Copy)
                    ins.then_inc(co_taken, ac.adds(co_taken))
                ac.skip(chunk_done, KT)
                layer_norm(2)
                feed_forward()
                layer_norm(3)

            for l in range(L):
                if l == 0:
                    eng.wait_ge(h_done, ac.now(h_done))
                    rms(x_t, 0, 0, 0)
                    ac.skip(x_final, KT)
                else:
                    rms(x_t, l, 0, 0, x_final)
                qkv(l, range(5), 2)
                attention([0, 1, 2, 3], l == 1)
                peer_scores(x_t, l, 0)
                top_exps(0)
                peer_gelu()
                top_exps(1)
                if l == 0:
                    eng.wait_ge(x_final, ac.now(x_final))
                    rms(ctx_t, 1, 0, 1)
                    qkv(1, [4], 0)
                peer_gelu()

        @block.vector
        def _(eng):
            ve = Lane(eng, ("down_done",))
            V = nc.vector
            phase = [0]

            def bcast(ap, *shape):
                return ap.to_broadcast([P, *shape])

            def modulation(l):
                ve.skip(chunk_done, ADA_CHUNKS)
                eng.wait_ge(ada_done, ve.next(ada_done, ADA_CHUNKS // (2 * WR)))
                at = sc_["ada_b"][0] + 48 * l
                V.tensor_tensor(mods[:, l], ps_d[:, 0:96].rearrange("p (j w) -> p j w", w=2),
                                     bcast(second[:, at:at + 48].unsqueeze(2), 48, 2), ALU.add).then_inc(dve_step, ve.adds(dve_step))
                eng.wait_ge(dve_step, ve.now(dve_step))
                for part in range(2):
                    at = sc_[("gain1", "gain2")[part]][0] + 8 * l
                    ins = V.scalar_tensor_tensor(gains[:, l, part], mods[:, l, 24 * part + 8:24 * part + 16, :], 1.0,
                                                 bcast(second[:, at:at + 8].unsqueeze(2), 8, 2), ALU.add, ALU.mult)
                    if part == 0:
                        ins.then_inc(dve_step, ve.adds(dve_step))
                eng.wait_ge(dve_step, ve.now(dve_step))
                ins.then_inc(mods_done, ve.adds(mods_done))

            def rms(src):
                eng.wait_ge(std2_done, ve.next(std2_done))
                V.reciprocal(std[:, :], std[:, :]).then_inc(dve_step, ve.adds(dve_step))
                eng.wait_ge(dve_step, ve.now(dve_step))
                for j in range(4):
                    V.tensor_tensor(h2[:, 2 * j:2 * j + 2, :], src[:, 2 * j:2 * j + 2, :],
                                                         bcast(std[:, :].unsqueeze(1), 2, T), ALU.mult).then_inc(norm2_done, ve.adds(norm2_done))

            def qk_norm(groups, rope, key_at):
                for g in groups:
                    raw, r = qk_raw[:, 2 * g:2 * g + 2, :], qk_r[:, 2 * g:2 * g + 2, :]
                    out = qk_n[:, 2 * g:2 * g + 2, :] if g < 4 else keys_t[:, :, key_at:key_at + T]
                    eng.wait_ge(qkv_taken, ve.next(qkv_taken))
                    eng.wait_ge(qk_std_done, ve.next(qk_std_done))
                    V.reciprocal(r, r).then_inc(dve_step, ve.adds(dve_step))
                    if rope:
                        eng.wait_ge(rot_done, ve.next(rot_done))
                        V.tensor_tensor(raw, raw, bcast(cos.unsqueeze(1), 2, T), ALU.mult).then_inc(
                            dve_step, ve.adds(dve_step))
                        V.tensor_tensor(out, view(ps_a, 1024 + (g % 2) * 512, 2, T), bcast(sin.unsqueeze(1), 2, T),
                                        ALU.mult).then_inc(rot_taken, ve.adds(rot_taken))
                        eng.wait_ge(dve_step, ve.now(dve_step))
                        eng.wait_ge(rot_taken, ve.now(rot_taken))
                        V.tensor_tensor(raw, raw, out, ALU.add).then_inc(dve_step, ve.adds(dve_step))
                    eng.wait_ge(dve_step, ve.now(dve_step))
                    ins = V.tensor_tensor(out, raw, r, ALU.mult)
                    if g < 4:
                        ins.then_inc(dve_step, ve.adds(dve_step))
                    else:
                        ins.then_inc(roped, ve.adds(roped))
                ve.skip(qkv_taken, 1)

            def attention(blocks, windowed):
                n = len(blocks) * P
                for u in range(NB * GROUPS):
                    b, g = u // GROUPS, u % GROUPS
                    eng.wait_ge(s_done, ve.next(s_done))
                    V.tensor_reduce(stats[:, 0:4], ps_a[:, :].rearrange("p (r k) -> p r k", r=REP)[:, :, 0:n], AX,
                                    ALU.max).then_inc(dve_step, ve.adds(dve_step))
                    eng.wait_ge(dve_step, ve.now(dve_step))
                    if windowed:
                        sink = second[:, sc_["sinks"][0] + REP * g:sc_["sinks"][0] + REP * (g + 1)]
                        V.scalar_tensor_tensor(stats[:, 0:4], stats[:, 0:4], SCALE, sink, ALU.mult,
                                               ALU.max).then_inc(dve_step, ve.adds(dve_step))
                        eng.wait_ge(dve_step, ve.now(dve_step))
                        V.tensor_tensor(stats[:, 12:16], sink, stats[:, 0:4], ALU.subtract).then_inc(
                            dve_step, ve.adds(dve_step))
                        eng.wait_ge(dve_step, ve.now(dve_step))
                    V.tensor_scalar(stats[:, 4:8], stats[:, 0:4], -1.0 if windowed else -SCALE, None,
                                    ALU.mult).then_inc(s_max, ve.adds(s_max))
                    if windowed:
                        eng.wait_ge(sink_exp, ve.next(sink_exp))
                    eng.wait_ge(s_exp, ve.next(s_exp))
                    if windowed:
                        V.tensor_tensor(stats[:, 8:12], stats[:, 8:12], stats[:, 16:20], ALU.add).then_inc(
                            dve_step, ve.adds(dve_step))
                        eng.wait_ge(dve_step, ve.now(dve_step))
                    V.reciprocal(stats[:, 20:24], stats[:, 8:12]).then_inc(dve_step, ve.adds(dve_step))
                    if u >= 2:
                        eng.wait_ge(pt_done, ve.next(pt_done, len(blocks)))
                    eng.wait_ge(dve_step, ve.now(dve_step))
                    V.tensor_tensor(over_sum[u % 2], bcast(ident.unsqueeze(1), REP, P),
                                    bcast(stats[:, 20:24].unsqueeze(2), REP, P), ALU.mult).then_inc(
                        s_prob, ve.adds(s_prob))
                ve.skip(pt_done, 2 * len(blocks))

            def gated_add(x, ps, l, part, who, added, ready=None):
                for k in range(KT):
                    if ready is not None and k % 2 == 0:
                        eng.wait_ge(ready, ve.next(ready, 2))
                    V.scalar_tensor_tensor(x[:, k, :], ps[:, k, :], mods[:, l, 24 * part + 16 + k, who:who + 1],
                                           x[:, k, :], ALU.mult, ALU.add).then_inc(added, ve.adds(added))

            def best_step(step, values, left, top, at):
                if step == 2:
                    return V.match_replace(left, top[:, 0:8], values, LOWEST)
                src, best = (values, slice(0, 8)) if step < 2 else (left, slice(8, 16))
                if step in (0, 3):
                    return V.max(top[:, best], src)
                return V.max_index(at[:, best], top[:, best], src)

            places = pos_u[:, 0:SLOTS].rearrange("p (h k) -> p h k", k=TOPK)
            key_lists = [(pscore[b], pscore2, top_v, top_iu) for b in range(NB)]
            sum_lists = [(cand, cand2, top_sc[b], places) for b in range(NB)]

            def sums_of_best():
                eng.wait_ge(dve_step, ve.now(dve_step))
                V.tensor_copy(top_i, top_iu).then_inc(dve_step, ve.adds(dve_step))
                halves = top_v.rearrange("p (h c) a -> p h c a", c=2)
                V.tensor_tensor(cand.rearrange("p h (a b) -> p h a b", b=TOPK),
                                bcast(halves[:, :, 0, :].unsqueeze(3), PEER_H, TOPK, TOPK),
                                bcast(halves[:, :, 1, :].unsqueeze(2), PEER_H, TOPK, TOPK),
                                ALU.add).then_inc(dve_step, ve.adds(dve_step))
                eng.wait_ge(dve_step, ve.now(dve_step))

            ID_PARTS = 5

            def expert_ids(l, b, part):
                ids = top_i.rearrange("p (h c) a -> p h c a", c=2)
                flat = [o.rearrange("p h k a -> p (h k) a") for o in onehot]
                eng.wait_ge(dve_step, ve.now(dve_step))
                if part == 0:
                    V.tensor_copy(stats[:, 0:8], top_sc[b][:, :, 0]).then_inc(dve_step, ve.adds(dve_step))
                    V.tensor_scalar(pos_u[:, SLOTS:2 * SLOTS], pos_u[:, 0:SLOTS], 4, None,
                                    ALU.logical_shift_right).then_inc(dve_step, ve.adds(dve_step))
                    V.tensor_scalar(pos_u[:, 2 * SLOTS:], pos_u[:, 0:SLOTS], 15, None,
                                    ALU.bitwise_and).then_inc(dve_step, ve.adds(dve_step))
                    eng.wait_ge(dve_step, ve.now(dve_step))
                    V.tensor_tensor(top_sc[b], top_sc[b], bcast(stats[:, 0:8].unsqueeze(2), PEER_H, TOPK),
                                    ALU.subtract).then_inc(top_ready, ve.adds(top_ready))
                    for c in range(2):
                        V.tensor_copy(sel[c], pos_u[:, (1 + c) * SLOTS:(2 + c) * SLOTS]).then_inc(
                            dve_step, ve.adds(dve_step))
                elif part == 1:
                    for c in range(2):
                        V.tensor_tensor(flat[c], bcast(sel[c].unsqueeze(2), SLOTS, TOPK),
                                        bcast(iota.unsqueeze(1), SLOTS, TOPK),
                                        ALU.is_equal).then_inc(dve_step, ve.adds(dve_step))
                elif part == 2:
                    for c in range(2):
                        V.tensor_tensor(onehot[c], onehot[c], bcast(ids[:, :, c, :].unsqueeze(2), PEER_H, TOPK, TOPK),
                                        ALU.mult).then_inc(dve_step, ve.adds(dve_step))
                elif part == 3:
                    for c in range(2):
                        V.tensor_reduce(sel[2 + c], flat[c], AX, ALU.add).then_inc(dve_step, ve.adds(dve_step))
                else:
                    V.tensor_scalar(sel[4], sel[2], float(N_KEYS), float(l * N_EXPERTS), ALU.mult,
                                    ALU.add).then_inc(dve_step, ve.adds(dve_step))
                    eng.wait_ge(dve_step, ve.now(dve_step))
                    V.tensor_tensor(sel[5], sel[4], sel[3], ALU.add).then_inc(dve_step, ve.adds(dve_step))
                    eng.wait_ge(dve_step, ve.now(dve_step))
                    V.tensor_copy(idx[:, b, :], sel[5]).then_inc(idx_done, ve.adds(idx_done))

            def top_experts(l, b):
                eng.wait_ge(sc_taken, ve.next(sc_taken))
                for step in range(5):
                    for j in range(2 * PEER_H):
                        best_step(step, *(v[:, j, :] for v in key_lists[b])).then_inc(dve_step, ve.adds(dve_step))
                    eng.wait_ge(dve_step, ve.now(dve_step))
                sums_of_best()
                for step in range(5):
                    for h in range(PEER_H):
                        best_step(step, *(v[:, h, :] for v in sum_lists[b])).then_inc(dve_step, ve.adds(dve_step))
                    eng.wait_ge(dve_step, ve.now(dve_step))
                for part in range(ID_PARTS):
                    expert_ids(l, b, part)

            def gate_experts(b):
                gate = gates[:, b, :].rearrange("p (h k) -> p h k", k=TOPK)
                eng.wait_ge(top_exp, ve.next(top_exp))
                V.tensor_reduce(stats[:, 8:16], top_sc[b], AX, ALU.add).then_inc(dve_step, ve.adds(dve_step))
                eng.wait_ge(dve_step, ve.now(dve_step))
                V.reciprocal(stats[:, 16:24], stats[:, 8:16]).then_inc(dve_step, ve.adds(dve_step))
                eng.wait_ge(dve_step, ve.now(dve_step))
                V.tensor_tensor(gate, top_sc[b], bcast(stats[:, 16:24].unsqueeze(2), PEER_H, TOPK),
                                ALU.mult).then_inc(dve_step, ve.adds(dve_step))

            def dot_slot(s, h, out, acc):
                eng.wait_ge(rows_in[s], ve.next(rows_in[s], 16))
                eng.wait_ge(row_used, ve.now(row_used, 1))
                V.scalar_tensor_tensor(acc[s % 2], rows[:, s, :], 1.0, h, ALU.mult, ALU.mult,
                                       accum_out=out).then_inc(row_used, ve.adds(row_used))

            def sum_slot(s, w, acc, first=False):
                eng.wait_ge(rows_in[s], ve.next(rows_in[s], 16))
                if first:
                    ins = V.tensor_scalar(acc[s % 2], rows[:, s, :], w, None, ALU.mult)
                else:
                    eng.wait_ge(row_used, ve.now(row_used, 1))
                    ins = V.scalar_tensor_tensor(acc[s % 2], rows[:, s, :], w, acc[s % 2], ALU.mult, ALU.add)
                ins.then_inc(row_used, ve.adds(row_used))

            def some_slots(summing, h, at, n, acc):
                for q in range(at, at + n):
                    if summing:
                        sum_slot(q % GR, wts[:, q:q + 1], acc, q < 2)
                    else:
                        dot_slot(q % GR, h, dots[:, q:q + 1], acc)

            def turn_begin(summing, i, at):
                eng.wait_ge(dve_step, ve.now(dve_step))
                if summing:
                    eng.wait_ge(row_used, ve.now(row_used))
                    V.tensor_copy(stage[:, :], wts[:, bass.ds(i * TURN_SLOTS + at, TURN_SLOTS)]).then_inc(
                        dve_step, ve.adds(dve_step))
                    eng.wait_ge(dve_step, ve.now(dve_step))

            def turn_slots(summing, h, at, n, acc):
                for q in range(at, at + n):
                    if summing:
                        sum_slot(q % GR, stage[:, q:q + 1], acc)
                    else:
                        dot_slot(q % GR, h, stage[:, q:q + 1], acc)

            def turn_end(summing, i, at):
                if not summing:
                    eng.wait_ge(row_used, ve.now(row_used))
                    V.tensor_copy(dots[:, bass.ds(i * TURN_SLOTS + at, TURN_SLOTS)], stage[:, :]).then_inc(
                        dve_step, ve.adds(dve_step))

            def phase_end(summing, out, acc):
                eng.wait_ge(row_used, ve.now(row_used))
                if summing:
                    V.tensor_tensor(out, acc[0], acc[1], ALU.add).then_inc(pout_done, ve.adds(pout_done))
                    eng.wait_ge(pout_done, ve.now(pout_done))
                else:
                    eng.wait_ge(dve_step, ve.now(dve_step))
                    V.tensor_copy(dots[:, 0:1], dots[:, 0:1]).then_inc(dots_done, ve.adds(dots_done))

            def weigh(gate):
                eng.wait_ge(gelu_done, ve.next(gelu_done))
                V.tensor_tensor(wts[:, :], wts[:, :], gate, ALU.mult).then_inc(dve_step, ve.adds(dve_step))
                eng.wait_ge(dve_step, ve.now(dve_step))

            per_turn = dict(row_used=TURN_SLOTS, dve_step=1, **{f"rows_{s}": 16 * TURN_SLOTS // GR for s in range(GR)})

            def plain_turns(summing, b, at):
                with ve.loop((SLOTS - at) // TURN_SLOTS, **per_turn) as i:
                    turn_begin(summing, i, at)
                    turn_slots(summing, h_tm[:, b, :], 0, TURN_SLOTS, acc_second)
                    turn_end(summing, i, at)

            def first_block_peer(l):
                h, half = h_tm[:, 0, :], SLOTS // 2
                turns = half // TURN_SLOTS
                eng.wait_ge(sc_taken, ve.next(sc_taken))
                for at, n, lists in ((0, 2 * PEER_H // turns, key_lists[1]), (half, PEER_H // turns, sum_lists[1])):
                    with ve.loop(turns, **per_turn | dict(dve_step=4 + 5 * n)) as i:
                        turn_begin(False, i, at)
                        now = [t[:, 0:n * c].rearrange("p (j k) -> p j k", j=n)
                               for t, c in zip(list_now, (512 // n, 512 // n, TOPK, TOPK))]
                        V.tensor_copy(now[0], lists[0][:, bass.ds(i * n, n), :]).then_inc(dve_step, ve.adds(dve_step))
                        for step in range(5):
                            eng.wait_ge(dve_step, ve.now(dve_step))
                            eng.sem_inc(dve_pause, 1)
                            for q in range(n):
                                best_step(step, *(t[:, q, :] for t in now)).then_inc(dve_step, ve.adds(dve_step))
                            turn_slots(False, h, 3 * step, 3 if step < 4 else TURN_SLOTS - 12, acc_second)
                        eng.wait_ge(dve_step, ve.now(dve_step))
                        for t, from_now in zip(lists[2:], now[2:]):
                            V.tensor_copy(t[:, bass.ds(i * n, n), :], from_now).then_inc(dve_step, ve.adds(dve_step))
                        turn_end(False, i, at)
                    if at == 0:
                        sums_of_best()
                        gate_experts(0)
                phase_end(False, h, acc_second)
                expert_ids(l, 1, 0)
                weigh(gates[:, 0, :])
                for part in range(1, ID_PARTS):
                    some_slots(True, h, 4 * (part - 1), 4, acc_second)
                    expert_ids(l, 1, part)
                plain_turns(True, 0, 4 * (ID_PARTS - 1))
                gate_experts(1)
                phase_end(True, h, acc_second)

            def second_block_peer(l):
                h = h_tm[:, 1, :]
                if l == 0:
                    rms(ctx_t)
                plain_turns(False, 1, 0)
                phase_end(False, h, acc_second)
                if l == 0:
                    ve.skip(chunk_done, 4)
                    qk_norm([4], False, 0)
                weigh(gates[:, 1, :])
                some_slots(True, h, 0, TURN_SLOTS, acc_second)
                plain_turns(True, 1, TURN_SLOTS)
                phase_end(True, h, acc_second)

            V.memset(zeros[:, :], 0.0).then_inc(zeros_set, ve.adds(zeros_set))
            V.memset(eps[:, 0:1], LN_EPS).then_inc(dve_step, ve.adds(dve_step))
            eng.wait_ge(dve_step, ve.now(dve_step))
            V.memset(eps[:, 1:2], RMS_EPS).then_inc(eps_set, ve.adds(eps_set))
            eng.sem_inc(row_used, AHEAD["row_used"])
            eng.sem_inc(hidden_done, AHEAD["hidden_done"])
            eng.wait_ge(vecs_in, 32)
            eng.wait_ge(consts_in, 16)
            raw = [vec(first, fc, "lb", l * n_first, 4) for l in range(L)]
            V.tensor_tensor(lbs[:, 24:28], raw[0], raw[1], ALU.max).then_inc(dve_step, ve.adds(dve_step))
            eng.wait_ge(dve_step, ve.now(dve_step))
            V.tensor_tensor(lbs[:, 0:4], raw[0], lbs[:, 24:28], ALU.subtract).then_inc(dve_step, ve.adds(dve_step))
            eng.wait_ge(dve_step, ve.now(dve_step))
            V.tensor_tensor(lbs[:, 4:8], raw[1], lbs[:, 24:28], ALU.subtract).then_inc(lb_max, ve.adds(lb_max))
            eng.wait_ge(lb_exp, ve.next(lb_exp))
            V.tensor_tensor(lbs[:, 16:20], lbs[:, 8:12], lbs[:, 12:16], ALU.add).then_inc(dve_step, ve.adds(dve_step))
            eng.wait_ge(dve_step, ve.now(dve_step))
            V.reciprocal(lbs[:, 20:24], lbs[:, 16:20]).then_inc(dve_step, ve.adds(dve_step))
            eng.wait_ge(dve_step, ve.now(dve_step))
            for l in range(L):
                V.tensor_tensor(
                    lbs[:, 4 * l:4 * l + 4], lbs[:, 8 + 4 * l:12 + 4 * l], lbs[:, 20:24], ALU.mult).then_inc(dve_step, ve.adds(dve_step))
            eng.wait_ge(dve_step, ve.now(dve_step))
            V.tensor_tensor(lbs[:, 8:12], lbs[:, 0:4], lbs[:, 4:8], ALU.add).then_inc(dve_step, ve.adds(dve_step))
            eng.wait_ge(dve_step, ve.now(dve_step))
            for l, upto in enumerate((lbs[:, 0:4], lbs[:, 8:12])):
                V.tensor_tensor(raw[l], upto, lbs[:, 0:4], ALU.subtract).then_inc(dve_step, ve.adds(dve_step))
            eng.wait_ge(dve_step, ve.now(dve_step))
            for l in range(L):
                V.tensor_scalar(
                    vec(first, fc, "omlb", l * n_first, 4), raw[l], -1.0, 1.0, ALU.mult, ALU.add).then_inc(dve_step, ve.adds(dve_step))
            eng.wait_ge(dve_step, ve.now(dve_step))

            modulation(0)
            rms(ctx_t)
            ve.skip(chunk_done, QKV_CHUNKS)
            qk_norm(range(5), False, 0)
            attention([0, 1], False)

            def project_out(x, l, who):
                gated_add(x, acc_t, l, 0, who, x_added, chunk_done)

            project_out(ctx_t, 0, 1)
            eng.wait_ge(x_added, ve.now(x_added))
            rms(ctx_t)
            ve.skip(chunk_done, PQ_CHUNKS)
            for b in range(NB):
                top_experts(0, b)
            for b in range(NB):
                gate_experts(b)
            modulation(1)

            eng.wait_ge(dve_step, ve.now(dve_step))
            eng.wait_ge(idx_done, ve.now(idx_done))
            V.memset(attn, 0.0).then_inc(dve_step, ve.adds(dve_step))
            V.memset(conv_u[:, :, 0:2], 0.0).then_inc(dve_step, ve.adds(dve_step))
            V.memset(pool_u[:, :, 0:16], 0.0).then_inc(dve_step, ve.adds(dve_step))
            for s in pool_s:
                V.memset(s, 0.0).then_inc(dve_step, ve.adds(dve_step))
            eng.wait_ge(masks_in, 16)
            eng.wait_ge(x_in, 16)
            eng.wait_ge(dve_step, ve.now(dve_step))

            def feed_forward(h, summing):
                at = SLOTS - FF_SLOTS if summing else 0

                def tile(ft):
                    eng.wait_ge(up_done, ve.next(up_done))
                    eng.wait_ge(silu_done, ve.next(silu_done))
                    eng.wait_ge(down_done, ve.next(down_done))
                    V.scalar_tensor_tensor(
                        hidden[:, ft % 2, :], ps_b[:, (ft % 2) * 512 + T:(ft % 2 + 1) * 512], 0.5, silu[:, ft % 2, :],
                        ALU.mult, ALU.mult).then_inc(hidden_done, ve.adds(hidden_done))

                tile(0)
                some_slots(summing, h, at, HEAD_SLOTS, acc_first)
                with ve.loop(FT_TURNS, up_done=FT_STEP, silu_done=FT_STEP, down_done=FT_STEP, hidden_done=FT_STEP,
                             **per_turn) as i:
                    turn_begin(summing, i, at + HEAD_SLOTS)
                    for q in range(FT_STEP):
                        tile(q + 1)
                        turn_slots(summing, h, q * FT_SLOTS, FT_SLOTS, acc_first)
                    turn_end(summing, i, at + HEAD_SLOTS)
                tile(FT - 1)
                if summing:
                    phase_end(summing, h, acc_first)
                eng.wait_ge(down_done, ve.now(down_done, -2))

            def layer_norm(wait=0):
                for j in range(4):
                    if wait == 2 or (wait and j == 0):
                        eng.wait_ge(chunk_done, ve.next(chunk_done, wait))
                    V.scalar_tensor_tensor(
                        resid[:, 2 * j:2 * j + 2, :], x_t[:, 2 * j:2 * j + 2, :], ALPHA, acc_t[:, 2 * j:2 * j + 2, :],
                        ALU.mult, ALU.add).then_inc(resid_done, ve.adds(resid_done))
                eng.wait_ge(mean_done, ve.next(mean_done))
                eng.wait_ge(resid_done, ve.now(resid_done))
                for j in range(4):
                    V.tensor_tensor(
                        resid[:, 2 * j:2 * j + 2, :], resid[:, 2 * j:2 * j + 2, :],
                        bcast(ps_c[:, 0:T].unsqueeze(1), 2, T), ALU.subtract).then_inc(centred_done, ve.adds(centred_done))
                eng.wait_ge(std_done, ve.next(std_done))
                V.reciprocal(std[:, :], std[:, :]).then_inc(dve_step, ve.adds(dve_step))
                eng.wait_ge(dve_step, ve.now(dve_step))
                eng.wait_ge(centred_done, ve.now(centred_done))
                for j in range(4):
                    V.tensor_tensor(
                        resid[:, 2 * j:2 * j + 2, :], resid[:, 2 * j:2 * j + 2, :],
                        bcast(std[:, :].unsqueeze(1), 2, T), ALU.mult).then_inc(scaled_done, ve.adds(scaled_done))

            all_slots = {f"rows_{s}": 32 * SLOTS // GR for s in range(GR)}
            with ve.loop(L, chunk_done=MIX_CHUNKS, up_done=2 * FT, silu_done=2 * FT, down_done=2 * FT, hidden_done=2 * FT,
                         resid_done=16, mean_done=4, centred_done=16, std_done=4, scaled_done=16, h_done=4 * KT,
                         z_done=24, f_done=1, log_done=1, decay_done=8, exp_done=8, qk_done=9, level_done=9,
                         level_taken=9, pooled_sums=1, o_std_done=1, conv_done=1, rec_done=1, cs_done=NB, cmax_done=NB, cexp_done=NB,
                         cprob_done=NB, row_used=2 * SLOTS, pout_done=1, dots_done=1, gelu_done=1, layer_vecs=1,
                         dve_step=DVE_STEPS, **all_slots) as l:
                eng.wait_ge(h_done, ve.now(h_done))
                V.tensor_copy(
                    cur[:, :], first[:, bass.ds(l * n_first, n_first)]).then_inc(layer_vecs, ve.adds(layer_vecs))
                h_ctx = h_tm[:, bass.ds(l, 1), :].rearrange("p a d -> p (a d)")
                feed_forward(h_ctx, False)
                layer_norm()
                some_slots(False, h_ctx, FF_SLOTS, EARLY_DOTS, acc_first)
                eng.wait_ge(row_used, ve.now(row_used))

                eng.wait_ge(z_done, ve.next(z_done, 2))
                eng.wait_ge(layer_vecs, ve.now(layer_vecs))
                for h in range(REC_H):
                    ins = V.tensor_scalar(z_f[:, h, :], z_f[:, h, :], vec(cur, fc, "omlb", h), vec(cur, fc, "lb", h),
                                          ALU.mult, ALU.add)
                    if h < REC_H - 1:
                        ins.then_inc(dve_step, ve.adds(dve_step))
                eng.wait_ge(dve_step, ve.now(dve_step))
                ins.then_inc(f_done, ve.adds(f_done))
                eng.wait_ge(log_done, ve.next(log_done))
                V.tensor_scalar(z_f, z_f, -1.0, 1.0, ALU.mult, ALU.add).then_inc(dve_step, ve.adds(dve_step))
                for h in range(REC_H):
                    V.tensor_tensor_scan(
                        csum[:, h, :], restart, dec[0][:, h, :], 0.0, ALU.mult, ALU.add).then_inc(dve_step, ve.adds(dve_step))
                eng.wait_ge(dve_step, ve.now(dve_step))

                def decays(i):
                    if i == 8:
                        d = dec[0].rearrange("p h (c s) -> p h c s", s=CHUNK)
                        b = csum.rearrange("p h (c s) -> p h c s", s=CHUNK)
                        end = [b[:, :, c, CHUNK - 1:CHUNK] for c in range(4)]
                        both = stats[:, 40:44].unsqueeze(2)
                        V.tensor_tensor(both, end[0], end[1], ALU.add).then_inc(dve_step, ve.adds(dve_step))
                        eng.wait_ge(dve_step, ve.now(dve_step))
                        full = (REC_H, CHUNK)
                        V.tensor_tensor(
                            d[:, :, 0, :], bcast(both, *full), b[:, :, 0, :], ALU.subtract).then_inc(dve_step, ve.adds(dve_step))
                        V.tensor_tensor(
                            d[:, :, 1, :], bcast(end[1], *full), b[:, :, 1, :], ALU.subtract).then_inc(dve_step, ve.adds(dve_step))
                        V.tensor_copy(d[:, :, 2, :], b[:, :, 2, :]).then_inc(dve_step, ve.adds(dve_step))
                        last = V.tensor_tensor(d[:, :, 3, :], b[:, :, 3, :], bcast(end[2], *full), ALU.add)
                    else:
                        m = 1 << (i - 1)
                        n = REC_H * T // (2 * m)
                        d = dec[i % 2].rearrange("p h t -> p (h t)").rearrange("p (n c s) -> p n c s", c=2, s=m)
                        b = csum.rearrange("p h t -> p (h t)").rearrange("p (n c s) -> p n c s", c=2, s=m)
                        mid = bcast(b[:, :, 0, m - 1:m], n, m)
                        V.tensor_tensor(
                            d[:, :, 0, :], mid, b[:, :, 0, :], ALU.subtract).then_inc(dve_step, ve.adds(dve_step))
                        if m == CHUNK:
                            last = V.tensor_copy(d[:, :, 1, :], b[:, :, 1, :])
                        else:
                            last = V.tensor_tensor(d[:, :, 1, :], b[:, :, 1, :], mid, ALU.subtract)
                    eng.wait_ge(dve_step, ve.now(dve_step))
                    last.then_inc(decay_done, ve.adds(decay_done))

                def take_level(i):
                    eng.wait_ge(level_done, ve.next(level_done))
                    eng.sem_inc(dve_pause, 1)
                    for b in range(NB if i < 8 else 1):
                        ps = view(ps_a, (i % 2) * 1024 + b * 512, REC_H, P)
                        if i == 8:
                            last = V.tensor_copy(attn[:, 2], ps)
                        else:
                            last = V.copy_predicated(attn[:, b], bcast(masks[:, i, :].unsqueeze(1), REC_H, P), ps)
                            if b == 0:
                                last.then_inc(dve_step, ve.adds(dve_step))
                    eng.wait_ge(dve_step, ve.now(dve_step))
                    last.then_inc(level_taken, ve.adds(level_taken))

                decays(1)
                eng.wait_ge(z_done, ve.next(z_done, 2))
                eng.wait_ge(dve_step, ve.now(dve_step))
                V.memset(
                    stats[:, 44:45], 0.0).then_inc(qk_done, ve.adds(qk_done))
                decays(2)
                for i in range(1, 9):
                    eng.wait_ge(exp_done, ve.next(exp_done))
                    if i >= 2:
                        take_level(i - 2)
                    V.tensor_tensor(qk[i % 2][0], z_q, dec[i % 2], ALU.mult).then_inc(dve_step, ve.adds(dve_step))
                    some_slots(False, h_ctx, FF_SLOTS + EARLY_DOTS + LEVEL_DOTS * (i - 1), LEVEL_DOTS, acc_levels)
                    ins = V.tensor_tensor(qk[i % 2][1], z_f, dec[i % 2], ALU.mult)
                    eng.wait_ge(dve_step, ve.now(dve_step))
                    ins.then_inc(qk_done, ve.adds(qk_done))
                    if i + 2 <= 8:
                        eng.wait_ge(qk_done, ve.now(qk_done))
                        decays(i + 2)
                take_level(7)
                take_level(8)
                eng.wait_ge(z_done, ve.next(z_done, 5))
                V.tensor_tensor(conv_u[:, :, 2:], z_c, z_h, ALU.mult).then_inc(dve_step, ve.adds(dve_step))
                eng.wait_ge(dve_step, ve.now(dve_step))
                for t in range(2):
                    V.tensor_scalar(
                        mix[:, t, :], conv_u[:, t, 0:T], vec(cur, fc, "conv_w", 3 * t), None, ALU.mult).then_inc(dve_step, ve.adds(dve_step))
                for j in range(1, 3):
                    eng.wait_ge(dve_step, ve.now(dve_step))
                    for t in range(2):
                        V.scalar_tensor_tensor(mix[:, t, :], conv_u[:, t, j:j + T], vec(cur, fc, "conv_w", 3 * t + j),
                                                    mix[:, t, :], ALU.mult, ALU.add).then_inc(dve_step, ve.adds(dve_step))
                eng.wait_ge(dve_step, ve.now(dve_step))
                V.tensor_tensor(mix[:, 0:2, :], mix[:, 0:2, :], z_b, ALU.mult).then_inc(conv_done, ve.adds(conv_done))
                eng.wait_ge(z_done, ve.next(z_done, 3))
                src, n = pool_u, 1
                for g, dst in enumerate((pool_s[0], pool_s[1], pool_s[0], pool_s[1])):
                    t, half = g // 2, slice(64 * (g % 2), 64 * (g % 2) + 64)
                    V.tensor_tensor(dst[:, :, 2 * n - 1:], src[:, :, 2 * n - 1:], src[:, :, n - 1:T + 16 - n],
                                    ALU.add).then_inc(dve_step, ve.adds(dve_step))
                    eng.wait_ge(dve_step, ve.now(dve_step))
                    V.tensor_tensor(pool_p[half, t, :], dst[half, t, 16:], rcount[half, t, :],
                                    ALU.mult).then_inc(dve_step, ve.adds(dve_step))
                    src, n = dst, 2 * n
                eng.wait_ge(dve_step, ve.now(dve_step))
                V.tensor_tensor(pool_p, pool_p, pool_u[:, :, 16:], ALU.subtract).then_inc(
                    pooled_sums, ve.adds(pooled_sums))
                eng.wait_ge(o_std_done, ve.next(o_std_done))
                r = dec[1]
                V.reciprocal(r, r).then_inc(dve_step, ve.adds(dve_step))
                eng.wait_ge(dve_step, ve.now(dve_step))
                V.tensor_tensor(dec[0], view(ps_a, 1024, REC_H, T), r, ALU.mult).then_inc(dve_step, ve.adds(dve_step))
                eng.wait_ge(dve_step, ve.now(dve_step))
                for h in range(REC_H):
                    ins = V.scalar_tensor_tensor(mix[:, 2 + h, :], dec[0][:, h, :], vec(cur, fc, "norm_g", h), z_g[:, h, :],
                                                 ALU.mult, ALU.mult)
                    if h < REC_H - 1:
                        ins.then_inc(dve_step, ve.adds(dve_step))
                eng.wait_ge(dve_step, ve.now(dve_step))
                ins.then_inc(rec_done, ve.adds(rec_done))
                eng.wait_ge(rec_done, ve.now(rec_done))
                some_slots(False, h_ctx, SLOTS - LATE_DOTS, LATE_DOTS, acc_first)
                phase_end(False, h_ctx, acc_first)
                weigh(gates[:, bass.ds(l, 1), :].rearrange("p a s -> p (a s)"))
                some_slots(True, h_ctx, 0, MIX_SUMS[0], acc_first)
                ve.skip(z_done, 12)
                ve.skip(chunk_done, 40)
                layer_norm(KT)
                some_slots(True, h_ctx, MIX_SUMS[0], MIX_SUMS[1], acc_first)
                ve.skip(chunk_done, KT)
                for b in range(NB):
                    eng.wait_ge(cs_done, ve.next(cs_done))
                    mx, neg = stats[:, 48 + 4 * b:52 + 4 * b], stats[:, 24 + 4 * b:28 + 4 * b]
                    V.tensor_reduce(
                        mx, view(ps_a, b * 1024, CA_H, T), AX, ALU.max).then_inc(dve_step, ve.adds(dve_step))
                    eng.wait_ge(dve_step, ve.now(dve_step))
                    V.tensor_scalar(neg, mx, -CA_SCALE, None, ALU.mult).then_inc(cmax_done, ve.adds(cmax_done))
                for b in range(NB):
                    eng.wait_ge(cexp_done, ve.next(cexp_done))
                    rs = stats[:, 32 + 4 * b:36 + 4 * b]
                    V.reciprocal(stats[:, 48 + 4 * b:52 + 4 * b], rs).then_inc(dve_step, ve.adds(dve_step))
                    eng.wait_ge(dve_step, ve.now(dve_step))
                    V.tensor_tensor(
                        ca_e[b], ca_e[b], bcast(stats[:, 48 + 4 * b:52 + 4 * b].unsqueeze(2), CA_H, T), ALU.mult).then_inc(cprob_done, ve.adds(cprob_done))
                some_slots(True, h_ctx, sum(MIX_SUMS[:2]), MIX_SUMS[2], acc_first)
                layer_norm(2)
                feed_forward(h_ctx, True)
                layer_norm()
                ve.skip(h_done, 4 * KT)

            eng.wait_ge(h_done, ve.now(h_done))
            for l in range(L):
                rms(x_t)
                if l == 0:
                    eng.wait_ge(po_tm_done, ve.next(po_tm_done))
                    gated_add(ctx_t, acc_t, 0, 1, 1, x_final)
                ve.skip(chunk_done, QKV_CHUNKS)
                qk_norm(range(5), True, T)
                attention([0, 1, 2, 3], l == 1)
                project_out(x_t, l, 0)
                eng.wait_ge(x_added, ve.now(x_added))
                rms(x_t)
                ve.skip(chunk_done, PQ_CHUNKS)
                top_experts(l, 0)
                first_block_peer(l)
                second_block_peer(l)
                eng.wait_ge(po_tm_done, ve.next(po_tm_done))
                gated_add(x_t, acc_t, l, 1, 0, x_final)
                eng.wait_ge(x_final, ve.now(x_final))


DVE_STEPS = 74


def shape_constants():
    t = np.arange(T)
    c = {"ident": np.eye(P), "mean_d": np.full((P, P), 1.0 / D)}
    rot = np.zeros((P, P))
    for d in range(P):
        if d // 32 % 2 == 0:
            rot[d + 32, d] = -1.0
        else:
            rot[d - 32, d] = 1.0
    c["rot"] = rot
    half = P // 2
    inv = np.float32(10000.0) ** (-np.arange(0, half, 2, dtype=np.float32) / np.float32(half))
    place = np.stack([t // 64, t % 64]).astype(np.float32)
    d = np.arange(P)
    angle = place[d // 64] * inv[d % 32][:, None].astype(np.float32)
    c["cos"], c["sin"] = np.cos(angle), np.sin(angle)
    count = np.stack([np.minimum(t + 1, w) for w in (2, 4, 8, 16)]).astype(np.float32)
    c["rcount"] = np.stack([(np.float32(1) / count)[2 * i + d // 64] for i in range(2)], 1).reshape(P, -1)
    c["restart"] = np.broadcast_to(t % CHUNK != 0, (P, T))
    q = np.arange(P)[:, None, None] + P * np.arange(NB)[None, :, None]
    window = np.where(np.abs(q - t[None, None, :]) <= 128, 0.0, NEG).astype(np.float32)
    c["iota"] = np.broadcast_to(np.arange(TOPK), (P, TOPK))
    s, u = np.arange(P)[:, None], np.arange(P)[None, :]
    masks = [s == u]
    for m in (1, 2, 4, 8, 16, 32, 64):
        masks.append((s // (2 * m) == u // (2 * m)) & (s // m % 2 == 0) & (u // m % 2 == 1))
    consts = np.concatenate([np.asarray(c[n], np.float32).reshape(P, -1) for n in CONSTS], 1)
    return consts, np.stack(masks, 1).astype(np.uint8).reshape(P, -1).view(np.uint32), window


def laid_out(x):
    def fm(v):
        return np.moveaxis(v.reshape(*v.shape[:-1], -1, P), -1, 0)

    def fm_chunks(w):
        return w.reshape(KT, P, -1, P).transpose(2, 1, 0, 3).reshape(-1, P, D)

    def tm_chunks(w):
        return w.reshape(2, 4, P, -1, T).transpose(3, 0, 2, 1, 4).reshape(-1, P, D)

    def ada_chunks(w):
        return w.reshape(4, 2, P, -1, 512).transpose(3, 0, 2, 1, 4).reshape(-1, P, D)

    def act(v):
        return v.T.reshape(KT, P, T).transpose(1, 0, 2)

    ffn, mixw, secw = [], [], []
    for l in range(L):
        for w in ("ffn1", "ffn2"):
            ffn.append(np.stack([fm_chunks(x[w + "_gate"][l]), fm_chunks(x[w + "_up"][l]),
                                 x[w + "_down"][l].reshape(FT, P, D)], 1))
        cb, cc, ch, rq, rf, ri, rg, pu = np.split(x["w_in"][l], np.cumsum([256, 256, 256, 512, 512, 512, 512]), axis=1)
        mixw += [fm_chunks(rf), fm_chunks(rq), tm_chunks(ri), fm_chunks(ch), fm_chunks(cc), fm_chunks(cb),
                 fm_chunks(pu), fm_chunks(rg), fm_chunks(x["ca_k"][l]), tm_chunks(x["ca_v"][l]),
                 fm_chunks(x["w_out"][l]), fm_chunks(x["ca_q"][l]), fm_chunks(x["ca_o"][l])]
        secw += [ada_chunks(x["ada_w_2"][l]), fm_chunks(x["w_qkv_2"][l][:, :1280]), tm_chunks(x["w_qkv_2"][l][:, 1280:]),
                 fm_chunks(x["w_o_2"][l]), fm_chunks(x["peer_w_q_2"][l])]
    vecs1 = []
    for l in range(L):
        blocks = np.zeros((P, 2, P), np.float32)
        for g in range(4):
            at = slice(64 * (g % 2), 64 * (g % 2) + 64)
            blocks[at, g // 2, at] = x["pool_w"][l, g]
        parts = dict(ln_g=fm(x["ln_g"][l]), ln_b=fm(x["ln_b"][l]), conv_w=fm(x["conv_w"][l]).transpose(0, 2, 1),
                     lb=fm(x["rec_lb"][l]), omlb=np.zeros((P, 4), np.float32), norm_g=fm(x["rec_norm_g"][l]),
                     pool_scale=fm(x["pool_scale"][l]), pool_w=blocks)
        vecs1 += [parts[n].reshape(P, -1) for n in FIRST]
    rows = lambda v: np.broadcast_to(v.reshape(1, -1), (P, v.size))
    parts = dict(ada_b=fm(x["ada_b_2"]), gain1=fm(x["norm1_gain_2"]), gain2=fm(x["norm2_gain_2"]),
                 q_gain=x["q_norm_gain_2"].T, k_gain=x["k_norm_gain_2"].T, sinks=rows(x["attn_sinks_2"][0]),
                 c=np.stack([fm(x["c_2"][0]), fm(x["c_ctx_2"])], 2))
    consts, masks, window = shape_constants()
    return dict(consts=consts, masks=masks, window=window, vecs1=np.concatenate(vecs1, 1),
                vecs2=np.concatenate([parts[n].reshape(P, -1) for n in SECOND], 1),
                x_t=act(x["x"][0]), mem_t=act(x["mem"][0]), ctx_t=act(x["ctx_2"][0]), ffn=np.concatenate(ffn),
                mix_w=np.concatenate(mixw), second_w=np.concatenate(secw),
                subk=x["peer_sub_keys_2"].transpose(3, 0, 1, 2),
                peer_u=x["peer_u_2"].reshape(-1, D), peer_v=x["peer_v_2"].reshape(-1, D))


def kernel(**inputs):
    import concourse.bacc as bacc
    from concourse.bass_utils import run_bass_kernel_spmd

    nc = bacc.Bacc("TRN2", target_bir_lowering=False, num_devices=1)
    arrays, args = {}, {}
    for name, v in laid_out({n: np.asarray(v) for n, v in inputs.items()}).items():
        v = np.ascontiguousarray(v)
        arrays[f"in_{name}"] = v
        args[name] = nc.dram_tensor(f"in_{name}", v.shape, mybir.dt.from_np(v.dtype), kind="ExternalInput").ap()
    out = nc.dram_tensor("out_x", (P, KT, T), F32, kind="ExternalOutput").ap()
    program(nc, args, out)
    r = run_bass_kernel_spmd(nc, [arrays], core_ids=[0])
    got = r.results[0]["out_x"]
    return np.ascontiguousarray(got.transpose(2, 1, 0).reshape(1, T, D))
```

```python
from contextlib import ExitStack, contextmanager

import numpy as np

import concourse.bass as bass
from concourse import mybir

F32 = mybir.dt.float32
BF16 = mybir.dt.bfloat16
U32 = mybir.dt.uint32
U8 = mybir.dt.uint8
ALU = mybir.AluOpType
ACT = mybir.ActivationFunctionType
AX = mybir.AxisListType.X

P = 128
D = 1024
KT = D // P
T = 256
NB = T // P
L = 2
FT = 2816 // P
ALPHA = (2.0 * L) ** 0.25
LN_EPS = 1e-5
RMS_EPS = 1e-6
CHUNK = 64
REC_H = 4
CA_H = 4
CA_SCALE = 256.0 ** -0.5
HEADS = 8
GROUPS = 2
REP = HEADS // GROUPS
SCALE = 128.0 ** -0.5
N_KEYS = 128
N_EXPERTS = N_KEYS * N_KEYS
PEER_H = 8
TOPK = 16
SLOTS = PEER_H * TOPK
LOWEST = -3.0e38
NEG = -1e30

WR = 4
MIX_CHUNKS = 64
ADA_CHUNKS, QKV_CHUNKS, WO_CHUNKS, PQ_CHUNKS = 48, 12, 8, 16
FIRST_ADA = ADA_CHUNKS // 2
SECOND_CHUNKS = QKV_CHUNKS + WO_CHUNKS + PQ_CHUNKS
PQ_AT = QKV_CHUNKS + WO_CHUNKS
LAYER_1 = FIRST_ADA + SECOND_CHUNKS
GR = 8
FT_STEP = 4
FT_TURNS = (FT - 2) // FT_STEP
TURN_SLOTS = 2 * GR
FT_SLOTS = TURN_SLOTS // FT_STEP
EARLY_TILES = 10
HEAD_SLOTS = GR
FF_SLOTS = HEAD_SLOTS + TURN_SLOTS * FT_TURNS
EARLY_DOTS = 8
LEVEL_DOTS = 3
LATE_DOTS = SLOTS - FF_SLOTS - EARLY_DOTS - 8 * LEVEL_DOTS
MIX_SUMS = 8, 16, 16
assert sum(MIX_SUMS) + FF_SLOTS == SLOTS

CONSTS = dict(ident=128, mean_d=128, rot=128, cos=256, sin=256, rcount=512, restart=256,
              iota=16)
FIRST = dict(ln_g=32, ln_b=32, conv_w=6, lb=4, omlb=4, norm_g=4, pool_scale=2, pool_w=256)
SECOND = dict(ada_b=L * 48, gain1=L * 8, gain2=L * 8, q_gain=L, k_gain=L, sinks=8, c=16)


def columns(parts):
    at, out = 0, {}
    for name, n in parts.items():
        out[name] = (at, n)
        at += n
    return out, at


AHEAD = dict(chunk_done=WR, gate_done=2, up_done=2, down_done=2, row_used=GR, h_done=1, z_done=1, hidden_done=1)


class Lane:

    def __init__(self, eng, refills=()):
        self.eng, self.refills, self.loops, self.count = eng, refills, [], {}

    def begin(self, name):
        return 0 if name in self.refills else AHEAD.get(name, 0)

    def now(self, sem, back=0):
        v = self.count.setdefault(sem.name, self.begin(sem.name)) - back
        for reg, per in self.loops:
            if per.get(sem.name):
                v = reg * per[sem.name] + v
        return v

    def skip(self, sem, by):
        self.count[sem.name] = self.count.get(sem.name, self.begin(sem.name)) + by

    def next(self, sem, by=1):
        self.skip(sem, by)
        return self.now(sem)

    def adds(self, sem, by=1):
        self.skip(sem, by)
        return by

    @contextmanager
    def loop(self, n, **per):
        begun = dict(self.count)
        with self.eng.Fori(0, n) as reg:
            self.loops.append((reg, per))
            yield reg
            self.loops.pop()
        for name, v in self.count.items():
            moved = v - begun.get(name, self.begin(name))
            assert moved == per.get(name, 0), (name, moved, per.get(name, 0))
            self.count[name] += (n - 1) * moved


def program(nc, a, out):
    with ExitStack() as ctx:
        def sems(names):
            return [ctx.enter_context(nc.semaphore(n)) for n in names.split()]

        (consts_in, window_in, vecs_in, masks_in, x_in, mem_in, ctx_in, subk_in) = sems(
            "consts_in window_in vecs_in masks_in x_in mem_in ctx_in subk_in")
        (chunk_done, gate_done, up_done, down_done) = sems(
            "chunk_done gate_done up_done down_done")
        (silu_done, hidden_done, resid_done, mean_done, centred_done, square_done, var_done, std_done,
         scaled_done, h_done) = sems(
            "silu_done hidden_done resid_done mean_done centred_done square_done var_done std_done "
            "scaled_done h_done")
        (layer_vecs, lb_max, lb_exp, eps_set, zeros_set) = sems(
            "layer_vecs lb_max lb_exp eps_set zeros_set")
        (z_done, f_done, log_done, decay_done, exp_done, qk_done, level_done, level_taken, o_done,
         o_square_done, o_ms_done, o_std_done) = sems(
            "z_done f_done log_done decay_done exp_done qk_done level_done level_taken o_done o_square_done "
            "o_ms_done o_std_done")
        (pooled_sums, pool_mm_done, pooled_done, conv_done, rec_done) = sems(
            "pooled_sums pool_mm_done pooled_done conv_done rec_done")
        (cs_done, cmax_done, cexp_done, cprob_done, cpt_done, cpt_taken, co_done, co_taken) = sems(
            "cs_done cmax_done cexp_done cprob_done cpt_done cpt_taken co_done co_taken")
        (c_silu, c_rows_in, c_rows_silu, ada_used, ada_taken, ada_done, mods_done) = sems(
            "c_silu c_rows_in c_rows_silu ada_used ada_taken ada_done mods_done")
        (sq2_done, ms2_done, std2_done, norm2_done, mod2_done) = sems(
            "sq2_done ms2_done std2_done norm2_done mod2_done")
        (qkv_taken, qk_sq_done, qk_ms_done, qk_std_done, rot_done, rot_taken, roped) = sems(
            "qkv_taken qk_sq_done qk_ms_done qk_std_done rot_done rot_taken roped")
        (s_done, s_max, sink_exp, s_exp, s_prob, pt_done, pt_taken, pv_done, pv_taken, x_added) = sems(
            "s_done s_max sink_exp s_exp s_prob pt_done pt_taken pv_done pv_taken x_added")
        (tm_done, tm_taken, pq_taken, sc_done, sc_taken, keys_used, top_ready, top_exp, idx_done) = sems(
            "tm_done tm_taken pq_taken sc_done sc_taken keys_used top_ready top_exp idx_done")
        (idx_now_done, row_used, dots_done, gelu_done, pout_done, po_tm_done, x_final) = sems(
            "idx_now_done row_used dots_done gelu_done pout_done po_tm_done x_final")
        (pool_pause, dve_pause, dve_step, stored) = sems(
            "pool_pause dve_pause dve_step stored")
        weights_in = sems(" ".join(f"weights_{s}" for s in range(WR)))
        rows_in = sems(" ".join(f"rows_{s}" for s in range(GR)))
        ff_in = [sems(f"{part}_in_0 {part}_in_1") for part in ("gate", "up", "down")]
        ada_in = sems(" ".join(f"ada_in_{s}" for s in range(GR)))
        ff_done = [gate_done, up_done, down_done]

        def sb(name, cols, dt=F32):
            return ctx.enter_context(nc.sbuf_tensor(name, [P, cols], dt))

        def view(tile, at, *dims):
            n = int(np.prod(dims))
            names = [f"d{i}" for i in range(len(dims))]
            if len(dims) == 1:
                return tile[:, at:at + n]
            return tile[:, at:at + n].rearrange(f"p ({' '.join(names)}) -> p {' '.join(names)}",
                                                **dict(zip(names[1:], dims[1:])))

        x_t = view(sb("x_t", KT * T), 0, KT, T)
        mem_tile = sb("mem_t", KT * T)
        mem_t = view(mem_tile, 0, KT, T)
        window = view(mem_tile, 0, NB, T)
        ctx_t = view(sb("ctx_t", KT * T), 0, KT, T)
        h_tm = view(sb("h_tm", NB * D), 0, NB, D)
        rows = view(sb("rows", GR * D), 0, GR, D)
        fw = view(sb("fw", 2 * 3 * D), 0, 2, 3, D)
        wring = view(sb("wring", WR * D), 0, WR, D)
        keys_t = view(sb("keys_t", GROUPS * 2 * T), 0, GROUPS, 2 * T)
        vals_tile = sb("vals", 4 * T)
        vals = view(vals_tile, 0, 4, GROUPS * P)
        cc, n_consts = columns(CONSTS)
        fc, n_first = columns(FIRST)
        sc_, n_second = columns(SECOND)
        consts = sb("consts", n_consts)
        masks_u32 = sb("masks", 8 * P // 4, U32)
        masks = masks_u32[:, :].bitcast(U8).rearrange("p (i t) -> p i t", t=P)
        first = sb("first", L * n_first)
        cur = sb("cur", n_first)
        second = sb("second", n_second)
        subk = view(sb("subk", L * 2 * N_KEYS), 0, L, 2, N_KEYS)
        mods = view(sb("mods", L * 48 * 2), 0, L, 48, 2)
        gains = view(sb("gains", L * 2 * 8 * 2), 0, L, 2, 8, 2)
        idx = view(sb("idx", NB * SLOTS, U32), 0, NB, SLOTS)
        idx_now = view(sb("idx_now", 2 * GR, U32), 0, 2, GR)
        gates = view(sb("gates", NB * SLOTS), 0, NB, SLOTS)
        dots = sb("dots", SLOTS)
        wts = sb("wts", SLOTS)
        stage = sb("stage", TURN_SLOTS)
        c_rows = fw[:, 0, 0:2, :]
        ada_unread = fw[:, 1, 0, :]
        ada_cols = view(dots, 0, FIRST_ADA, 2)
        zeros = sb("zeros", 512, BF16)
        iota_b = sb("iota_b", TOPK, BF16)
        eps = sb("eps", 2)
        cond = sb("cond", 2 * KT)
        std = sb("std", T)
        stats = sb("stats", 64)
        lbs = sb("lbs", 32)
        arena = sb("arena", 19044)

        def const(name, *dims):
            at, n = cc[name]
            return view(consts, at, *(dims or (n,)))

        ident, mean_d, rot = const("ident"), const("mean_d"), const("rot")
        cos, sin, restart, iota = const("cos"), const("sin"), const("restart"), const("iota")
        rcount = const("rcount", 2, T)

        def vec(tile, where, name, i=0, n=1):
            at = where[name][0] + i
            return tile[:, at:at + n]

        resid = view(arena, 0, KT, T)
        mix = view(arena, 0, KT, T)
        sq = view(arena, 2048, KT, T)
        z_f, z_q, z_g = (view(arena, 2048 + 1024 * i, REC_H, T) for i in range(3))
        z_h, z_c, z_b = (view(arena, 5120 + 512 * i, 2, T) for i in range(3))
        v_tm = view(arena, 6656, NB, 2, T)
        ca_q, ca_o = (view(arena, 2048 + 2048 * i, KT, T) for i in range(2))
        csum = view(arena, 7680, 4, T)
        dec = [view(arena, 8704 + 1024 * i, 4, T) for i in range(2)]
        ca_e = [view(arena, 1024 * i, CA_H, T) for i in range(2)]
        ca_pt = view(arena, 9728, NB, CA_H, P)
        qk = [[view(arena, 10752 + 2048 * i + 1024 * j, 4, T) for j in range(2)] for i in range(2)]
        ca_k = view(arena, 10752, KT, T)
        ca_v = view(arena, 12800, CA_H, NB, T)
        acc_levels = [view(arena, D * i, D) for i in range(2)]
        acc_first = [view(arena, 7680 + D * i, D) for i in range(2)]
        attn = view(arena, 14848, 3, REC_H, P)
        conv_u = view(arena, 16384, 2, T + 2)
        pool_u = view(arena, 16900, 2, T + 16)
        pool_s = [view(arena, 17444 + 544 * i, 2, T + 16) for i in range(2)]
        pool_p = view(arena, 18532, 2, T)
        silu = view(arena, 17444, 2, T)
        hidden = view(arena, 17956, 2, T)

        sq2 = view(arena, 0, KT, T)
        probs = [view(arena, at, REP, 2 * T) for at in (0, 13312)]
        over_sum = [view(arena, 15360 + 512 * i, REP, P) for i in range(2)]
        pscore = view(arena, 0, 2 * PEER_H, N_KEYS)
        h2 = view(arena, 2048, KT, T)
        top_i = arena[:, 10240:10368].bitcast(BF16).rearrange("p (j k) -> p j k", k=TOPK)
        place = [arena[:, 10368 + 64 * c:10432 + 64 * c].bitcast(BF16) for c in range(2)]
        top_sc = [view(arena, 10496 + 128 * b, PEER_H, TOPK) for b in range(NB)]
        sel = [view(arena, 10752 + 128 * i, SLOTS) for i in range(4)]
        pos_u = arena[:, 11520:11904].bitcast(U32)
        qk_raw = view(arena, 4096, 10, T)
        qk_n = view(arena, 6656, 10, T)
        qk_r = view(arena, 9216, 10, T)
        pt = view(arena, 9216, 4, REP * P)
        o_t = view(arena, 11264, HEADS, T)
        pq_t = view(arena, 4096, 16, T)
        cand = view(arena, 8192, PEER_H, TOPK * TOPK)
        top_v = view(arena, 12288, 2 * PEER_H, TOPK)
        top_iu = arena[:, 12544:12800].bitcast(U32).rearrange("p (j k) -> p j k", k=TOPK)
        cand2 = view(arena, 12800, PEER_H, TOPK * TOPK)
        onehot = [arena[:, at:at + D].bitcast(BF16).rearrange("p (h k a) -> p h k a", k=TOPK, a=TOPK)
                  for at in (8192, 12800)]
        pscore2 = view(arena, 14848, 2 * PEER_H, N_KEYS)
        acc_second = [view(arena, 16896 + D * i, D) for i in range(2)]
        list_now = [arena[:, 4096:5120], arena[:, 5120:6144], arena[:, 6144:6208],
                    arena[:, 6208:6272].bitcast(U32)]
        ada_row = view(arena, 16896, 2, 512)

        ps_a = ctx.enter_context(nc.psum_tensor("ps_a", [P, 2048], F32))
        ps_b = ctx.enter_context(nc.psum_tensor("ps_b", [P, 1024], F32))
        ps_c = ctx.enter_context(nc.psum_tensor("ps_c", [P, 512], F32))
        ps_d = ctx.enter_context(nc.psum_tensor("ps_d", [P, 512], F32))
        acc_t = view(ps_a, 0, KT, T)
        block = ctx.enter_context(nc.Block())

        @block.sync
        def _(eng):
            sp = Lane(eng, ("chunk_done", "gate_done", "up_done", "down_done"))
            eng.dma_start(second[:, :], a["vecs2"]).then_inc(vecs_in, 16)
            eng.dma_start(first[:, :], a["vecs1"]).then_inc(vecs_in, 16)
            eng.dma_start(consts[:, :], a["consts"]).then_inc(consts_in, 16)
            def chunk_loads(src, at, n):
                def load(s, row):
                    eng.wait_ge(chunk_done, sp.next(chunk_done))
                    eng.dma_start(wring[:, s, :], row).then_inc(weights_in[s], sp.adds(weights_in[s], 16))
                turns = n // WR
                per = {f"weights_{s}": 16 for s in range(WR)}
                if turns > 2:
                    with sp.loop(turns, chunk_done=WR, **per) as i:
                        for s in range(WR):
                            load(s, src[bass.ds(i * WR + (at + s), 1), :, :].rearrange("a p c -> (a p) c"))
                else:
                    for j in range(n):
                        load(j % WR, src[bass.ds(at + j, 1), :, :].rearrange("a p c -> (a p) c"))

            def ff_loads(tile, ft, part):
                eng.wait_ge(ff_done[part], sp.next(ff_done[part]))
                eng.dma_start(
                    fw[:, ft % 2, part, :],
                    a["ffn"][bass.ds(tile, 1), part, :, :].rearrange("a p c -> (a p) c")).then_inc(
                    ff_in[part][ft % 2], sp.adds(ff_in[part][ft % 2], 16))

            chunk_loads(a["second_w"], 0, FIRST_ADA)
            eng.dma_start(ctx_t, a["ctx_t"]).then_inc(ctx_in, 16)
            eng.dma_start(subk, a["subk"]).then_inc(subk_in, 16)
            chunk_loads(a["second_w"], FIRST_ADA, SECOND_CHUNKS)
            eng.dma_start(masks_u32[:, :], a["masks"]).then_inc(masks_in, 16)
            eng.dma_start(x_t, a["x_t"]).then_inc(x_in, 16)
            eng.dma_start(mem_t, a["mem_t"]).then_inc(mem_in, 16)
            chunk_loads(a["second_w"], FIRST_ADA + PQ_AT, PQ_CHUNKS)
            chunk_loads(a["second_w"], LAYER_1, ADA_CHUNKS)
            eng.wait_ge(mods_done, 2)
            ff_per = {f"{n}_in_{s}": 16 for n in ("gate", "up", "down") for s in range(2)}
            ff_turn = {k: 16 * FT_STEP // 2 for k in ff_per} | dict(gate_done=FT_STEP, up_done=FT_STEP,
                                                                    down_done=FT_STEP)
            ff_layer = {k: 16 * FT for k in ff_per} | dict(gate_done=2 * FT, up_done=2 * FT, down_done=2 * FT)
            with sp.loop(L, chunk_done=MIX_CHUNKS, **{f"weights_{s}": 16 * MIX_CHUNKS // WR for s in range(WR)},
                         **ff_layer) as l:
                for w in range(2):
                    for ft in range(2):
                        for part in range(3):
                            ff_loads(l * (2 * FT) + (w * FT + ft), ft, part)
                    if w == 0:
                        chunk_loads(a["mix_w"], l * MIX_CHUNKS, WR)
                    else:
                        chunk_loads(a["mix_w"], l * MIX_CHUNKS + (MIX_CHUNKS - WR), WR)
                    with sp.loop(FT_TURNS, **ff_turn) as i:
                        for ft in range(FT_STEP):
                            for part in range(3):
                                ff_loads(l * (2 * FT) + (w * FT + 2 + ft) + i * FT_STEP, ft, part)
                    if w == 0:
                        chunk_loads(a["mix_w"], l * MIX_CHUNKS + WR, MIX_CHUNKS - 2 * WR)
            chunk_loads(a["second_w"], FIRST_ADA, SECOND_CHUNKS)
            chunk_loads(a["second_w"], FIRST_ADA + PQ_AT, PQ_CHUNKS)
            chunk_loads(a["second_w"], LAYER_1 + ADA_CHUNKS + 8, 4)
            eng.wait_ge(chunk_done, sp.now(chunk_done))
            eng.dma_start(window, a["window"]).then_inc(window_in, 16)
            chunk_loads(a["second_w"], LAYER_1 + ADA_CHUNKS, SECOND_CHUNKS)
            chunk_loads(a["second_w"], LAYER_1 + ADA_CHUNKS + PQ_AT, PQ_CHUNKS)
            eng.wait_ge(x_final, sp.next(x_final, 3 * KT))
            eng.dma_start(out, x_t).then_inc(stored, 16)
            eng.wait_ge(stored, 16)

        @block.gpsimd
        def _(eng):
            po = Lane(eng, ("row_used",))
            G = nc.gpsimd

            def pause():
                eng.sem_inc(pool_pause, 1)

            def gather(table, where, at=0, n=SLOTS):
                per = {f"rows_{s}": 32 for s in range(GR)}
                with po.loop(n // (2 * GR), row_used=2 * GR, idx_now_done=2, **per) as i:
                    for half in range(2):
                        eng.wait_ge(row_used, po.now(row_used, -1))
                        G.tensor_copy(
                            idx_now[:, half, :], where[:, bass.ds(i * (2 * GR) + (at + half * GR), GR)]).then_inc(
                                idx_now_done, po.adds(idx_now_done))
                        eng.wait_ge(idx_now_done, po.now(idx_now_done))
                        for s in range(GR):
                            eng.wait_ge(row_used, po.next(row_used))
                            pause()
                            G.indirect_dma_start(
                                rows[:, s, :], None, table,
                                bass.IndirectOffsetOnAxis(ap=idx_now[:, half, s:s + 1], axis=0)).then_inc(
                                    rows_in[s], po.adds(rows_in[s], 16))

            eng.dma_start(c_rows, a["c_rows"]).then_inc(c_rows_in, 16)
            for j in range(FIRST_ADA):
                if j >= GR:
                    eng.wait_ge(ada_used, j - GR + 1)
                eng.dma_start(rows[:, j % GR, :], a["ada_rows"][j]).then_inc(ada_in[j % GR], 16)
            eng.wait_ge(ada_used, FIRST_ADA)
            pause()

            slots = dict(row_used=2 * SLOTS, idx_now_done=4 * SLOTS // (2 * GR),
                         **{f"rows_{s}": 64 * SLOTS // (2 * GR) for s in range(GR)})
            with po.loop(L, idx_done=1, **slots) as l:
                eng.wait_ge(idx_done, po.next(idx_done))
                pause()
                where = idx[:, bass.ds(l, 1), :].rearrange("p a s -> p (a s)")
                gather(a["peer_u"], where)
                gather(a["peer_v"], where)
            with po.loop(L, idx_done=3, **{k: 2 * v for k, v in slots.items()}):
                for half in range(2):
                    eng.wait_ge(idx_done, po.next(idx_done))
                    pause()
                    gather(a["peer_u"], idx[:, 0, :], half * (SLOTS // 2), SLOTS // 2)
                gather(a["peer_v"], idx[:, 0, :])
                eng.wait_ge(idx_done, po.next(idx_done))
                pause()
                gather(a["peer_u"], idx[:, 1, :])
                gather(a["peer_v"], idx[:, 1, :])

        @block.tensor
        def _(eng):
            pe = Lane(eng)
            mm = nc.tensor.matmul

            def chunk(s):
                eng.wait_ge(weights_in[s], pe.next(weights_in[s], 16))
                return wring[:, s, :]

            def acc_groups(src, act_ready=None):
                for j in range(KT):
                    w = chunk(j % WR)
                    for k in range(KT):
                        if j == 0 and act_ready:
                            act_ready(k)
                        ins = mm(acc_t[:, j, :], w[:, k * P:(k + 1) * P], src[:, k, :], start=k == 0, stop=k == KT - 1)
                    ins.then_inc(chunk_done, pe.adds(chunk_done))

            def fm_group(c, bank, src, act_ready=None):
                for t in range(2):
                    w = chunk((c + t) % WR)
                    for k in range(KT):
                        if t == 0 and act_ready:
                            act_ready(k)
                        ins = mm(bank[:, t * T:(t + 1) * T], w[:, k * P:(k + 1) * P], src[:, k, :],
                                 start=k == 0, stop=k == KT - 1)
                    ins.then_inc(chunk_done, pe.adds(chunk_done))

            def tm_group(c, bank, src):
                w = [chunk((c + t) % WR) for t in range(2)]
                for b in range(NB):
                    for k in range(KT):
                        ins = mm(bank[:, b * T:(b + 1) * T], src[:, k, b * P:(b + 1) * P],
                                 w[k // 4][:, (k % 4) * T:(k % 4 + 1) * T], start=k == 0, stop=k == KT - 1)
                        if b == NB - 1 and k in (3, 7):
                            ins.then_inc(chunk_done, pe.adds(chunk_done))

            def mean_of(src, bank, weights, ready, n_ready):
                for k in range(KT):
                    if k % (KT // n_ready) == 0:
                        eng.wait_ge(ready, pe.next(ready))
                    ins = mm(bank, weights, src[:, k, :], start=k == 0, stop=k == KT - 1)
                return ins

            def ada(n):
                per = {f"weights_{s}": 32 for s in range(WR)}
                with pe.loop(n // (2 * WR), chunk_done=2 * WR, ada_taken=2, ada_done=1, **per) as i:
                    for half in range(2):
                        for s in range(WR):
                            w = chunk(s)
                            for k in range(2):
                                ins = mm(ps_b[0:2, half * 512:(half + 1) * 512], cond[:, 4 * s + 2 * k:4 * s + 2 * k + 2],
                                         w[:, k * 512:(k + 1) * 512], start=s + k == 0, stop=(s, k) == (WR - 1, 1))
                            ins.then_inc(chunk_done, pe.adds(chunk_done))
                    for half in range(2):
                        eng.wait_ge(ada_taken, pe.next(ada_taken))
                        for q in range(4):
                            ins = mm(ps_d[:, bass.ds(i * 16 + half * 8 + 2 * q, 2)], ada_row[0:2, half, q * P:(q + 1) * P],
                                     ident[0:2, 0:2], start=True, stop=True)
                    ins.then_inc(ada_done, pe.adds(ada_done))

            def rms():
                mean_of(sq2, ps_c[:, 0:T], mean_d, sq2_done, 4).then_inc(ms2_done, pe.adds(ms2_done))

            def mod_ready(k):
                eng.wait_ge(mod2_done, pe.next(mod2_done))

            def qkv(groups, rope):
                def stats(n, g):
                    eng.wait_ge(qk_sq_done, pe.next(qk_sq_done))
                    if n >= 2:
                        eng.wait_ge(qk_std_done, pe.next(qk_std_done))
                    mm(ps_a[:, (g % 2) * 512:(g % 2 + 1) * 512], mean_d, view(arena, 9216 + 512 * g, 512),
                       start=True, stop=True).then_inc(qk_ms_done, pe.adds(qk_ms_done))
                    eng.wait_ge(qkv_taken, pe.next(qkv_taken))
                    if rope:
                        if n >= 2:
                            eng.wait_ge(rot_taken, pe.next(rot_taken))
                        mm(ps_a[:, 1024 + (g % 2) * 512:1024 + (g % 2 + 1) * 512], rot, view(arena, 4096 + 512 * g, 512),
                           start=True, stop=True).then_inc(rot_done, pe.adds(rot_done))

                for n, g in enumerate(groups):
                    fm_group(2 * g, ps_b[:, (g % 2) * 512:(g % 2 + 1) * 512], h2, None if n else mod_ready)
                    if n:
                        stats(n - 1, groups[n - 1])
                tm_group(2, ps_b[:, 512:1024], h2)
                stats(len(groups) - 1, groups[-1])
                eng.wait_ge(qkv_taken, pe.next(qkv_taken))
                pe.skip(qk_std_done, min(len(groups), 2))
                pe.skip(rot_taken, 2 if rope else 0)

            def attention(blocks, windowed):
                n, units = len(blocks) * P, NB * GROUPS
                eng.wait_ge(roped, pe.next(roped))

                def unit_scores(u):
                    b, g = u // GROUPS, u % GROUPS
                    if u:
                        eng.wait_ge(s_exp, pe.next(s_exp))
                    for r in range(REP):
                        q = qk_n[:, REP * g + r, b * P:(b + 1) * P]
                        if windowed:
                            mm(ps_a[:, r * 512:r * 512 + T], q, keys_t[:, g, 0:T], start=True, stop=True)
                            mm(ps_a[:, r * 512 + T:r * 512 + 2 * T], q, keys_t[:, g, T:2 * T], start=True, stop=False)
                            ins = mm(ps_a[:, r * 512 + T:r * 512 + 2 * T], ident, window[:, b, :], start=False, stop=True)
                        else:
                            ins = mm(ps_a[:, r * 512:r * 512 + n], q, keys_t[:, g, 0:n], start=True, stop=True)
                    ins.then_inc(s_done, pe.adds(s_done))

                unit_scores(0)
                for u in range(units):
                    if u + 1 < units:
                        unit_scores(u + 1)
                    eng.wait_ge(s_prob, pe.next(s_prob))
                    for j in blocks:
                        if u or j >= 2:
                            eng.wait_ge(pt_taken, pe.next(pt_taken))
                        for r in range(REP):
                            ins = mm((ps_c, ps_d)[j % 2][:, r * P:(r + 1) * P], probs[u % 2][:, r, j * P:(j + 1) * P],
                                     over_sum[u % 2][:, r, :], start=True, stop=True)
                        ins.then_inc(pt_done, pe.adds(pt_done))
                    eng.wait_ge(pt_taken, pe.now(pt_taken, -2))
                    if u >= 2:
                        eng.wait_ge(pv_taken, pe.next(pv_taken))
                    for j in blocks:
                        ins = mm(ps_b[:, (u % 2) * 512:(u % 2 + 1) * 512],
                                 vals[:, j, u % GROUPS * P:(u % GROUPS + 1) * P], pt[:, j, :],
                                 start=j == blocks[0], stop=j == blocks[-1])
                    ins.then_inc(pv_done, pe.adds(pv_done))
                pe.skip(pt_taken, 2)
                eng.wait_ge(s_exp, pe.next(s_exp))
                eng.wait_ge(pv_taken, pe.next(pv_taken, 2))

            def project_out():
                acc_groups(o_t)

            def peer_scores(l):
                rms()
                for k in range(KT):
                    eng.wait_ge(mod2_done, pe.next(mod2_done))
                for b in range(NB):
                    for g in range(PQ_CHUNKS // WR):
                        if b and g == 2:
                            eng.wait_ge(sc_taken, pe.next(sc_taken))
                            for c in range(NB):
                                for k in range(KT):
                                    ins = nc.tensor.transpose(ps_a[:, c * D + k * P:c * D + (k + 1) * P],
                                                              h2[:, k, c * P:(c + 1) * P], ident)
                            ins.then_inc(tm_done, pe.adds(tm_done))
                        if g >= 2:
                            eng.wait_ge(pq_taken, pe.next(pq_taken))
                        for t in range(WR):
                            w = chunk(t)
                            for k in range(KT):
                                ins = mm(ps_b[:, (g % 2) * 512 + t * P:(g % 2) * 512 + (t + 1) * P],
                                         w[:, k * P:(k + 1) * P], h2[:, k, b * P:(b + 1) * P],
                                         start=k == 0, stop=k == KT - 1)
                            ins.then_inc(chunk_done, pe.adds(chunk_done))
                    eng.wait_ge(pq_taken, pe.next(pq_taken, 2))
                    if b:
                        eng.wait_ge(tm_taken, pe.next(tm_taken))
                    for j in range(2 * PEER_H):
                        ins = mm(ps_a[:, j * N_KEYS:(j + 1) * N_KEYS], pq_t[:, j, b * P:(b + 1) * P],
                                 subk[:, l, j % 2, :], start=True, stop=True)
                    ins.then_inc(sc_done, pe.adds(sc_done))
                eng.wait_ge(sc_taken, pe.next(sc_taken))

            def finish():
                eng.wait_ge(pout_done, pe.next(pout_done, NB))
                for k in range(KT):
                    for b in range(NB):
                        ins = nc.tensor.transpose(acc_t[:, k, b * P:(b + 1) * P], h_tm[:, b, k * P:(k + 1) * P], ident)
                ins.then_inc(po_tm_done, pe.adds(po_tm_done))

            eng.sem_inc(chunk_done, AHEAD["chunk_done"])
            eng.sem_inc(gate_done, AHEAD["gate_done"])
            eng.sem_inc(up_done, AHEAD["up_done"])
            eng.sem_inc(down_done, AHEAD["down_done"])
            eng.wait_ge(consts_in, 16)
            eng.wait_ge(c_silu, pe.next(c_silu))
            ada(FIRST_ADA)
            rms()
            qkv([0, 1, 2, 3, 4], False)
            attention([0, 1], False)
            project_out()
            eng.wait_ge(subk_in, 16)
            peer_scores(0)
            ada(ADA_CHUNKS)

            eng.wait_ge(x_in, 16)
            eng.wait_ge(mem_in, 16)
            eng.wait_ge(zeros_set, 1)

            def feed_forward(h_ready):
                for j in range(4):
                    mm(ps_a[:, j * 512:(j + 1) * 512], zeros[:, 0:P], zeros[:, :], start=True, stop=False,
                       skip_group_check=True)

                def gate_up(ft, first=False):
                    bank = ps_b[:, (ft % 2) * 512:(ft % 2 + 1) * 512]
                    for part in range(2):
                        eng.wait_ge(ff_in[part][ft % 2], pe.next(ff_in[part][ft % 2], 16))
                        for k in range(KT):
                            if first and part == 0:
                                h_ready(k)
                            ins = mm(bank[:, part * T:(part + 1) * T], fw[:, ft % 2, part, k * P:(k + 1) * P],
                                     x_t[:, k, :], start=k == 0, stop=k == KT - 1)
                        ins.then_inc(ff_done[part], pe.adds(ff_done[part]))

                def down(ft, last=False):
                    eng.wait_ge(hidden_done, pe.next(hidden_done))
                    eng.wait_ge(ff_in[2][ft % 2], pe.next(ff_in[2][ft % 2], 16))
                    for j in range(KT):
                        ins = mm(acc_t[:, j, :], fw[:, ft % 2, 2, j * P:(j + 1) * P], hidden[:, ft % 2, :],
                                 start=False, stop=last, skip_group_check=True)
                        if j == KT - 1:
                            ins.then_inc(down_done, pe.adds(down_done))

                gate_up(0, True)
                per = {f"{n}_in_{s}": 16 * FT_STEP // 2 for n in ("gate", "up", "down") for s in range(2)}
                with pe.loop(FT_TURNS, hidden_done=FT_STEP, gate_done=FT_STEP, up_done=FT_STEP, down_done=FT_STEP,
                             **per):
                    for q in range(FT_STEP):
                        gate_up(q + 1)
                        down(q)
                gate_up(FT - 1)
                down(FT - 2)
                down(FT - 1, True)

            def layer_norm():
                mean_of(resid, ps_c[:, 0:T], mean_d, resid_done, 4).then_inc(mean_done, pe.adds(mean_done))
                mean_of(sq, ps_d[:, 0:T], mean_d, square_done, 4).then_inc(var_done, pe.adds(var_done))

            def h_take(k):
                eng.wait_ge(h_done, pe.next(h_done))

            def h_have(k):
                if k == 0:
                    eng.wait_ge(h_done, pe.now(h_done))

            ff = {f"{n}_in_{s}": 16 * FT for n in ("gate", "up", "down") for s in range(2)}
            with pe.loop(L, chunk_done=MIX_CHUNKS, **{f"weights_{s}": 16 * MIX_CHUNKS // WR for s in range(WR)},
                         hidden_done=2 * FT, gate_done=2 * FT, up_done=2 * FT, down_done=2 * FT, **ff,
                         h_done=4 * KT, resid_done=16, square_done=16, mean_done=4, var_done=4, z_done=24,
                         qk_done=9, level_done=9, level_taken=9, o_done=1, o_square_done=2, o_ms_done=1,
                         pooled_sums=1, pool_mm_done=1, pooled_done=1, conv_done=1, rec_done=1, cs_done=NB,
                         cprob_done=NB, cpt_done=2 * NB, cpt_taken=2 * NB, co_done=NB, co_taken=NB) as l:
                feed_forward(h_have)
                layer_norm()

                def group(g, c, src, ready=None, tm=False):
                    if g:
                        eng.wait_ge(z_done, pe.now(z_done, 1))
                    bank = ps_b[:, (g % 2) * 512:(g % 2 + 1) * 512]
                    if tm:
                        tm_group(c, bank, src)
                    else:
                        fm_group(c, bank, src, ready)
                    pe.skip(z_done, 1)

                def level(i):
                    eng.wait_ge(qk_done, pe.next(qk_done))
                    if i >= 2:
                        eng.wait_ge(level_taken, pe.next(level_taken))
                    q, k = (z_q, z_f) if i == 0 else qk[i % 2]
                    for b in range(NB if i < 8 else 1):
                        for h in range(REC_H):
                            ks = slice(b * P, (b + 1) * P)
                            qs = ks if i < 8 else slice(P, 2 * P)
                            ins = mm(ps_a[:, (i % 2) * 1024 + b * 512 + h * P:(i % 2) * 1024 + b * 512 + (h + 1) * P],
                                     k[:, h, ks], q[:, h, qs], start=True, stop=True)
                    ins.then_inc(level_done, pe.adds(level_done))

                for g in range(4):
                    group(g, 2 * g, x_t, h_take if g == 0 else None)
                for g in range(4, 12):
                    group(g, 2 * g, x_t, tm=g < 6)
                    level(g - 4)
                level(8)
                eng.wait_ge(level_taken, pe.next(level_taken, 2))
                eng.wait_ge(z_done, pe.now(z_done, 0))
                for h in range(REC_H):
                    o = ps_a[:, 1024 + h * T:1024 + (h + 1) * T]
                    vs = [v_tm[:, h // 2, b, (h % 2) * P:(h % 2 + 1) * P] for b in range(NB)]
                    mm(o[:, 0:P], vs[0], attn[:, 0, h, :], start=True, stop=True)
                    mm(o[:, P:T], vs[0], attn[:, 2, h, :], start=True, stop=False)
                    ins = mm(o[:, P:T], vs[1], attn[:, 1, h, :], start=False, stop=True)
                ins.then_inc(o_done, pe.adds(o_done))
                group(12, 24, mem_t)
                for j in range(2):
                    eng.wait_ge(o_square_done, pe.next(o_square_done))
                    ins = mm(ps_a[:, j * 512:(j + 1) * 512], mean_d, view(arena, 8704 + 512 * j, 512),
                             start=True, stop=True)
                ins.then_inc(o_ms_done, pe.adds(o_ms_done))
                for g in range(13, 20):
                    group(g, 2 * g, mem_t, tm=g >= 16)
                eng.wait_ge(pooled_sums, pe.next(pooled_sums))
                eng.wait_ge(mods_done, 2 * L)
                for t in range(2):
                    at = fc["pool_w"][0] + t * P
                    ins = mm(ps_d[:, t * T:(t + 1) * T], cur[:, at:at + P], pool_p[:, t, :], start=True, stop=True)
                ins.then_inc(pool_mm_done, pe.adds(pool_mm_done))
                for part_done in (pooled_done, conv_done, rec_done):
                    eng.wait_ge(part_done, pe.next(part_done))
                acc_groups(mix)
                layer_norm()
                for g in range(20, 24):
                    group(g, 2 * g, x_t, h_take if g == 20 else None)
                eng.wait_ge(z_done, pe.now(z_done, 0))
                def ca_scores(b):
                    for h in range(CA_H):
                        for c in range(2):
                            ins = mm(ps_a[:, b * 1024 + h * T:b * 1024 + (h + 1) * T],
                                     ca_q[:, 2 * h + c, b * P:(b + 1) * P], ca_k[:, 2 * h + c, :],
                                     start=c == 0, stop=c == 1)
                    ins.then_inc(cs_done, pe.adds(cs_done))
                ca_scores(0)
                ca_scores(1)
                for b in range(NB):
                    eng.wait_ge(cprob_done, pe.next(cprob_done))
                    for m in range(NB):
                        for h in range(CA_H):
                            ins = nc.tensor.transpose((ps_c, ps_d)[m][:, h * P:(h + 1) * P],
                                                      ca_e[b][:, h, m * P:(m + 1) * P], ident)
                        ins.then_inc(cpt_done, pe.adds(cpt_done))
                    eng.wait_ge(cpt_taken, pe.next(cpt_taken, 2))
                    if b:
                        eng.wait_ge(co_taken, pe.next(co_taken))
                    for h in range(CA_H):
                        for c in range(2):
                            for m in range(NB):
                                ins = mm(ps_b[:, (2 * h + c) * P:(2 * h + c + 1) * P],
                                         ca_v[:, h, m, c * P:(c + 1) * P], ca_pt[:, m, h, :],
                                         start=m == 0, stop=m == 1)
                    ins.then_inc(co_done, pe.adds(co_done))
                eng.wait_ge(co_taken, pe.next(co_taken))
                acc_groups(ca_o)
                layer_norm()
                feed_forward(h_take)
                layer_norm()
                pe.skip(h_done, KT)

            for l in range(L):
                rms()
                if l == 0:
                    finish()
                    eng.wait_ge(x_final, pe.next(x_final, KT))
                qkv([0, 1, 2, 3, 4], True)
                if l == 1:
                    eng.wait_ge(window_in, 16)
                attention([0, 1, 2, 3], l == 1)
                project_out()
                peer_scores(l)
                if l == 0:
                    rms()
                    qkv([4], False)
                    eng.wait_ge(roped, pe.next(roped))
                finish()

        @block.scalar
        def _(eng):
            ac = Lane(eng)

            def act(out, in_, func, **k):
                return nc.scalar.activation(out, in_, func, **k)

            def rms(src, l, part, who, ready=None):
                for j in range(4):
                    if ready is not None:
                        eng.wait_ge(ready, ac.next(ready, 2))
                    act(
                        sq2[:, 2 * j:2 * j + 2, :], src[:, 2 * j:2 * j + 2, :], ACT.Square).then_inc(
                            sq2_done, ac.adds(sq2_done))
                eng.wait_ge(ms2_done, ac.next(ms2_done))
                act(std[:, :], ps_c[:, 0:T], ACT.Sqrt, bias=eps[:, 1:2]).then_inc(std2_done, ac.adds(std2_done))
                for k in range(KT):
                    if k % 2 == 0:
                        eng.wait_ge(norm2_done, ac.next(norm2_done))
                    act(h2[:, k, :], h2[:, k, :], ACT.Identity, scale=gains[:, l, part, k, who:who + 1],
                                            bias=mods[:, l, 24 * part + k, who:who + 1]).then_inc(
                                                mod2_done, ac.adds(mod2_done))

            def qkv(l, groups, first_block):
                def deviation(g):
                    eng.wait_ge(qk_ms_done, ac.next(qk_ms_done))
                    act(view(arena, 9216 + 512 * g, 512), ps_a[:, (g % 2) * 512:(g % 2 + 1) * 512], ACT.Sqrt,
                        scale=D / P, bias=eps[:, 1:2]).then_inc(qk_std_done, ac.adds(qk_std_done))

                for n, g in enumerate(groups):
                    bank = ps_b[:, (g % 2) * 512:(g % 2 + 1) * 512]
                    gain = second[:, sc_["q_gain" if g < 4 else "k_gain"][0] + l:][:, 0:1]
                    eng.wait_ge(chunk_done, ac.next(chunk_done, 2))
                    act(view(arena, 9216 + 512 * g, 512), bank, ACT.Square).then_inc(qk_sq_done, ac.adds(qk_sq_done))
                    act(view(arena, 4096 + 512 * g, 512), bank, ACT.Copy, scale=gain).then_inc(
                        qkv_taken, ac.adds(qkv_taken))
                    if n:
                        deviation(groups[n - 1])
                eng.wait_ge(chunk_done, ac.next(chunk_done, 2))
                act(view(vals_tile, first_block * T, 512), ps_b[:, 512:1024], ACT.Copy).then_inc(
                    qkv_taken, ac.adds(qkv_taken))
                deviation(groups[-1])

            def attention(blocks, sink):
                n, units = len(blocks) * P, NB * GROUPS

                def exps(u):
                    eng.wait_ge(s_max, ac.next(s_max))
                    if sink:
                        act(stats[:, 16:20], stats[:, 12:16], ACT.Exp).then_inc(sink_exp, ac.adds(sink_exp))
                    for r in range(REP):
                        ins = act(probs[u % 2][:, r, 0:n], ps_a[:, r * 512:r * 512 + n], ACT.Exp, scale=SCALE,
                                  bias=stats[:, 4 + r:5 + r], accum_out=stats[:, 8 + r:9 + r])
                    ins.then_inc(s_exp, ac.adds(s_exp))

                exps(0)
                for u in range(units):
                    b, g = u // GROUPS, u % GROUPS
                    if u:
                        eng.wait_ge(pv_done, ac.now(pv_done))
                    for j in blocks:
                        eng.wait_ge(pt_done, ac.next(pt_done))
                        act(pt[:, j, :], (ps_c, ps_d)[j % 2][:, :], ACT.Copy).then_inc(pt_taken, ac.adds(pt_taken))
                    if u + 1 < units:
                        exps(u + 1)
                    eng.wait_ge(pv_done, ac.next(pv_done))
                    act(o_t[:, REP * g:REP * (g + 1), b * P:(b + 1) * P],
                        ps_b[:, (u % 2) * 512:(u % 2 + 1) * 512].rearrange("p (r t) -> p r t", t=P),
                        ACT.Copy).then_inc(pv_taken, ac.adds(pv_taken))

            def peer_scores(src, l, who):
                ac.skip(chunk_done, WO_CHUNKS)
                rms(src, l, 1, who, x_added)
                for b in range(NB):
                    for g in range(PQ_CHUNKS // WR):
                        if b and g == 2:
                            eng.wait_ge(tm_done, ac.next(tm_done))
                            for j in range(4):
                                ins = act(h_tm[:, j // 2, (j % 2) * 512:(j % 2 + 1) * 512],
                                          ps_a[:, j * 512:(j + 1) * 512], ACT.Copy)
                            ins.then_inc(tm_taken, ac.adds(tm_taken))
                        eng.wait_ge(chunk_done, ac.next(chunk_done, WR))
                        act(pq_t[:, WR * g:WR * (g + 1), b * P:(b + 1) * P],
                            ps_b[:, (g % 2) * 512:(g % 2 + 1) * 512].rearrange("p (j t) -> p j t", t=P),
                            ACT.Copy).then_inc(pq_taken, ac.adds(pq_taken))
                    eng.wait_ge(sc_done, ac.next(sc_done))
                    if b:
                        eng.wait_ge(keys_used, ac.next(keys_used))
                    for j in range(4):
                        ins = act(pscore[:, 4 * j:4 * j + 4, :], ps_a[:, j * 512:(j + 1) * 512], ACT.Copy)
                    ins.then_inc(sc_taken, ac.adds(sc_taken))
                ac.skip(keys_used, 1)

            def top_exps(b):
                eng.wait_ge(top_ready, ac.next(top_ready))
                act(top_sc[b], top_sc[b], ACT.Exp).then_inc(top_exp, ac.adds(top_exp))

            def ada(n):
                with ac.loop(n // (2 * WR), chunk_done=2 * WR, ada_taken=2):
                    for half in range(2):
                        eng.wait_ge(chunk_done, ac.next(chunk_done, WR))
                        act(ada_row[0:2, half, :], ps_b[0:2, half * 512:(half + 1) * 512], ACT.Copy).then_inc(
                            ada_taken, ac.adds(ada_taken))

            def peer_gelu():
                eng.wait_ge(dots_done, ac.next(dots_done))
                act(wts[:, :], dots[:, :], ACT.Gelu_apprx_tanh).then_inc(gelu_done, ac.adds(gelu_done))

            eng.sem_inc(h_done, AHEAD["h_done"])
            eng.sem_inc(z_done, AHEAD["z_done"])
            eng.wait_ge(vecs_in, 32)
            at = sc_["c"][0]
            act(cond[:, :], second[:, at:at + 2 * KT], ACT.Silu).then_inc(c_silu, ac.adds(c_silu))

            eng.wait_ge(c_rows_in, 16)
            act(c_rows, c_rows, ACT.Silu).then_inc(c_rows_silu, ac.adds(c_rows_silu))
            eng.wait_ge(lb_max, ac.next(lb_max))
            act(lbs[:, 8:16], lbs[:, 0:8], ACT.Exp).then_inc(lb_exp, ac.adds(lb_exp))
            ada(FIRST_ADA)
            eng.wait_ge(ctx_in, 16)
            eng.wait_ge(eps_set, ac.next(eps_set))
            rms(ctx_t, 0, 0, 1)
            qkv(0, range(5), 0)
            attention([0, 1], False)
            peer_scores(ctx_t, 0, 1)
            ada(ADA_CHUNKS)
            for b in range(NB):
                top_exps(b)

            def feed_forward():
                def tile(ft):
                    eng.wait_ge(up_done, ac.next(up_done))
                    act(
                        silu[:, ft % 2, :], ps_b[:, (ft % 2) * 512:(ft % 2) * 512 + T], ACT.Silu).then_inc(
                            silu_done, ac.adds(silu_done))
                tile(0)
                with ac.loop(FT_TURNS, up_done=FT_STEP, silu_done=FT_STEP, hidden_done=FT_STEP):
                    for q in range(FT_STEP):
                        eng.wait_ge(hidden_done, ac.now(hidden_done))
                        tile(q + 1)
                        ac.skip(hidden_done, 1)
                eng.wait_ge(hidden_done, ac.now(hidden_done))
                tile(FT - 1)
                ac.skip(hidden_done, 2)

            def layer_norm(n):
                for j in range(4):
                    eng.wait_ge(centred_done, ac.next(centred_done))
                    act(
                        sq[:, 2 * j:2 * j + 2, :], resid[:, 2 * j:2 * j + 2, :], ACT.Square).then_inc(
                            square_done, ac.adds(square_done))
                eng.wait_ge(var_done, ac.next(var_done))
                act(std[:, :], ps_d[:, 0:T], ACT.Sqrt, bias=eps[:, 0:1]).then_inc(std_done, ac.adds(std_done))
                for k in range(KT):
                    if k % 2 == 0:
                        eng.wait_ge(scaled_done, ac.next(scaled_done))
                    act(x_t[:, k, :], resid[:, k, :], ACT.Identity, scale=vec(cur, fc, "ln_g", n * KT + k),
                                         bias=vec(cur, fc, "ln_b", n * KT + k)).then_inc(h_done, ac.adds(h_done))

            with ac.loop(L, chunk_done=MIX_CHUNKS, up_done=2 * FT, silu_done=2 * FT, hidden_done=2 * FT,
                         centred_done=16, square_done=16, var_done=4, std_done=4, scaled_done=16, h_done=4 * KT,
                         z_done=24, f_done=1, log_done=1, decay_done=8, exp_done=8, o_done=1, o_square_done=2,
                         o_ms_done=1, o_std_done=1, pool_mm_done=1, pooled_done=1, cmax_done=NB, cexp_done=NB,
                         cpt_done=2 * NB, cpt_taken=2 * NB, co_done=NB, co_taken=NB, dots_done=1, gelu_done=1,
                         layer_vecs=1, qk_done=9) as l:
                eng.wait_ge(layer_vecs, ac.next(layer_vecs))
                feed_forward()
                layer_norm(0)

                def group(g, dst, func=ACT.Copy):
                    eng.wait_ge(chunk_done, ac.next(chunk_done, 2))
                    act(dst, ps_b[:, (g % 2) * 512:(g % 2 + 1) * 512], func).then_inc(z_done, ac.adds(z_done))

                def exps(i):
                    eng.wait_ge(decay_done, ac.next(decay_done))
                    act(dec[i % 2], dec[i % 2], ACT.Exp).then_inc(exp_done, ac.adds(exp_done))

                group(0, z_f[:, 0:2, :], ACT.Sigmoid)
                group(1, z_f[:, 2:4, :], ACT.Sigmoid)
                group(2, z_q[:, 0:2, :])
                group(3, z_q[:, 2:4, :])
                eng.wait_ge(f_done, ac.next(f_done))
                act(dec[0], z_f, ACT.Ln).then_inc(log_done, ac.adds(log_done))
                for g, dst in ((4, v_tm[:, 0]), (5, v_tm[:, 1]), (6, z_h), (7, z_c), (8, z_b)):
                    group(g, dst)
                    exps(g - 3)
                group(9, pool_u[:, :, 16:])
                exps(6)
                group(10, z_g[:, 0:2, :], ACT.Sigmoid)
                exps(7)
                group(11, z_g[:, 2:4, :], ACT.Sigmoid)
                exps(8)
                eng.wait_ge(o_done, ac.next(o_done))
                eng.wait_ge(qk_done, ac.next(qk_done, 9))
                for j in range(2):
                    act(view(arena, 8704 + 512 * j, 512), ps_a[:, 1024 + 512 * j:1536 + 512 * j],
                                                ACT.Square).then_inc(o_square_done, ac.adds(o_square_done))
                group(12, ca_k[:, 0:2, :])
                eng.wait_ge(o_ms_done, ac.next(o_ms_done))
                act(view(arena, 9728, 1024), ps_a[:, 0:1024], ACT.Sqrt, scale=D / P,
                                          bias=eps[:, 1:2]).then_inc(o_std_done, ac.adds(o_std_done))
                for g in range(13, 16):
                    group(g, ca_k[:, 2 * g - 24:2 * g - 22, :])
                for g in range(16, 20):
                    group(g, ca_v[:, g - 16])
                eng.wait_ge(pool_mm_done, ac.next(pool_mm_done))
                for t in range(2):
                    ins = act(mix[:, 6 + t, :], ps_d[:, t * T:(t + 1) * T], ACT.Copy, scale=vec(cur, fc, "pool_scale", t))
                ins.then_inc(pooled_done, ac.adds(pooled_done))
                peer_gelu()
                ac.skip(chunk_done, KT)
                layer_norm(1)
                for g in range(20, 24):
                    group(g, ca_q[:, 2 * g - 40:2 * g - 38, :])
                for b in range(NB):
                    eng.wait_ge(cmax_done, ac.next(cmax_done))
                    for h in range(CA_H):
                        ins = act(ca_e[b][:, h, :], ps_a[:, b * 1024 + h * T:b * 1024 + (h + 1) * T], ACT.Exp,
                                  scale=CA_SCALE, bias=stats[:, 24 + 4 * b + h:25 + 4 * b + h],
                                  accum_out=stats[:, 32 + 4 * b + h:33 + 4 * b + h])
                    ins.then_inc(cexp_done, ac.adds(cexp_done))
                for b in range(NB):
                    if b:
                        eng.wait_ge(co_done, ac.now(co_done))
                    for m in range(NB):
                        eng.wait_ge(cpt_done, ac.next(cpt_done))
                        act(ca_pt[:, m, :, :], (ps_c, ps_d)[m][:, :], ACT.Copy).then_inc(cpt_taken, ac.adds(cpt_taken))
                    eng.wait_ge(co_done, ac.next(co_done))
                    for j in range(2):
                        ins = act(ca_o[:, 4 * j:4 * j + 4, b * P:(b + 1) * P],
                                  ps_b[:, j * 512:(j + 1) * 512].rearrange("p (k t) -> p k t", t=P), ACT.Copy)
                    ins.then_inc(co_taken, ac.adds(co_taken))
                ac.skip(chunk_done, KT)
                layer_norm(2)
                feed_forward()
                layer_norm(3)

            for l in range(L):
                if l == 0:
                    eng.wait_ge(h_done, ac.now(h_done))
                    rms(x_t, 0, 0, 0)
                    ac.skip(x_final, KT)
                else:
                    rms(x_t, l, 0, 0, x_final)
                qkv(l, range(5), 2)
                attention([0, 1, 2, 3], l == 1)
                peer_scores(x_t, l, 0)
                top_exps(0)
                peer_gelu()
                top_exps(1)
                if l == 0:
                    eng.wait_ge(x_final, ac.now(x_final))
                    rms(ctx_t, 1, 0, 1)
                    qkv(1, [4], 0)
                peer_gelu()

        @block.vector
        def _(eng):
            ve = Lane(eng, ("down_done",))
            V = nc.vector

            def bcast(ap, *shape):
                return ap.to_broadcast([P, *shape])

            def modulation(l, part, product):
                at = sc_["ada_b"][0] + ADA_CHUNKS * l + 24 * part
                V.tensor_tensor(mods[:, l, 24 * part:24 * part + 24], product, bcast(second[:, at:at + 24].unsqueeze(2), 24, 2),
                                ALU.add).then_inc(mods_done, ve.adds(mods_done))
                eng.wait_ge(mods_done, ve.now(mods_done))
                at = sc_[("gain1", "gain2")[part]][0] + 8 * l
                V.scalar_tensor_tensor(gains[:, l, part], mods[:, l, 24 * part + 8:24 * part + 16, :], 1.0,
                                       bcast(second[:, at:at + 8].unsqueeze(2), 8, 2), ALU.add, ALU.mult).then_inc(
                    dve_step, ve.adds(dve_step))
                eng.wait_ge(dve_step, ve.now(dve_step))

            tiles_done = [0]

            def ada_tiles(n):
                for j in range(tiles_done[0], min(tiles_done[0] + n, FIRST_ADA)):
                    eng.wait_ge(ada_in[j % GR], ve.next(ada_in[j % GR], 16))
                    for c in range(2):
                        eng.wait_ge(dve_step, ve.now(dve_step))
                        ins = V.scalar_tensor_tensor(ada_unread, rows[:, j % GR, :], 1.0, c_rows[:, c, :], ALU.mult,
                                                     ALU.mult, accum_out=ada_cols[:, j, c:c + 1])
                        if c == 0:
                            ins.then_inc(dve_step, ve.adds(dve_step))
                    eng.wait_ge(dve_step, ve.now(dve_step))
                    ins.then_inc(ada_used, ve.adds(ada_used))
                    eng.wait_ge(ada_used, ve.now(ada_used))
                    tiles_done[0] += 1

            def rms(src):
                eng.wait_ge(std2_done, ve.next(std2_done))
                V.reciprocal(std[:, :], std[:, :]).then_inc(dve_step, ve.adds(dve_step))
                eng.wait_ge(dve_step, ve.now(dve_step))
                for j in range(4):
                    V.tensor_tensor(h2[:, 2 * j:2 * j + 2, :], src[:, 2 * j:2 * j + 2, :],
                                                         bcast(std[:, :].unsqueeze(1), 2, T), ALU.mult).then_inc(
                                                             norm2_done, ve.adds(norm2_done))

            def qk_norm(groups, rope, key_at, tiles=0):
                for g in groups:
                    raw, r = qk_raw[:, 2 * g:2 * g + 2, :], qk_r[:, 2 * g:2 * g + 2, :]
                    out = qk_n[:, 2 * g:2 * g + 2, :] if g < 4 else keys_t[:, :, key_at:key_at + T]
                    eng.wait_ge(qkv_taken, ve.next(qkv_taken))
                    ada_tiles(tiles)
                    eng.wait_ge(qk_std_done, ve.next(qk_std_done))
                    V.reciprocal(r, r).then_inc(dve_step, ve.adds(dve_step))
                    if rope:
                        eng.wait_ge(rot_done, ve.next(rot_done))
                        V.tensor_tensor(raw, raw, bcast(cos.unsqueeze(1), 2, T), ALU.mult).then_inc(
                            dve_step, ve.adds(dve_step))
                        V.tensor_tensor(out, view(ps_a, 1024 + (g % 2) * 512, 2, T), bcast(sin.unsqueeze(1), 2, T),
                                        ALU.mult).then_inc(rot_taken, ve.adds(rot_taken))
                        eng.wait_ge(dve_step, ve.now(dve_step))
                        eng.wait_ge(rot_taken, ve.now(rot_taken))
                        V.tensor_tensor(raw, raw, out, ALU.add).then_inc(dve_step, ve.adds(dve_step))
                    eng.wait_ge(dve_step, ve.now(dve_step))
                    ins = V.tensor_tensor(out, raw, r, ALU.mult)
                    if g < 4:
                        ins.then_inc(dve_step, ve.adds(dve_step))
                    else:
                        ins.then_inc(roped, ve.adds(roped))
                ve.skip(qkv_taken, 1)

            def attention(blocks, windowed, tiles=0):
                n = len(blocks) * P
                for u in range(NB * GROUPS):
                    b, g = u // GROUPS, u % GROUPS
                    ada_tiles(tiles)
                    eng.wait_ge(s_done, ve.next(s_done))
                    V.tensor_reduce(stats[:, 0:4], ps_a[:, :].rearrange("p (r k) -> p r k", r=REP)[:, :, 0:n], AX,
                                    ALU.max).then_inc(dve_step, ve.adds(dve_step))
                    eng.wait_ge(dve_step, ve.now(dve_step))
                    if windowed:
                        sink = second[:, sc_["sinks"][0] + REP * g:sc_["sinks"][0] + REP * (g + 1)]
                        V.scalar_tensor_tensor(stats[:, 0:4], stats[:, 0:4], SCALE, sink, ALU.mult,
                                               ALU.max).then_inc(dve_step, ve.adds(dve_step))
                        eng.wait_ge(dve_step, ve.now(dve_step))
                        V.tensor_tensor(stats[:, 12:16], sink, stats[:, 0:4], ALU.subtract).then_inc(
                            dve_step, ve.adds(dve_step))
                        eng.wait_ge(dve_step, ve.now(dve_step))
                    V.tensor_scalar(stats[:, 4:8], stats[:, 0:4], -1.0 if windowed else -SCALE, None,
                                    ALU.mult).then_inc(s_max, ve.adds(s_max))
                    if windowed:
                        eng.wait_ge(sink_exp, ve.next(sink_exp))
                    eng.wait_ge(s_exp, ve.next(s_exp))
                    if windowed:
                        V.tensor_tensor(stats[:, 8:12], stats[:, 8:12], stats[:, 16:20], ALU.add).then_inc(
                            dve_step, ve.adds(dve_step))
                        eng.wait_ge(dve_step, ve.now(dve_step))
                    V.reciprocal(stats[:, 20:24], stats[:, 8:12]).then_inc(dve_step, ve.adds(dve_step))
                    if u >= 2:
                        eng.wait_ge(pt_done, ve.next(pt_done, len(blocks)))
                    eng.wait_ge(dve_step, ve.now(dve_step))
                    V.tensor_tensor(over_sum[u % 2], bcast(ident.unsqueeze(1), REP, P),
                                    bcast(stats[:, 20:24].unsqueeze(2), REP, P), ALU.mult).then_inc(
                        s_prob, ve.adds(s_prob))
                ve.skip(pt_done, 2 * len(blocks))

            def gated_add(x, ps, l, part, who, added, ready=None):
                for k in range(KT):
                    if ready is not None and k % 2 == 0:
                        eng.wait_ge(ready, ve.next(ready, 2))
                    V.scalar_tensor_tensor(x[:, k, :], ps[:, k, :], mods[:, l, 24 * part + 16 + k, who:who + 1],
                                           x[:, k, :], ALU.mult, ALU.add).then_inc(added, ve.adds(added))

            def best_step(step, values, left, top, at):
                if step == 2:
                    return V.match_replace(left, top[:, 0:8], values, LOWEST)
                src, best = (values, slice(0, 8)) if step < 2 else (left, slice(8, 16))
                if step in (0, 3):
                    return V.max(top[:, best], src)
                return V.max_index(at[:, best], top[:, best], src)

            places = pos_u[:, 0:SLOTS].rearrange("p (h k) -> p h k", k=TOPK)
            key_lists = (pscore, pscore2, top_v, top_iu)
            sum_lists = [(cand, cand2, top_sc[b], places) for b in range(NB)]

            def sums_of_best(h0, h1):
                eng.wait_ge(dve_step, ve.now(dve_step))
                ins = V.tensor_copy(top_i[:, 2 * h0:2 * h1, :], top_iu[:, 2 * h0:2 * h1, :])
                if h1 == PEER_H:
                    ins.then_inc(keys_used, ve.adds(keys_used))
                else:
                    ins.then_inc(dve_step, ve.adds(dve_step))
                halves = top_v.rearrange("p (h c) a -> p h c a", c=2)
                V.tensor_tensor(cand[:, h0:h1, :].rearrange("p h (a b) -> p h a b", b=TOPK),
                                bcast(halves[:, h0:h1, 0, :].unsqueeze(3), h1 - h0, TOPK, TOPK),
                                bcast(halves[:, h0:h1, 1, :].unsqueeze(2), h1 - h0, TOPK, TOPK),
                                ALU.add).then_inc(dve_step, ve.adds(dve_step))
                eng.wait_ge(keys_used, ve.now(keys_used))

            ID_PARTS = 5

            def expert_ids(l, b, part, h0=0, h1=PEER_H):
                n, s0, s1 = h1 - h0, h0 * TOPK, h1 * TOPK
                ids = top_i.rearrange("p (h c) a -> p h c a", c=2)
                matches = [o[:, h0:h1] for o in onehot]
                flat = [o.rearrange("p h k a -> p (h k) a") for o in matches]
                eng.wait_ge(dve_step, ve.now(dve_step))
                if part == 0:
                    if h1 == PEER_H:
                        V.tensor_copy(stats[:, 0:8], top_sc[b][:, :, 0]).then_inc(dve_step, ve.adds(dve_step))
                    V.tensor_scalar(pos_u[:, SLOTS + s0:SLOTS + s1], pos_u[:, s0:s1], 4, None,
                                    ALU.logical_shift_right).then_inc(dve_step, ve.adds(dve_step))
                    V.tensor_scalar(pos_u[:, 2 * SLOTS + s0:2 * SLOTS + s1], pos_u[:, s0:s1], 15, None,
                                    ALU.bitwise_and).then_inc(dve_step, ve.adds(dve_step))
                    eng.wait_ge(dve_step, ve.now(dve_step))
                    if h1 == PEER_H:
                        V.tensor_tensor(top_sc[b], top_sc[b], bcast(stats[:, 0:8].unsqueeze(2), PEER_H, TOPK),
                                        ALU.subtract).then_inc(top_ready, ve.adds(top_ready))
                    for c in range(2):
                        V.tensor_copy(place[c][:, s0:s1], pos_u[:, (1 + c) * SLOTS + s0:(1 + c) * SLOTS + s1]).then_inc(
                            dve_step, ve.adds(dve_step))
                elif part == 1:
                    for c in range(2):
                        V.tensor_tensor(flat[c], bcast(place[c][:, s0:s1].unsqueeze(2), s1 - s0, TOPK),
                                        bcast(iota_b[:, :].unsqueeze(1), s1 - s0, TOPK),
                                        ALU.is_equal).then_inc(dve_step, ve.adds(dve_step))
                elif part == 2:
                    for c in range(2):
                        V.tensor_tensor(matches[c], matches[c], bcast(ids[:, h0:h1, c, :].unsqueeze(2), n, TOPK, TOPK),
                                        ALU.mult).then_inc(dve_step, ve.adds(dve_step))
                elif part == 3:
                    for c in range(2):
                        V.tensor_reduce(sel[c][:, s0:s1], flat[c], AX, ALU.add).then_inc(dve_step, ve.adds(dve_step))
                else:
                    V.tensor_scalar(sel[2][:, s0:s1], sel[0][:, s0:s1], float(N_KEYS), float(l * N_EXPERTS), ALU.mult,
                                    ALU.add).then_inc(dve_step, ve.adds(dve_step))
                    eng.wait_ge(dve_step, ve.now(dve_step))
                    V.tensor_tensor(sel[3][:, s0:s1], sel[2][:, s0:s1], sel[1][:, s0:s1], ALU.add).then_inc(
                        dve_step, ve.adds(dve_step))
                    eng.wait_ge(dve_step, ve.now(dve_step))
                    V.tensor_copy(idx[:, b, s0:s1], sel[3][:, s0:s1]).then_inc(idx_done, ve.adds(idx_done))

            def search_keys(step, h0, h1):
                eng.wait_ge(dve_step, ve.now(dve_step))
                for j in range(2 * h0, 2 * h1):
                    best_step(step, *(v[:, j, :] for v in key_lists)).then_inc(dve_step, ve.adds(dve_step))

            def search_sums(step, b, h0, h1):
                eng.wait_ge(dve_step, ve.now(dve_step))
                for h in range(h0, h1):
                    best_step(step, *(v[:, h, :] for v in sum_lists[b])).then_inc(dve_step, ve.adds(dve_step))

            def top_experts(l, b, h1=PEER_H):
                eng.wait_ge(sc_taken, ve.next(sc_taken))
                for step in range(5):
                    search_keys(step, 0, h1)
                sums_of_best(0, h1)
                for step in range(5):
                    search_sums(step, b, 0, h1)
                for part in range(ID_PARTS):
                    expert_ids(l, b, part, 0, h1)

            def gate_experts(b):
                gate = gates[:, b, :].rearrange("p (h k) -> p h k", k=TOPK)
                eng.wait_ge(top_exp, ve.next(top_exp))
                V.tensor_reduce(stats[:, 8:16], top_sc[b], AX, ALU.add).then_inc(dve_step, ve.adds(dve_step))
                eng.wait_ge(dve_step, ve.now(dve_step))
                V.reciprocal(stats[:, 16:24], stats[:, 8:16]).then_inc(dve_step, ve.adds(dve_step))
                eng.wait_ge(dve_step, ve.now(dve_step))
                V.tensor_tensor(gate, top_sc[b], bcast(stats[:, 16:24].unsqueeze(2), PEER_H, TOPK),
                                ALU.mult).then_inc(dve_step, ve.adds(dve_step))

            def dot_slot(s, h, out, acc):
                eng.wait_ge(rows_in[s], ve.next(rows_in[s], 16))
                eng.wait_ge(row_used, ve.now(row_used, 1))
                V.scalar_tensor_tensor(acc[s % 2], rows[:, s, :], 1.0, h, ALU.mult, ALU.mult,
                                       accum_out=out).then_inc(row_used, ve.adds(row_used))

            def sum_slot(s, w, acc, first=False):
                eng.wait_ge(rows_in[s], ve.next(rows_in[s], 16))
                if first:
                    ins = V.tensor_scalar(acc[s % 2], rows[:, s, :], w, None, ALU.mult)
                else:
                    eng.wait_ge(row_used, ve.now(row_used, 1))
                    ins = V.scalar_tensor_tensor(acc[s % 2], rows[:, s, :], w, acc[s % 2], ALU.mult, ALU.add)
                ins.then_inc(row_used, ve.adds(row_used))

            def some_slots(summing, h, at, n, acc):
                for q in range(at, at + n):
                    if summing:
                        sum_slot(q % GR, wts[:, q:q + 1], acc, q < 2)
                    else:
                        dot_slot(q % GR, h, dots[:, q:q + 1], acc)

            def turn_begin(summing, i, at):
                eng.wait_ge(dve_step, ve.now(dve_step))
                if summing:
                    eng.wait_ge(row_used, ve.now(row_used))
                    V.tensor_copy(stage[:, :], wts[:, bass.ds(i * TURN_SLOTS + at, TURN_SLOTS)]).then_inc(
                        dve_step, ve.adds(dve_step))
                    eng.wait_ge(dve_step, ve.now(dve_step))

            def turn_slots(summing, h, at, n, acc):
                for q in range(at, at + n):
                    if summing:
                        sum_slot(q % GR, stage[:, q:q + 1], acc)
                    else:
                        dot_slot(q % GR, h, stage[:, q:q + 1], acc)

            def turn_end(summing, i, at):
                if not summing:
                    eng.wait_ge(row_used, ve.now(row_used))
                    V.tensor_copy(dots[:, bass.ds(i * TURN_SLOTS + at, TURN_SLOTS)], stage[:, :]).then_inc(
                        dve_step, ve.adds(dve_step))

            def phase_end(summing, out, acc):
                eng.wait_ge(row_used, ve.now(row_used))
                if summing:
                    V.tensor_tensor(out, acc[0], acc[1], ALU.add).then_inc(pout_done, ve.adds(pout_done))
                    eng.wait_ge(pout_done, ve.now(pout_done))
                else:
                    eng.wait_ge(dve_step, ve.now(dve_step))
                    V.tensor_copy(dots[:, 0:1], dots[:, 0:1]).then_inc(dots_done, ve.adds(dots_done))

            def weigh(gate):
                eng.wait_ge(gelu_done, ve.next(gelu_done))
                V.tensor_tensor(wts[:, :], wts[:, :], gate, ALU.mult).then_inc(dve_step, ve.adds(dve_step))
                eng.wait_ge(dve_step, ve.now(dve_step))

            per_turn = dict(row_used=TURN_SLOTS, dve_step=1, **{f"rows_{s}": 16 * TURN_SLOTS // GR for s in range(GR)})

            def plain_turns(summing, b, at):
                with ve.loop((SLOTS - at) // TURN_SLOTS, **per_turn) as i:
                    turn_begin(summing, i, at)
                    turn_slots(summing, h_tm[:, b, :], 0, TURN_SLOTS, acc_second)
                    turn_end(summing, i, at)

            def search_turns(summing, h, at, lists, count, size):
                n, width = 4, (size, size, TOPK, TOPK)
                with ve.loop(count // n, **per_turn | dict(dve_step=4 + 5 * n)) as i:
                    turn_begin(summing, i, at)
                    now = [t[:, 0:n * w].rearrange("p (j k) -> p j k", j=n) for t, w in zip(list_now, width)]
                    V.tensor_copy(now[0], lists[0][:, bass.ds(i * n, n), :]).then_inc(dve_step, ve.adds(dve_step))
                    for step in range(5):
                        eng.wait_ge(dve_step, ve.now(dve_step))
                        eng.sem_inc(dve_pause, 1)
                        for q in range(n):
                            best_step(step, *(t[:, q, :] for t in now)).then_inc(dve_step, ve.adds(dve_step))
                        turn_slots(summing, h, 3 * step, 3 if step < 4 else TURN_SLOTS - 12, acc_second)
                    eng.wait_ge(dve_step, ve.now(dve_step))
                    for t, from_now in zip(lists[2:], now[2:]):
                        V.tensor_copy(t[:, bass.ds(i * n, n), :], from_now).then_inc(dve_step, ve.adds(dve_step))
                    turn_end(summing, i, at)
                return at + TURN_SLOTS * (count // n)

            def first_block_peer(l):
                h, h0 = h_tm[:, 0, :], PEER_H // 2
                for step in range(5):
                    search_keys(step, h0, PEER_H)
                sums_of_best(h0, PEER_H)
                eng.wait_ge(tm_taken, ve.next(tm_taken))
                for step in range(5):
                    search_sums(step, 0, h0, PEER_H)
                    some_slots(False, h, 2 * step, 2, acc_second)
                for part in range(ID_PARTS):
                    expert_ids(l, 0, part, h0, PEER_H)
                    some_slots(False, h, 10 + part, 1, acc_second)
                some_slots(False, h, 15, 1, acc_second)
                eng.wait_ge(sc_taken, ve.next(sc_taken))
                done = search_turns(False, h, TURN_SLOTS, key_lists, 2 * PEER_H, N_KEYS)
                gate_experts(0)
                plain_turns(False, 0, done)
                phase_end(False, h, acc_second)
                sums_of_best(0, PEER_H)
                weigh(gates[:, 0, :])
                some_slots(True, h, 0, TURN_SLOTS, acc_second)
                done = search_turns(True, h, TURN_SLOTS, sum_lists[1], PEER_H, TOPK * TOPK)
                eng.wait_ge(row_used, ve.now(row_used))
                for part in range(ID_PARTS):
                    expert_ids(l, 1, part)
                    some_slots(True, h, done + 3 * part, 3 if part < 4 else TURN_SLOTS - 12, acc_second)
                plain_turns(True, 0, done + TURN_SLOTS)
                gate_experts(1)
                phase_end(True, h, acc_second)

            def second_block_peer(l):
                h = h_tm[:, 1, :]
                if l == 0:
                    rms(ctx_t)
                plain_turns(False, 1, 0)
                phase_end(False, h, acc_second)
                if l == 0:
                    ve.skip(chunk_done, 4)
                    qk_norm([4], False, 0)
                weigh(gates[:, 1, :])
                some_slots(True, h, 0, TURN_SLOTS, acc_second)
                plain_turns(True, 1, TURN_SLOTS)
                phase_end(True, h, acc_second)

            V.memset(zeros[:, :], 0.0).then_inc(zeros_set, ve.adds(zeros_set))
            V.memset(eps[:, 0:1], LN_EPS).then_inc(dve_step, ve.adds(dve_step))
            eng.wait_ge(dve_step, ve.now(dve_step))
            V.memset(eps[:, 1:2], RMS_EPS).then_inc(eps_set, ve.adds(eps_set))
            eng.sem_inc(row_used, AHEAD["row_used"])
            eng.sem_inc(hidden_done, AHEAD["hidden_done"])
            eng.wait_ge(vecs_in, 32)
            eng.wait_ge(consts_in, 16)
            V.tensor_copy(iota_b[:, :], iota).then_inc(dve_step, ve.adds(dve_step))
            raw = [vec(first, fc, "lb", l * n_first, 4) for l in range(L)]
            V.tensor_tensor(lbs[:, 24:28], raw[0], raw[1], ALU.max).then_inc(dve_step, ve.adds(dve_step))
            eng.wait_ge(dve_step, ve.now(dve_step))
            V.tensor_tensor(lbs[:, 0:4], raw[0], lbs[:, 24:28], ALU.subtract).then_inc(dve_step, ve.adds(dve_step))
            eng.wait_ge(dve_step, ve.now(dve_step))
            V.tensor_tensor(lbs[:, 4:8], raw[1], lbs[:, 24:28], ALU.subtract).then_inc(lb_max, ve.adds(lb_max))
            eng.wait_ge(lb_exp, ve.next(lb_exp))
            V.tensor_tensor(lbs[:, 16:20], lbs[:, 8:12], lbs[:, 12:16], ALU.add).then_inc(dve_step, ve.adds(dve_step))
            eng.wait_ge(dve_step, ve.now(dve_step))
            V.reciprocal(lbs[:, 20:24], lbs[:, 16:20]).then_inc(dve_step, ve.adds(dve_step))
            eng.wait_ge(dve_step, ve.now(dve_step))
            for l in range(L):
                V.tensor_tensor(
                    lbs[:, 4 * l:4 * l + 4], lbs[:, 8 + 4 * l:12 + 4 * l], lbs[:, 20:24], ALU.mult).then_inc(
                        dve_step, ve.adds(dve_step))
            eng.wait_ge(dve_step, ve.now(dve_step))
            V.tensor_tensor(lbs[:, 8:12], lbs[:, 0:4], lbs[:, 4:8], ALU.add).then_inc(dve_step, ve.adds(dve_step))
            eng.wait_ge(dve_step, ve.now(dve_step))
            for l, upto in enumerate((lbs[:, 0:4], lbs[:, 8:12])):
                V.tensor_tensor(raw[l], upto, lbs[:, 0:4], ALU.subtract).then_inc(dve_step, ve.adds(dve_step))
            eng.wait_ge(dve_step, ve.now(dve_step))
            for l in range(L):
                V.tensor_scalar(
                    vec(first, fc, "omlb", l * n_first, 4), raw[l], -1.0, 1.0, ALU.mult, ALU.add).then_inc(
                        dve_step, ve.adds(dve_step))
            eng.wait_ge(dve_step, ve.now(dve_step))

            eng.wait_ge(c_rows_silu, 1)
            ada_tiles(EARLY_TILES)
            ve.skip(chunk_done, FIRST_ADA)
            eng.wait_ge(ada_done, ve.next(ada_done, FIRST_ADA // (2 * WR)))
            modulation(0, 0, ps_d[:, 0:2 * FIRST_ADA].rearrange("p (j w) -> p j w", w=2))
            rms(ctx_t)
            ve.skip(chunk_done, QKV_CHUNKS)
            qk_norm(range(5), False, 0, 1)
            attention([0, 1], False, 1)

            def project_out(x, l, who):
                gated_add(x, acc_t, l, 0, who, x_added, chunk_done)

            ada_tiles(FIRST_ADA)
            modulation(0, 1, ada_cols)
            project_out(ctx_t, 0, 1)
            eng.wait_ge(x_added, ve.now(x_added))
            rms(ctx_t)
            ve.skip(chunk_done, NB * PQ_CHUNKS)
            for b in range(NB):
                top_experts(0, b)
            eng.wait_ge(tm_taken, ve.next(tm_taken))
            for b in range(NB):
                gate_experts(b)
            ve.skip(chunk_done, ADA_CHUNKS)
            eng.wait_ge(ada_done, ve.next(ada_done, ADA_CHUNKS // (2 * WR)))
            for part in range(2):
                at = part * ADA_CHUNKS
                modulation(1, part, ps_d[:, at:at + ADA_CHUNKS].rearrange("p (j w) -> p j w", w=2))

            eng.wait_ge(dve_step, ve.now(dve_step))
            eng.wait_ge(idx_done, ve.now(idx_done))
            V.memset(attn, 0.0).then_inc(dve_step, ve.adds(dve_step))
            V.memset(conv_u[:, :, 0:2], 0.0).then_inc(dve_step, ve.adds(dve_step))
            V.memset(pool_u[:, :, 0:16], 0.0).then_inc(dve_step, ve.adds(dve_step))
            for s in pool_s:
                V.memset(s, 0.0).then_inc(dve_step, ve.adds(dve_step))
            eng.wait_ge(masks_in, 16)
            eng.wait_ge(x_in, 16)
            eng.wait_ge(dve_step, ve.now(dve_step))

            def feed_forward(h, summing):
                at = SLOTS - FF_SLOTS if summing else 0

                def tile(ft):
                    eng.wait_ge(up_done, ve.next(up_done))
                    eng.wait_ge(silu_done, ve.next(silu_done))
                    eng.wait_ge(down_done, ve.next(down_done))
                    V.scalar_tensor_tensor(
                        hidden[:, ft % 2, :], ps_b[:, (ft % 2) * 512 + T:(ft % 2 + 1) * 512], 0.5, silu[:, ft % 2, :],
                        ALU.mult, ALU.mult).then_inc(hidden_done, ve.adds(hidden_done))

                tile(0)
                some_slots(summing, h, at, HEAD_SLOTS, acc_first)
                with ve.loop(FT_TURNS, up_done=FT_STEP, silu_done=FT_STEP, down_done=FT_STEP, hidden_done=FT_STEP,
                             **per_turn) as i:
                    turn_begin(summing, i, at + HEAD_SLOTS)
                    for q in range(FT_STEP):
                        tile(q + 1)
                        turn_slots(summing, h, q * FT_SLOTS, FT_SLOTS, acc_first)
                    turn_end(summing, i, at + HEAD_SLOTS)
                tile(FT - 1)
                if summing:
                    phase_end(summing, h, acc_first)
                eng.wait_ge(down_done, ve.now(down_done, -2))

            def layer_norm(wait=0):
                for j in range(4):
                    if wait == 2 or (wait and j == 0):
                        eng.wait_ge(chunk_done, ve.next(chunk_done, wait))
                    V.scalar_tensor_tensor(
                        resid[:, 2 * j:2 * j + 2, :], x_t[:, 2 * j:2 * j + 2, :], ALPHA, acc_t[:, 2 * j:2 * j + 2, :],
                        ALU.mult, ALU.add).then_inc(resid_done, ve.adds(resid_done))
                eng.wait_ge(mean_done, ve.next(mean_done))
                eng.wait_ge(resid_done, ve.now(resid_done))
                for j in range(4):
                    V.tensor_tensor(
                        resid[:, 2 * j:2 * j + 2, :], resid[:, 2 * j:2 * j + 2, :],
                        bcast(ps_c[:, 0:T].unsqueeze(1), 2, T), ALU.subtract).then_inc(
                            centred_done, ve.adds(centred_done))
                eng.wait_ge(std_done, ve.next(std_done))
                V.reciprocal(std[:, :], std[:, :]).then_inc(dve_step, ve.adds(dve_step))
                eng.wait_ge(dve_step, ve.now(dve_step))
                eng.wait_ge(centred_done, ve.now(centred_done))
                for j in range(4):
                    V.tensor_tensor(
                        resid[:, 2 * j:2 * j + 2, :], resid[:, 2 * j:2 * j + 2, :],
                        bcast(std[:, :].unsqueeze(1), 2, T), ALU.mult).then_inc(scaled_done, ve.adds(scaled_done))

            all_slots = {f"rows_{s}": 32 * SLOTS // GR for s in range(GR)}
            with ve.loop(L, chunk_done=MIX_CHUNKS, up_done=2 * FT, silu_done=2 * FT, down_done=2 * FT, hidden_done=2 * FT,
                         resid_done=16, mean_done=4, centred_done=16, std_done=4, scaled_done=16, h_done=4 * KT,
                         z_done=24, f_done=1, log_done=1, decay_done=8, exp_done=8, qk_done=9, level_done=9,
                         level_taken=9, pooled_sums=1, o_std_done=1, conv_done=1, rec_done=1, cs_done=NB, cmax_done=NB, cexp_done=NB,
                         cprob_done=NB, row_used=2 * SLOTS, pout_done=1, dots_done=1, gelu_done=1, layer_vecs=1,
                         dve_step=DVE_STEPS, **all_slots) as l:
                eng.wait_ge(h_done, ve.now(h_done))
                V.tensor_copy(
                    cur[:, :], first[:, bass.ds(l * n_first, n_first)]).then_inc(layer_vecs, ve.adds(layer_vecs))
                h_ctx = h_tm[:, bass.ds(l, 1), :].rearrange("p a d -> p (a d)")
                feed_forward(h_ctx, False)
                layer_norm()
                some_slots(False, h_ctx, FF_SLOTS, EARLY_DOTS, acc_first)
                eng.wait_ge(row_used, ve.now(row_used))

                eng.wait_ge(z_done, ve.next(z_done, 2))
                eng.wait_ge(layer_vecs, ve.now(layer_vecs))
                for h in range(REC_H):
                    ins = V.tensor_scalar(z_f[:, h, :], z_f[:, h, :], vec(cur, fc, "omlb", h), vec(cur, fc, "lb", h),
                                          ALU.mult, ALU.add)
                    if h < REC_H - 1:
                        ins.then_inc(dve_step, ve.adds(dve_step))
                eng.wait_ge(dve_step, ve.now(dve_step))
                ins.then_inc(f_done, ve.adds(f_done))
                eng.wait_ge(log_done, ve.next(log_done))
                V.tensor_scalar(z_f, z_f, -1.0, 1.0, ALU.mult, ALU.add).then_inc(dve_step, ve.adds(dve_step))
                for h in range(REC_H):
                    V.tensor_tensor_scan(
                        csum[:, h, :], restart, dec[0][:, h, :], 0.0, ALU.mult, ALU.add).then_inc(
                            dve_step, ve.adds(dve_step))
                eng.wait_ge(dve_step, ve.now(dve_step))

                def decays(i):
                    if i == 8:
                        d = dec[0].rearrange("p h (c s) -> p h c s", s=CHUNK)
                        b = csum.rearrange("p h (c s) -> p h c s", s=CHUNK)
                        end = [b[:, :, c, CHUNK - 1:CHUNK] for c in range(4)]
                        both = stats[:, 40:44].unsqueeze(2)
                        V.tensor_tensor(both, end[0], end[1], ALU.add).then_inc(dve_step, ve.adds(dve_step))
                        eng.wait_ge(dve_step, ve.now(dve_step))
                        full = (REC_H, CHUNK)
                        V.tensor_tensor(
                            d[:, :, 0, :], bcast(both, *full), b[:, :, 0, :], ALU.subtract).then_inc(
                                dve_step, ve.adds(dve_step))
                        V.tensor_tensor(
                            d[:, :, 1, :], bcast(end[1], *full), b[:, :, 1, :], ALU.subtract).then_inc(
                                dve_step, ve.adds(dve_step))
                        V.tensor_copy(d[:, :, 2, :], b[:, :, 2, :]).then_inc(dve_step, ve.adds(dve_step))
                        last = V.tensor_tensor(d[:, :, 3, :], b[:, :, 3, :], bcast(end[2], *full), ALU.add)
                    else:
                        m = 1 << (i - 1)
                        n = REC_H * T // (2 * m)
                        d = dec[i % 2].rearrange("p h t -> p (h t)").rearrange("p (n c s) -> p n c s", c=2, s=m)
                        b = csum.rearrange("p h t -> p (h t)").rearrange("p (n c s) -> p n c s", c=2, s=m)
                        mid = bcast(b[:, :, 0, m - 1:m], n, m)
                        V.tensor_tensor(
                            d[:, :, 0, :], mid, b[:, :, 0, :], ALU.subtract).then_inc(dve_step, ve.adds(dve_step))
                        if m == CHUNK:
                            last = V.tensor_copy(d[:, :, 1, :], b[:, :, 1, :])
                        else:
                            last = V.tensor_tensor(d[:, :, 1, :], b[:, :, 1, :], mid, ALU.subtract)
                    eng.wait_ge(dve_step, ve.now(dve_step))
                    last.then_inc(decay_done, ve.adds(decay_done))

                def take_level(i):
                    eng.wait_ge(level_done, ve.next(level_done))
                    eng.sem_inc(dve_pause, 1)
                    for b in range(NB if i < 8 else 1):
                        ps = view(ps_a, (i % 2) * 1024 + b * 512, REC_H, P)
                        if i == 8:
                            last = V.tensor_copy(attn[:, 2], ps)
                        else:
                            last = V.copy_predicated(attn[:, b], bcast(masks[:, i, :].unsqueeze(1), REC_H, P), ps)
                            if b == 0:
                                last.then_inc(dve_step, ve.adds(dve_step))
                    eng.wait_ge(dve_step, ve.now(dve_step))
                    last.then_inc(level_taken, ve.adds(level_taken))

                decays(1)
                eng.wait_ge(z_done, ve.next(z_done, 2))
                eng.wait_ge(dve_step, ve.now(dve_step))
                V.memset(
                    stats[:, 44:45], 0.0).then_inc(qk_done, ve.adds(qk_done))
                decays(2)
                for i in range(1, 9):
                    eng.wait_ge(exp_done, ve.next(exp_done))
                    if i >= 2:
                        take_level(i - 2)
                    V.tensor_tensor(qk[i % 2][0], z_q, dec[i % 2], ALU.mult).then_inc(dve_step, ve.adds(dve_step))
                    some_slots(False, h_ctx, FF_SLOTS + EARLY_DOTS + LEVEL_DOTS * (i - 1), LEVEL_DOTS, acc_levels)
                    ins = V.tensor_tensor(qk[i % 2][1], z_f, dec[i % 2], ALU.mult)
                    eng.wait_ge(dve_step, ve.now(dve_step))
                    ins.then_inc(qk_done, ve.adds(qk_done))
                    if i + 2 <= 8:
                        eng.wait_ge(qk_done, ve.now(qk_done))
                        decays(i + 2)
                take_level(7)
                take_level(8)
                eng.wait_ge(z_done, ve.next(z_done, 5))
                V.tensor_tensor(conv_u[:, :, 2:], z_c, z_h, ALU.mult).then_inc(dve_step, ve.adds(dve_step))
                eng.wait_ge(dve_step, ve.now(dve_step))
                for t in range(2):
                    V.tensor_scalar(
                        mix[:, t, :], conv_u[:, t, 0:T], vec(cur, fc, "conv_w", 3 * t), None, ALU.mult).then_inc(
                            dve_step, ve.adds(dve_step))
                for j in range(1, 3):
                    eng.wait_ge(dve_step, ve.now(dve_step))
                    for t in range(2):
                        V.scalar_tensor_tensor(mix[:, t, :], conv_u[:, t, j:j + T], vec(cur, fc, "conv_w", 3 * t + j),
                                                    mix[:, t, :], ALU.mult, ALU.add).then_inc(
                                                        dve_step, ve.adds(dve_step))
                eng.wait_ge(dve_step, ve.now(dve_step))
                V.tensor_tensor(mix[:, 0:2, :], mix[:, 0:2, :], z_b, ALU.mult).then_inc(conv_done, ve.adds(conv_done))
                eng.wait_ge(z_done, ve.next(z_done, 3))
                src, n = pool_u, 1
                for g, dst in enumerate((pool_s[0], pool_s[1], pool_s[0], pool_s[1])):
                    t, half = g // 2, slice(64 * (g % 2), 64 * (g % 2) + 64)
                    V.tensor_tensor(dst[:, :, 2 * n - 1:], src[:, :, 2 * n - 1:], src[:, :, n - 1:T + 16 - n],
                                    ALU.add).then_inc(dve_step, ve.adds(dve_step))
                    eng.wait_ge(dve_step, ve.now(dve_step))
                    V.tensor_tensor(pool_p[half, t, :], dst[half, t, 16:], rcount[half, t, :],
                                    ALU.mult).then_inc(dve_step, ve.adds(dve_step))
                    src, n = dst, 2 * n
                eng.wait_ge(dve_step, ve.now(dve_step))
                V.tensor_tensor(pool_p, pool_p, pool_u[:, :, 16:], ALU.subtract).then_inc(
                    pooled_sums, ve.adds(pooled_sums))
                eng.wait_ge(o_std_done, ve.next(o_std_done))
                r = dec[1]
                V.reciprocal(r, r).then_inc(dve_step, ve.adds(dve_step))
                eng.wait_ge(dve_step, ve.now(dve_step))
                V.tensor_tensor(dec[0], view(ps_a, 1024, REC_H, T), r, ALU.mult).then_inc(dve_step, ve.adds(dve_step))
                eng.wait_ge(dve_step, ve.now(dve_step))
                for h in range(REC_H):
                    ins = V.scalar_tensor_tensor(mix[:, 2 + h, :], dec[0][:, h, :], vec(cur, fc, "norm_g", h), z_g[:, h, :],
                                                 ALU.mult, ALU.mult)
                    if h < REC_H - 1:
                        ins.then_inc(dve_step, ve.adds(dve_step))
                eng.wait_ge(dve_step, ve.now(dve_step))
                ins.then_inc(rec_done, ve.adds(rec_done))
                eng.wait_ge(rec_done, ve.now(rec_done))
                some_slots(False, h_ctx, SLOTS - LATE_DOTS, LATE_DOTS, acc_first)
                phase_end(False, h_ctx, acc_first)
                weigh(gates[:, bass.ds(l, 1), :].rearrange("p a s -> p (a s)"))
                some_slots(True, h_ctx, 0, MIX_SUMS[0], acc_first)
                ve.skip(z_done, 12)
                ve.skip(chunk_done, 40)
                layer_norm(KT)
                some_slots(True, h_ctx, MIX_SUMS[0], MIX_SUMS[1], acc_first)
                ve.skip(chunk_done, KT)
                for b in range(NB):
                    eng.wait_ge(cs_done, ve.next(cs_done))
                    mx, neg = stats[:, 48 + 4 * b:52 + 4 * b], stats[:, 24 + 4 * b:28 + 4 * b]
                    V.tensor_reduce(
                        mx, view(ps_a, b * 1024, CA_H, T), AX, ALU.max).then_inc(dve_step, ve.adds(dve_step))
                    eng.wait_ge(dve_step, ve.now(dve_step))
                    V.tensor_scalar(neg, mx, -CA_SCALE, None, ALU.mult).then_inc(cmax_done, ve.adds(cmax_done))
                for b in range(NB):
                    eng.wait_ge(cexp_done, ve.next(cexp_done))
                    rs = stats[:, 32 + 4 * b:36 + 4 * b]
                    V.reciprocal(stats[:, 48 + 4 * b:52 + 4 * b], rs).then_inc(dve_step, ve.adds(dve_step))
                    eng.wait_ge(dve_step, ve.now(dve_step))
                    V.tensor_tensor(
                        ca_e[b], ca_e[b], bcast(stats[:, 48 + 4 * b:52 + 4 * b].unsqueeze(2), CA_H, T),
                        ALU.mult).then_inc(cprob_done, ve.adds(cprob_done))
                some_slots(True, h_ctx, sum(MIX_SUMS[:2]), MIX_SUMS[2], acc_first)
                layer_norm(2)
                feed_forward(h_ctx, True)
                layer_norm()
                ve.skip(h_done, 4 * KT)

            eng.wait_ge(h_done, ve.now(h_done))
            for l in range(L):
                rms(x_t)
                if l == 0:
                    eng.wait_ge(po_tm_done, ve.next(po_tm_done))
                    gated_add(ctx_t, acc_t, 0, 1, 1, x_final)
                ve.skip(chunk_done, QKV_CHUNKS)
                qk_norm(range(5), True, T)
                attention([0, 1, 2, 3], l == 1)
                project_out(x_t, l, 0)
                eng.wait_ge(x_added, ve.now(x_added))
                rms(x_t)
                ve.skip(chunk_done, NB * PQ_CHUNKS)
                top_experts(l, 0, PEER_H // 2)
                first_block_peer(l)
                second_block_peer(l)
                eng.wait_ge(po_tm_done, ve.next(po_tm_done))
                gated_add(x_t, acc_t, l, 1, 0, x_final)
                eng.wait_ge(x_final, ve.now(x_final))


DVE_STEPS = 74


def shape_constants():
    t = np.arange(T)
    c = {"ident": np.eye(P), "mean_d": np.full((P, P), 1.0 / D)}
    rot = np.zeros((P, P))
    for d in range(P):
        if d // 32 % 2 == 0:
            rot[d + 32, d] = -1.0
        else:
            rot[d - 32, d] = 1.0
    c["rot"] = rot
    half = P // 2
    inv = np.float32(10000.0) ** (-np.arange(0, half, 2, dtype=np.float32) / np.float32(half))
    place = np.stack([t // 64, t % 64]).astype(np.float32)
    d = np.arange(P)
    angle = place[d // 64] * inv[d % 32][:, None].astype(np.float32)
    c["cos"], c["sin"] = np.cos(angle), np.sin(angle)
    count = np.stack([np.minimum(t + 1, w) for w in (2, 4, 8, 16)]).astype(np.float32)
    c["rcount"] = np.stack([(np.float32(1) / count)[2 * i + d // 64] for i in range(2)], 1).reshape(P, -1)
    c["restart"] = np.broadcast_to(t % CHUNK != 0, (P, T))
    q = np.arange(P)[:, None, None] + P * np.arange(NB)[None, :, None]
    window = np.where(np.abs(q - t[None, None, :]) <= 128, 0.0, NEG).astype(np.float32)
    c["iota"] = np.broadcast_to(np.arange(TOPK), (P, TOPK))
    s, u = np.arange(P)[:, None], np.arange(P)[None, :]
    masks = [s == u]
    for m in (1, 2, 4, 8, 16, 32, 64):
        masks.append((s // (2 * m) == u // (2 * m)) & (s // m % 2 == 0) & (u // m % 2 == 1))
    consts = np.concatenate([np.asarray(c[n], np.float32).reshape(P, -1) for n in CONSTS], 1)
    return consts, np.stack(masks, 1).astype(np.uint8).reshape(P, -1).view(np.uint32), window


def laid_out(x):
    def fm(v):
        return np.moveaxis(v.reshape(*v.shape[:-1], -1, P), -1, 0)

    def fm_chunks(w):
        return w.reshape(KT, P, -1, P).transpose(2, 1, 0, 3).reshape(-1, P, D)

    def tm_chunks(w):
        return w.reshape(2, 4, P, -1, T).transpose(3, 0, 2, 1, 4).reshape(-1, P, D)

    def ada_chunks(w):
        return w.reshape(4, 2, P, -1, 512).transpose(3, 0, 2, 1, 4).reshape(-1, P, D)

    def row_chunks(w):
        return w.T.reshape(-1, P, D)

    def act(v):
        return v.T.reshape(KT, P, T).transpose(1, 0, 2)

    ffn, mixw, secw = [], [], []
    for l in range(L):
        for w in ("ffn1", "ffn2"):
            ffn.append(np.stack([fm_chunks(x[w + "_gate"][l]), fm_chunks(x[w + "_up"][l]),
                                 x[w + "_down"][l].reshape(FT, P, D)], 1))
        cb, cc, ch, rq, rf, ri, rg, pu = np.split(x["w_in"][l], np.cumsum([256, 256, 256, 512, 512, 512, 512]), axis=1)
        mixw += [fm_chunks(rf), fm_chunks(rq), tm_chunks(ri), fm_chunks(ch), fm_chunks(cc), fm_chunks(cb),
                 fm_chunks(pu), fm_chunks(rg), fm_chunks(x["ca_k"][l]), tm_chunks(x["ca_v"][l]),
                 fm_chunks(x["w_out"][l]), fm_chunks(x["ca_q"][l]), fm_chunks(x["ca_o"][l])]
        if l == 0:
            secw.append(ada_chunks(x["ada_w_2"][0][:, :FIRST_ADA * P]))
        else:
            secw.append(ada_chunks(x["ada_w_2"][l]))
        secw += [fm_chunks(x["w_qkv_2"][l][:, :1280]), tm_chunks(x["w_qkv_2"][l][:, 1280:]),
                 fm_chunks(x["w_o_2"][l]), fm_chunks(x["peer_w_q_2"][l])]
    vecs1 = []
    for l in range(L):
        blocks = np.zeros((P, 2, P), np.float32)
        for g in range(4):
            at = slice(64 * (g % 2), 64 * (g % 2) + 64)
            blocks[at, g // 2, at] = x["pool_w"][l, g]
        parts = dict(ln_g=fm(x["ln_g"][l]), ln_b=fm(x["ln_b"][l]), conv_w=fm(x["conv_w"][l]).transpose(0, 2, 1),
                     lb=fm(x["rec_lb"][l]), omlb=np.zeros((P, 4), np.float32), norm_g=fm(x["rec_norm_g"][l]),
                     pool_scale=fm(x["pool_scale"][l]), pool_w=blocks)
        vecs1 += [parts[n].reshape(P, -1) for n in FIRST]
    rows = lambda v: np.broadcast_to(v.reshape(1, -1), (P, v.size))
    parts = dict(ada_b=fm(x["ada_b_2"]), gain1=fm(x["norm1_gain_2"]), gain2=fm(x["norm2_gain_2"]),
                 q_gain=x["q_norm_gain_2"].T, k_gain=x["k_norm_gain_2"].T, sinks=rows(x["attn_sinks_2"][0]),
                 c=np.stack([fm(x["c_2"][0]), fm(x["c_ctx_2"])], 2))
    consts, masks, window = shape_constants()
    return dict(consts=consts, masks=masks, window=window, vecs1=np.concatenate(vecs1, 1),
                vecs2=np.concatenate([parts[n].reshape(P, -1) for n in SECOND], 1),
                x_t=act(x["x"][0]), mem_t=act(x["mem"][0]), ctx_t=act(x["ctx_2"][0]), ffn=np.concatenate(ffn),
                mix_w=np.concatenate(mixw), second_w=np.concatenate(secw),
                ada_rows=row_chunks(x["ada_w_2"][0][:, FIRST_ADA * P:]),
                c_rows=np.broadcast_to(np.stack([x["c_2"][0], x["c_ctx_2"]]), (P, 2, D)),
                subk=x["peer_sub_keys_2"].transpose(3, 0, 1, 2),
                peer_u=x["peer_u_2"].reshape(-1, D), peer_v=x["peer_v_2"].reshape(-1, D))


def kernel(**inputs):
    import concourse.bacc as bacc
    from concourse.bass_utils import run_bass_kernel_spmd

    nc = bacc.Bacc("TRN2", target_bir_lowering=False, num_devices=1)
    arrays, args = {}, {}
    for name, v in laid_out({n: np.asarray(v) for n, v in inputs.items()}).items():
        v = np.ascontiguousarray(v)
        arrays[f"in_{name}"] = v
        args[name] = nc.dram_tensor(f"in_{name}", v.shape, mybir.dt.from_np(v.dtype), kind="ExternalInput").ap()
    out = nc.dram_tensor("out_x", (P, KT, T), F32, kind="ExternalOutput").ap()
    program(nc, args, out)
    r = run_bass_kernel_spmd(nc, [arrays], core_ids=[0])
    got = r.results[0]["out_x"]
    return np.ascontiguousarray(got.transpose(2, 1, 0).reshape(1, T, D))
```
